# Optimizing a Trainium2 kernel written in Bass

```python
import math
import jax, jax.numpy as jnp
from jax import lax
import numpy as np

D_MODEL = 1024
BATCH = 1
SEQ = 256
DEPTH = 1
DEC_BATCH = 8
DEC_SEQ = 4
PAST_LEN = 1024
PAGE_SIZE = 128

NSA_HEADS = 8
NSA_KV_HEADS = 2
NSA_GROUP = NSA_HEADS // NSA_KV_HEADS
NSA_DH = 64
CMP_BLOCK = 32
CMP_STRIDE = 16
CMP_HIDDEN = 128
SLC_BLOCK = 64
SLC_TOPK = 16
WINDOW = 512
Q_BLOCK = 128
HG_HEADS = 4
HG_DK = 128
HG_DV = 128
HG_CHUNK = 64
N_EXPERTS = 32
TOP_K = 4
D_EXPERT = D_MODEL
SWIGLU_LIMIT = 7.0
SWIGLU_ALPHA = 1.702
EPS = 1e-6
NEG_INF = -1e30
FORCE_SCORE = 1e4
Q_W = NSA_HEADS * NSA_DH
KV_W = NSA_KV_HEADS * NSA_DH
NSA_GATE_W = 3 * NSA_HEADS
HG_QK_W = HG_HEADS * HG_DK
HG_V_W = HG_HEADS * HG_DV
SPLIT_SIZES = (Q_W, KV_W, KV_W, KV_W, KV_W, KV_W, KV_W, NSA_GATE_W, HG_QK_W, HG_QK_W, HG_V_W, HG_V_W, D_MODEL, D_MODEL)
IN_W = sum(SPLIT_SIZES)

kernel_name = 'nsa_hgrn2_gated_moe_decode_step'

def rms_norm(x, g):
    xf = x.astype(jnp.float32)
    y = xf * lax.rsqrt(jnp.mean(xf * xf, axis=-1, keepdims=True) + EPS)
    return (y * g.astype(jnp.float32)).astype(x.dtype)

def modulation(c, w_ada, b_ada):
    mod = jax.nn.silu(c) @ w_ada + b_ada
    return [m[:, None, :] for m in jnp.split(mod, 6, axis=-1)]

def split_projection(z):
    offsets, acc = [], 0
    for s in SPLIT_SIZES[:-1]:
        acc += s
        offsets.append(acc)
    return jnp.split(z, offsets, axis=-1)

def alibi_slopes():
    return jnp.exp2(-8.0 * jnp.arange(1, NSA_HEADS + 1, dtype=jnp.float32) / NSA_HEADS).reshape(NSA_KV_HEADS, NSA_GROUP)

def compress(k, pe, w1, w2):
    B, L, G, dh = k.shape
    r = CMP_BLOCK // CMP_STRIDE
    n_chunks = L // CMP_STRIDE
    n_cmp = n_chunks - r + 1
    chunks = k[:, :n_chunks * CMP_STRIDE].reshape(B, n_chunks, CMP_STRIDE, G, dh)
    chunks = chunks.transpose(0, 1, 3, 2, 4).reshape(B, n_chunks, G, CMP_STRIDE * dh)
    w1r = w1.reshape(r, CMP_STRIDE * dh, CMP_HIDDEN)
    pre = pe.reshape(-1) @ w1
    for j in range(r):
        pre = pre + jnp.einsum('bngf,fh->bngh', chunks[:, j:j + n_cmp], w1r[j])
    return jax.nn.gelu(pre) @ w2

def compressed_attend(q, kcb, vcb, q_pos, n_slc, slopes):
    n_cmp = kcb.shape[1]
    start = jnp.arange(n_cmp, dtype=jnp.int32) * CMP_STRIDE
    dist = (q_pos[:, None] - (start + CMP_BLOCK - 1)[None, :]).astype(jnp.float32)
    valid = (dist >= 0)[:, None, None, :]
    s = jnp.einsum('btgrd,bngd->btgrn', q, kcb).astype(jnp.float32) * (NSA_DH ** -0.5)
    s = jnp.where(valid, s - slopes[:, :, None] * dist[:, None, None, :], NEG_INF)
    p = jnp.where(valid, jax.nn.softmax(s, axis=-1), 0.0)
    o = jnp.einsum('btgrn,bngd->btgrd', p.astype(vcb.dtype), vcb)
    slc_start = jnp.arange(n_slc, dtype=jnp.int32) * SLC_BLOCK
    overlap = ((start[:, None] < slc_start[None, :] + SLC_BLOCK) & (start[:, None] + CMP_BLOCK > slc_start[None, :])).astype(jnp.float32)
    imp = jnp.einsum('btgrn,nj->btgj', p, overlap)
    return o, imp

def select_blocks(imp, q_pos, n_slc):
    j = jnp.arange(n_slc, dtype=jnp.int32)
    cur = q_pos // SLC_BLOCK
    forced = (j[None, :] == 0) | (j[None, :] == cur[:, None]) | (j[None, :] == cur[:, None] - 1)
    causal = j[None, :] <= cur[:, None]
    score = jnp.where(forced[None, :, None, :], FORCE_SCORE, jnp.where(causal[None, :, None, :], imp, -FORCE_SCORE))
    _, idx = lax.top_k(score, min(SLC_TOPK, n_slc))
    return idx

def sparse_attend(q, k, v, k_pos, q_pos, slopes):
    dist = (q_pos[:, None, None] - k_pos).astype(jnp.float32)
    valid = (dist >= 0)[..., None, :]
    s = jnp.einsum('...tgrd,...tgnd->...tgrn', q, k).astype(jnp.float32) * (NSA_DH ** -0.5)
    s = jnp.where(valid, s - slopes[:, :, None] * dist[..., None, :], NEG_INF)
    p = jax.nn.softmax(s, axis=-1)
    return jnp.einsum('...tgrn,...tgnd->...tgrd', p.astype(v.dtype), v)

def window_attend(q, k, v, q_pos, k_pos, slopes):
    dist = q_pos[:, None] - k_pos[None, :]
    valid = ((dist >= 0) & (dist < WINDOW) & (k_pos[None, :] >= 0))[:, None, None, :]
    s = jnp.einsum('btgrd,bngd->btgrn', q, k).astype(jnp.float32) * (NSA_DH ** -0.5)
    s = jnp.where(valid, s - slopes[:, :, None] * dist.astype(jnp.float32)[:, None, None, :], NEG_INF)
    p = jax.nn.softmax(s, axis=-1)
    return jnp.einsum('btgrn,bngd->btgrd', p.astype(v.dtype), v)

def prompt_selected(q, k, v, idx, slopes):
    B, T, G, R, dh = q.shape
    offs = jnp.arange(SLC_BLOCK, dtype=jnp.int32)
    gidx = jnp.arange(G, dtype=jnp.int32)[None, :, None]

    def per_seq(args):
        qb, kb, vb, ib = args

        def per_block(n):
            start = n * Q_BLOCK
            qs = lax.dynamic_slice_in_dim(qb, start, Q_BLOCK, axis=0)
            isel = lax.dynamic_slice_in_dim(ib, start, Q_BLOCK, axis=0)
            tok = (isel[..., None] * SLC_BLOCK + offs).reshape(Q_BLOCK, G, -1)
            q_pos = start + jnp.arange(Q_BLOCK, dtype=jnp.int32)
            return sparse_attend(qs, kb[tok, gidx], vb[tok, gidx], tok, q_pos, slopes)

        out = lax.map(per_block, jnp.arange(T // Q_BLOCK, dtype=jnp.int32))
        return out.reshape(T, G, R, dh)

    return lax.map(per_seq, (q, k, v, idx))

def prompt_window(q, k, v, slopes):
    B, T, G, R, dh = q.shape
    pad = jnp.zeros((B, WINDOW, G, dh), k.dtype)
    kp = jnp.concatenate([pad, k], axis=1)
    vp = jnp.concatenate([pad, v], axis=1)
    span = WINDOW + Q_BLOCK

    def per_block(n):
        start = n * Q_BLOCK
        qs = lax.dynamic_slice_in_dim(q, start, Q_BLOCK, axis=1)
        kb = lax.dynamic_slice_in_dim(kp, start, span, axis=1)
        vb = lax.dynamic_slice_in_dim(vp, start, span, axis=1)
        q_pos = start + jnp.arange(Q_BLOCK, dtype=jnp.int32)
        k_pos = start - WINDOW + jnp.arange(span, dtype=jnp.int32)
        return window_attend(qs, kb, vb, q_pos, k_pos, slopes)

    out = lax.map(per_block, jnp.arange(T // Q_BLOCK, dtype=jnp.int32))
    return out.transpose(1, 0, 2, 3, 4, 5).reshape(B, T, G, R, dh)

def nsa_combine(o_cmp, o_slc, o_win, g_nsa):
    B, T = g_nsa.shape[:2]
    g = jax.nn.sigmoid(g_nsa).reshape(B, T, 3, NSA_KV_HEADS, NSA_GROUP, 1)
    o = g[:, :, 0] * o_cmp + g[:, :, 1] * o_slc + g[:, :, 2] * o_win
    return o.reshape(B, T, Q_W)

def hgrn2(hq, hf, hi, hg, lb, S0, norm_w):
    B, T, _ = hq.shape
    q = jax.nn.silu(hq.astype(jnp.float32)).reshape(B, T, HG_HEADS, HG_DK)
    lbh = lb.reshape(HG_HEADS, HG_DK)
    f = lbh + (1.0 - lbh) * jax.nn.sigmoid(hf.astype(jnp.float32).reshape(B, T, HG_HEADS, HG_DK))
    k = 1.0 - f
    g = jnp.log(f)
    v = hi.astype(jnp.float32).reshape(B, T, HG_HEADS, HG_DV)
    C = math.gcd(T, HG_CHUNK)
    n = T // C

    def to_chunks(a):
        return a.reshape(B, n, C, HG_HEADS, a.shape[-1]).transpose(1, 0, 3, 2, 4)

    tri = jnp.tril(jnp.ones((C, C), dtype=bool))

    def step(S, inp):
        qc, kc, gc, vc = inp
        b = jnp.cumsum(gc, axis=2)
        o_inter = jnp.einsum('bhtk,bhkv->bhtv', qc * jnp.exp(b), S)
        rel = b[:, :, :, None, :] - b[:, :, None, :, :]
        decay = jnp.exp(jnp.where(tri[:, :, None], rel, -jnp.inf))
        A = jnp.einsum('bhtk,bhsk,bhtsk->bhts', qc, kc, decay)
        o_intra = jnp.einsum('bhts,bhsv->bhtv', A, vc)
        bC = b[:, :, -1]
        S = jnp.exp(bC)[..., None] * S + jnp.einsum('bhsk,bhsv->bhkv', kc * jnp.exp(bC[:, :, None] - b), vc)
        return S, o_inter + o_intra

    S, o = lax.scan(step, S0.astype(jnp.float32), (to_chunks(q), to_chunks(k), to_chunks(g), to_chunks(v)))
    o = o.transpose(1, 0, 3, 2, 4).reshape(B, T, HG_HEADS, HG_DV)
    o = o * lax.rsqrt(jnp.mean(o * o, axis=-1, keepdims=True) + EPS) * norm_w.astype(jnp.float32)
    o = o * jax.nn.silu(hg.astype(jnp.float32).reshape(B, T, HG_HEADS, HG_DV))
    return o.reshape(B, T, HG_V_W).astype(hq.dtype), S.astype(S0.dtype)

def merge_branches(o_nsa, o_hg, ga, gb, w_branch_a, w_branch_b, w_out):
    m = jax.nn.sigmoid(ga) * (o_nsa @ w_branch_a) + jax.nn.sigmoid(gb) * (o_hg @ w_branch_b)
    return m @ w_out

def mixer_prompt(h, w_in, cmp_pe, cmp_w1, cmp_w2, lb, hg_norm, w_branch_a, w_branch_b, w_out, slopes):
    B, T, _ = h.shape
    q, kc, vc, ks, vs, kw, vw, g_nsa, hq, hf, hi, hg, ga, gb = split_projection(h @ w_in)
    q = q.reshape(B, T, NSA_KV_HEADS, NSA_GROUP, NSA_DH)
    kc, vc, ks, vs, kw, vw = [a.reshape(B, T, NSA_KV_HEADS, NSA_DH) for a in (kc, vc, ks, vs, kw, vw)]
    q_pos = jnp.arange(T, dtype=jnp.int32)
    n_slc = -(-T // SLC_BLOCK)
    kcb = compress(kc, cmp_pe[0], cmp_w1[0], cmp_w2[0])
    vcb = compress(vc, cmp_pe[1], cmp_w1[1], cmp_w2[1])
    o_cmp, imp = compressed_attend(q, kcb, vcb, q_pos, n_slc, slopes)
    idx = select_blocks(imp, q_pos, n_slc)
    o_slc = prompt_selected(q, ks, vs, idx, slopes)
    o_win = prompt_window(q, kw, vw, slopes)
    o_nsa = nsa_combine(o_cmp, o_slc, o_win, g_nsa)
    S0 = jnp.zeros((B, HG_HEADS, HG_DK, HG_DV), h.dtype)
    o_hg, S = hgrn2(hq, hf, hi, hg, lb, S0, hg_norm)
    out = merge_branches(o_nsa, o_hg, ga, gb, w_branch_a, w_branch_b, w_out)
    keep = min(WINDOW, T)
    kv_cmp = jnp.stack([kc, vc], axis=2)
    kv_sel = jnp.stack([ks, vs], axis=2)
    win = jnp.stack([kw, vw], axis=2)[:, T - keep:]
    return out, kv_cmp, kv_sel, win, S

def mixer_sample(h, cache_cmp, cache_sel, win_buf, S0, page_table, w_in, cmp_pe, cmp_w1, cmp_w2, lb, hg_norm, w_branch_a, w_branch_b, w_out, slopes):
    B, T, _ = h.shape
    L = PAST_LEN + T
    q, kc, vc, ks, vs, kw, vw, g_nsa, hq, hf, hi, hg, ga, gb = split_projection(h @ w_in)
    q = q.reshape(B, T, NSA_KV_HEADS, NSA_GROUP, NSA_DH)
    kc, vc, ks, vs, kw, vw = [a.reshape(B, T, NSA_KV_HEADS, NSA_DH) for a in (kc, vc, ks, vs, kw, vw)]
    q_pos = PAST_LEN + jnp.arange(T, dtype=jnp.int32)
    past_cmp = cache_cmp[page_table].reshape(B, PAST_LEN, 2, NSA_KV_HEADS, NSA_DH)
    kc_all = jnp.concatenate([past_cmp[:, :, 0], kc], axis=1)
    vc_all = jnp.concatenate([past_cmp[:, :, 1], vc], axis=1)
    kcb = compress(kc_all, cmp_pe[0], cmp_w1[0], cmp_w2[0])
    vcb = compress(vc_all, cmp_pe[1], cmp_w1[1], cmp_w2[1])
    n_slc = -(-L // SLC_BLOCK)
    o_cmp, imp = compressed_attend(q, kcb, vcb, q_pos, n_slc, slopes)
    idx = select_blocks(imp, q_pos, n_slc)
    tok = (idx[..., None] * SLC_BLOCK + jnp.arange(SLC_BLOCK, dtype=jnp.int32)).reshape(B, T, NSA_KV_HEADS, -1)
    bi = jnp.arange(B, dtype=jnp.int32)[:, None, None, None]
    gi = jnp.arange(NSA_KV_HEADS, dtype=jnp.int32)[None, None, :, None]
    tp = jnp.minimum(tok, PAST_LEN - 1)
    phys = page_table[bi, tp // PAGE_SIZE]
    off = tp % PAGE_SIZE
    tn = jnp.clip(tok - PAST_LEN, 0, T - 1)
    in_past = (tok < PAST_LEN)[..., None]
    k_sel = jnp.where(in_past, cache_sel[phys, off, 0, gi], ks[bi, tn, gi])
    v_sel = jnp.where(in_past, cache_sel[phys, off, 1, gi], vs[bi, tn, gi])
    o_slc = sparse_attend(q, k_sel, v_sel, tok, q_pos, slopes)
    WB = win_buf.shape[1]
    buf = jnp.concatenate([win_buf, jnp.stack([kw, vw], axis=2)], axis=1)
    k_pos = PAST_LEN - WB + jnp.arange(WB + T, dtype=jnp.int32)
    o_win = window_attend(q, buf[:, :, 0], buf[:, :, 1], q_pos, k_pos, slopes)
    o_nsa = nsa_combine(o_cmp, o_slc, o_win, g_nsa)
    o_hg, S = hgrn2(hq, hf, hi, hg, lb, S0, hg_norm)
    out = merge_branches(o_nsa, o_hg, ga, gb, w_branch_a, w_branch_b, w_out)
    kv_cmp = jnp.stack([kc, vc], axis=2)
    kv_sel = jnp.stack([ks, vs], axis=2)
    return out, kv_cmp, kv_sel, buf[:, T:], S

def moe_ffn(h, w_router, b_router, w_up, b_up, w_down, b_down):
    B, T, D = h.shape
    xt = h.reshape(-1, D)
    logits = (xt @ w_router + b_router).astype(jnp.float32)
    top_v, top_i = lax.top_k(logits, TOP_K)
    wts = jax.nn.softmax(top_v, axis=-1)
    gate_dense = jnp.sum(jax.nn.one_hot(top_i, N_EXPERTS, dtype=jnp.float32) * wts[..., None], axis=1).astype(h.dtype)
    out = jnp.zeros_like(xt)
    for e in range(N_EXPERTS):
        z = xt @ w_up[e] + b_up[e]
        gate = jnp.minimum(z[:, :D_EXPERT], SWIGLU_LIMIT)
        up = jnp.clip(z[:, D_EXPERT:], -SWIGLU_LIMIT, SWIGLU_LIMIT)
        act = (up + 1.0) * gate * jax.nn.sigmoid(SWIGLU_ALPHA * gate)
        out = out + gate_dense[:, e:e + 1] * (act @ w_down[e] + b_down[e])
    return out.reshape(B, T, D)

def setup_inputs(seed: int = 0) -> dict:
    key = jax.random.key(seed)
    ks = jax.random.split(key, 32)
    f32 = jnp.float32
    n_pages = PAST_LEN // PAGE_SIZE
    n_pool = (DEC_BATCH * n_pages * 5) // 4
    win_buf = min(WINDOW, PAST_LEN)

    def nrm(k, shape, scale):
        return jax.random.normal(k, shape, f32) * scale

    page_table = jax.random.permutation(ks[8], n_pool)[: DEC_BATCH * n_pages].reshape(DEC_BATCH, n_pages).astype(jnp.int32)
    return {
        'x_prompt': nrm(ks[0], (BATCH, SEQ, D_MODEL), 1.0),
        'x_sample': nrm(ks[1], (DEC_BATCH, DEC_SEQ, D_MODEL), 1.0),
        'c_prompt': nrm(ks[2], (BATCH, D_MODEL), 1.0),
        'c_sample': nrm(ks[3], (DEC_BATCH, D_MODEL), 1.0),
        'cache_cmp': nrm(ks[4], (DEPTH, n_pool, PAGE_SIZE, 2, NSA_KV_HEADS, NSA_DH), 1.0),
        'cache_sel': nrm(ks[5], (DEPTH, n_pool, PAGE_SIZE, 2, NSA_KV_HEADS, NSA_DH), 1.0),
        'state_win': nrm(ks[6], (DEPTH, DEC_BATCH, win_buf, 2, NSA_KV_HEADS, NSA_DH), 1.0),
        'state_hgrn': nrm(ks[7], (DEPTH, DEC_BATCH, HG_HEADS, HG_DK, HG_DV), 0.5),
        'page_table': page_table,
        'w_ada': nrm(ks[9], (DEPTH, D_MODEL, 6 * D_MODEL), 0.5 * D_MODEL ** -0.5),
        'b_ada': nrm(ks[10], (DEPTH, 6 * D_MODEL), 0.02),
        'norm_mix_pre': 1.0 + nrm(ks[11], (DEPTH, D_MODEL), 0.05),
        'norm_mix_post': 1.0 + nrm(ks[12], (DEPTH, D_MODEL), 0.05),
        'norm_ffn_pre': 1.0 + nrm(ks[13], (DEPTH, D_MODEL), 0.05),
        'norm_ffn_post': 1.0 + nrm(ks[14], (DEPTH, D_MODEL), 0.05),
        'w_in': nrm(ks[15], (DEPTH, D_MODEL, IN_W), D_MODEL ** -0.5),
        'cmp_pe': nrm(ks[16], (DEPTH, 2, CMP_BLOCK, NSA_DH), 0.1),
        'cmp_w1': nrm(ks[17], (DEPTH, 2, CMP_BLOCK * NSA_DH, CMP_HIDDEN), (CMP_BLOCK * NSA_DH) ** -0.5),
        'cmp_w2': nrm(ks[18], (DEPTH, 2, CMP_HIDDEN, NSA_DH), CMP_HIDDEN ** -0.5),
        'hg_lb_logits': nrm(ks[19], (DEPTH + 1, HG_QK_W), 0.5),
        'hg_norm': 1.0 + nrm(ks[20], (DEPTH, HG_DV), 0.05),
        'w_branch_a': nrm(ks[21], (DEPTH, Q_W, D_MODEL), Q_W ** -0.5),
        'w_branch_b': nrm(ks[22], (DEPTH, HG_V_W, D_MODEL), HG_V_W ** -0.5),
        'w_out': nrm(ks[23], (DEPTH, D_MODEL, D_MODEL), D_MODEL ** -0.5),
        'w_router': nrm(ks[24], (DEPTH, D_MODEL, N_EXPERTS), D_MODEL ** -0.5),
        'b_router': nrm(ks[25], (DEPTH, N_EXPERTS), 0.01),
        'w_up': nrm(ks[26], (DEPTH, N_EXPERTS, D_MODEL, 2 * D_EXPERT), D_MODEL ** -0.5),
        'b_up': nrm(ks[27], (DEPTH, N_EXPERTS, 2 * D_EXPERT), 0.02),
        'w_down': nrm(ks[28], (DEPTH, N_EXPERTS, D_EXPERT, D_MODEL), D_EXPERT ** -0.5),
        'b_down': nrm(ks[29], (DEPTH, N_EXPERTS, D_MODEL), 0.02),
    }

def reference(x_prompt, x_sample, c_prompt, c_sample, cache_cmp, cache_sel, state_win, state_hgrn, page_table,
              w_ada, b_ada, norm_mix_pre, norm_mix_post, norm_ffn_pre, norm_ffn_post, w_in, cmp_pe, cmp_w1, cmp_w2,
              hg_lb_logits, hg_norm, w_branch_a, w_branch_b, w_out, w_router, b_router, w_up, b_up, w_down, b_down):
    slopes = alibi_slopes()
    lb_all = jnp.cumsum(jax.nn.softmax(hg_lb_logits.astype(jnp.float32), axis=0), axis=0)
    yp, ys = x_prompt, x_sample
    cmp_p, cmp_s, sel_p, sel_s, win_p, win_s, hg_p, hg_s = [], [], [], [], [], [], [], []
    for l in range(DEPTH):
        shared = (w_in[l], cmp_pe[l], cmp_w1[l], cmp_w2[l], lb_all[l], hg_norm[l], w_branch_a[l], w_branch_b[l], w_out[l], slopes)
        moe_w = (w_router[l], b_router[l], w_up[l], b_up[l], w_down[l], b_down[l])
        sh1, sc1, g1, sh2, sc2, g2 = modulation(c_prompt, w_ada[l], b_ada[l])
        h = rms_norm(yp, norm_mix_pre[l]) * (1.0 + sc1) + sh1
        out, kvc, kvs, win, S = mixer_prompt(h, *shared)
        yp = yp + g1 * rms_norm(out, norm_mix_post[l])
        h = rms_norm(yp, norm_ffn_pre[l]) * (1.0 + sc2) + sh2
        yp = yp + g2 * rms_norm(moe_ffn(h, *moe_w), norm_ffn_post[l])
        cmp_p.append(kvc)
        sel_p.append(kvs)
        win_p.append(win)
        hg_p.append(S)
        sh1, sc1, g1, sh2, sc2, g2 = modulation(c_sample, w_ada[l], b_ada[l])
        h = rms_norm(ys, norm_mix_pre[l]) * (1.0 + sc1) + sh1
        out, kvc, kvs, win, S = mixer_sample(h, cache_cmp[l], cache_sel[l], state_win[l], state_hgrn[l], page_table, *shared)
        ys = ys + g1 * rms_norm(out, norm_mix_post[l])
        h = rms_norm(ys, norm_ffn_pre[l]) * (1.0 + sc2) + sh2
        ys = ys + g2 * rms_norm(moe_ffn(h, *moe_w), norm_ffn_post[l])
        cmp_s.append(kvc)
        sel_s.append(kvs)
        win_s.append(win)
        hg_s.append(S)
    return (yp, ys, jnp.stack(cmp_p), jnp.stack(cmp_s), jnp.stack(sel_p), jnp.stack(sel_s), jnp.stack(win_p), jnp.stack(win_s), jnp.stack(hg_p), jnp.stack(hg_s))


_drawn_inputs = setup_inputs


def setup_inputs(seed=0):
    import zlib

    import numpy as np

    out = dict(_drawn_inputs(seed))
    spreads = {}
    factors = {'norm_ffn_post': 3.854, 'b_router': 2.894, 'b_up': 8.0, 'b_down': 8.0}
    for name, (base, spread) in spreads.items():
        noise = np.random.default_rng([zlib.crc32(name.encode()), seed]).standard_normal(out[name].shape)
        drawn = base * np.exp(spread * noise) if base else spread * noise
        out[name] = __import__('jax').numpy.asarray(drawn.astype(out[name].dtype))
    for name, factor in factors.items():
        out[name] = (out[name] * factor).astype(out[name].dtype)
    return out
```

```python
from contextlib import ExitStack

import numpy as np

import concourse.bass as bass
from concourse import mybir

F32 = mybir.dt.float32
I32 = mybir.dt.int32
U32 = mybir.dt.uint32
ALU = mybir.AluOpType
ACT = mybir.ActivationFunctionType
AX = mybir.AxisListType.X

P = 128
D = 1024
KD = D // P
TP, NB, TS = 256, 8, 4
NS = NB * TS
PAST, PAGE = 1024, 128
NPG = PAST // PAGE
G, R, DH, H = 2, 4, 64, 8
WIN = 512
NCMP = PAST // 16 - 1
NCMP_P = TP // 16 - 1
HH, DK = 4, 128
E, TOPK = 32, 4
EPS = 1e-6
OFF = {}
IN_W = 0
for _n, _w in (("q", 512), ("kc", 128), ("vc", 128), ("ks", 128), ("vs", 128), ("kw", 128), ("vw", 128), ("gn", 24),
               ("hq", 512), ("hf", 512), ("hi", 512), ("hg", 512), ("ga", 1024), ("gb", 1024)):
    OFF[_n] = IN_W
    IN_W += _w
ROWS = (P, P, NS)
SLOT = 64
CMAX = E + (TOPK * (TP + NS) - E) // SLOT
NCHUNK = CMAX + 1
JMAX = -(-(TP + NS) // SLOT)
SEL_W = PAST + NS
WIN_W = WIN + NS
FAR = -1e33
CLIP = 1e18
TOP = 41.0

CONSTS = {}
_cat = []


def _put(name, a):
    t = np.zeros((P, a.shape[1]), np.float32)
    t[:a.shape[0]] = a
    CONSTS[name] = (sum(x.shape[1] for x in _cat), a.shape[1])
    _cat.append(t)


def const_table():
    _cat.clear()
    p = np.arange(P)
    _put("ident", np.eye(P))
    _put("tri", (p[:, None] <= p[None, :]) * 1.0)
    _put("stri", (p[:, None] < p[None, :]) * 1.0)
    dist = P + p[:, None] - np.arange(2 * P)[None, :]
    _put("nd", np.where(dist >= 0, -dist, FAR))
    for i in range(2):
        dist = i * P + p[:, None] - (16 * np.arange(16)[None, :] + 31)
        _put(f"ndc{i}", np.where(dist >= 0, -dist, FAR))
    _put("rowv", np.stack([(p >= 31) * 1.0, np.ones(P)], 1))
    b32 = np.arange(NS) // TS
    same = b32[:, None] == b32[None, :]
    _put("bt32", (same & (np.arange(NS)[:, None] <= np.arange(NS)[None, :])) * 1.0)
    _put("bmask", (b32[:, None] == np.arange(NB)[None, :]) * 1.0)
    _put("jp1", np.broadcast_to(np.arange(1, 17), (P, 16)))
    _put("iota", np.broadcast_to(np.arange(E), (P, E)))
    _put("selp", np.repeat(p[:, None] == 32 * np.arange(4)[None, :], P, 1) * 1.0)
    _put("sels", np.concatenate([p[:, None] == 32 * j + 1 + b32[None, :] for j in range(4)], 1) * 1.0)
    rb, rr, rt = p // 16, (p // 4) % 4, p % 4
    _put("rdiag", (rr[:, None] == np.arange(4)[None, :]) * 1.0)
    _put("expand", (np.arange(NS)[:, None] == (rb * TS + rt)[None, :]) * 1.0)
    _put("gsum", ((rb[:, None] == rb[None, :]) & (rt[:, None] == rt[None, :])) * 1.0)
    _put("slope", np.stack([2.0 ** -(g * R + rr + 1.0) for g in range(G)], 1))
    qpos = PAST + rt
    nb, nt = np.arange(NS) // TS, np.arange(NS) % TS
    new = np.where((nb[None, :] == rb[:, None]) & (nt[None, :] <= rt[:, None]),
                   -(rt[:, None] - nt[None, :]).astype(np.float64), FAR)
    _put("ndsel", np.concatenate([-(qpos[:, None] - np.arange(PAST)[None, :]), new], 1))
    d = qpos[:, None] - (PAST - WIN + np.arange(WIN)[None, :])
    _put("ndwin", np.concatenate([np.where(d < WIN, -d, FAR), new], 1))
    _put("ndcs", -(qpos[:, None] - (16 * np.arange(64)[None, :] + 31)))
    return np.concatenate(_cat, 1).astype(np.float32)


CONST = const_table()


STEPS = {
    "pe_step": ('sct_ps', 'peT_ps', 'pconst_ps', 'comp_ps', 'sq_ps', 'sgate_ps', 'imp_ps', 'lg_ps', 'cnt_ps', 'base_ps'),
    "act_step": ('silu_c', 'sg_gate', 'comp_a', 'lb', 'hf_sig', 'gl', 'all_out'),
    "dve_step": ('zeroed', 'zero_t', 'sct', 'mod_w', 'peT', 'pconst', 'comp_v', 'sq', 'imp', 'lb_d', 'f', 'hk', 'vm', 's_free', 's_kq', 'onS', 'nch', 'tab'),
}
STEP_OF = {name: (sem, n + 1) for sem, names in STEPS.items() for n, name in enumerate(names)}


def _ppt(i, branch):
    return sum((j + 1 if b else 1) for j in range(2) for b in range(3) if (j, b) < (i, branch))


def build(nc, A, O):
    with ExitStack() as ctx:
        arena_w = 53200
        arena = ctx.enter_context(nc.sbuf_tensor("arena", [P, arena_w], F32))
        banks = [ctx.enter_context(nc.psum_tensor(f"bank{i}", [P, 512], F32)) for i in range(8)]
        sems = {}

        def S(name):
            name = STEP_OF[name][0] if name in STEP_OF else name
            if name not in sems:
                sems[name] = ctx.enter_context(nc.semaphore(name))
            return sems[name]

        def after(eng, name):
            eng.wait_ge(S(name), STEP_OF[name][1])

        place = {"at": 0}

        def take(n, *shape):
            a = place["at"]
            place["at"] = a + n
            assert place["at"] <= arena_w, place["at"]
            return view(a, n, *shape)

        def view(a, n, *shape):
            v = arena[:, a:a + n]
            if len(shape) == 2:
                v = v.rearrange("p (a b) -> p a b", b=shape[1])
            elif len(shape) == 3:
                v = v.rearrange("p (a b c) -> p a b c", b=shape[1], c=shape[2])
            elif len(shape) == 4:
                v = v.rearrange("p (a b c d) -> p a b c d", b=shape[1], c=shape[2], d=shape[3])
            return v

        ctab = take(CONST.shape[1])

        def C(name, rows=P, r0=0):
            o, w = CONSTS[name]
            return ctab[r0:r0 + rows, o:o + w]

        ident = C("ident")
        x = take(3 * D, 3, D)
        mod = take(12 * P, 12, P)
        gate_rows = take(2 * D, 2, D)
        mod_rows_at = place["at"]
        mod_rows = take(4 * D, 2, 2, D)
        ones = take(P)
        wr = take(KD * E, KD, E)
        br = take(E)
        tab = take(3 * E).bitcast(I32)
        rowu = take(12).bitcast(U32)
        zero_t = take(P)
        ptab = take(NB * NPG).bitcast(I32)
        small = take(768)
        sm = {"at": 0}

        def tiny(n):
            a = sm["at"]
            sm["at"] = a + n
            assert sm["at"] <= 768
            return small[:, a:a + n]

        eps_t = tiny(1)
        ss = tiny(4)
        rt_ = tiny(4)
        rstd = tiny(4)
        pr_max, pr_sum, pr_coef = tiny(8), tiny(8), tiny(8)
        sg_gate = tiny(3 * 24).rearrange("p (a b) -> p a b", b=24)
        sa_gate3 = tiny(24)
        sa_gate = tiny(6)
        sa_max, sa_sum, sa_coef = tiny(2), tiny(2), tiny(2)
        imp, impg, cand = tiny(32), tiny(32), tiny(32)
        lowest, dropj = tiny(2), tiny(2)
        dmask = tiny(32)
        pconst = tiny(2)
        hss, hrt, hrs = tiny(12), tiny(12), tiny(12)
        top8 = tiny(8)
        top8i = tiny(8)
        idxf = tiny(4)
        wts = tiny(12).rearrange("p (a b) -> p a b", b=4)
        wsum, wrec, negtop = tiny(1), tiny(1), tiny(1)
        rowf = tiny(12)
        gathered = tiny(1)
        n_t = place["at"]

        z = take(3 * IN_W, 3, IN_W)
        free0 = place["at"]
        h_rows = view(free0 + 3 * 4096 + 2304, D)
        hT = view(free0 + 3 * 4096, KD * (TP + NS), KD, TP + NS)
        slabs = [view(free0 + 4096 * i, 4096, KD, 512) for i in range(3)]
        bada = view(n_t, 12 * P, 12, P)
        wn = view(n_t + 12 * P, 8 * P, 8, P)
        c9 = view(n_t + 20 * P, D)
        sc32 = view(n_t + 20 * P + D, D)
        scT = view(n_t + 20 * P + 2 * D, KD * 32, KD, 32)

        dram = {}

        def internal(name, shape):
            dram[name] = nc.dram_tensor(name, shape, F32, kind="Internal").ap()
            return dram[name]

        slots = internal("slots", (NCHUNK * SLOT, D))

        w_in = A["w_in"][0]
        w_ada = A["w_ada"][0]
        zc = lambda i, name, w, r=None: z[0:ROWS[i], i, OFF[name]:OFF[name] + w]

        order = {"act": 0, "dve": 0, "pool": 0}

        def link(eng, key, ins):
            order[key] += 1
            ins.then_inc(S(f"own_{key}"), 1)
            eng.wait_ge(S(f"own_{key}"), order[key])


        fr = {"at": free0}

        def ftake(n, *shape):
            a = fr["at"]
            fr["at"] = a + n
            assert fr["at"] <= arena_w, fr["at"] - arena_w
            return view(a, n, *shape)

        NC_ALL = NB * NCMP + NCMP_P
        kcT = ftake(520)
        vcb = ftake(9 * P, 9, P)
        w2 = ftake(2 * DH, 2, DH)
        pe_rows = ftake(P)
        peT = ftake(32)
        attn0 = fr["at"]
        raw_at = arena_w - 2080
        raw = [view(raw_at + 512 * v, 512) for v in range(4)]
        geT = view(raw_at, 4 * 520, 2, 2, 520)
        UN = NB * 4 + 1
        pairT = ftake(4 * UN * P, 2, 2, UN * P)
        w1 = view(mod_rows_at, 4 * D, 2, 16, P)

        fr["at"] = attn0
        qT = view(mod_rows_at, 4 * TP, 4, TP)
        kT = ftake(2 * TP, 2, TP)
        qf = ftake(P, NB, R, TS)
        qz_at = fr["at"]
        qz = ftake(NB * 144)
        knT = ftake(2 * NS, 2, NS)
        onT = ftake(4 * 288, 4, 288)
        ohT = ftake(4 * 288, 4, 288)
        on = view(mod_rows_at + D, 2 * 512, 2, 512)
        oS = ftake(256)
        work0 = fr["at"]
        kst_at = fr["at"]
        kst = [ftake(D, 8, P) for _ in range(2)]
        vpages_at = fr["at"]
        vpages = ftake(NB * NPG * P, NB * NPG, P)
        sS = ftake(2 * SEL_W, 2, SEL_W)
        pTs = ftake(9 * 256, 9, 2, P)
        kTb = [view(mod_rows_at + D * (2 + i), D) for i in range(2)]
        fr["at"] = work0
        sP = ftake(8 * 256, 8, 256)
        pTp = ftake(2 * 8 * P, 2, 8, P)
        fr["at"] = work0
        gl = ftake(3 * 512, 3, 512)
        lb = ftake(512)
        oml = ftake(512)
        hgn = ftake(P)
        state = ftake(512, HH, DK)
        bT = ftake(512, HH, P)
        hqT = ftake(512, HH, P)
        hkT = ftake(512, HH, P)
        ebT = ftake(512, HH, P)
        qe = ftake(512, HH, P)
        dk = ftake(D, 8, P)
        dq = ftake(P, 8, 16)
        att = ftake(P)
        kh = ftake(512)
        oh = ftake(512, HH, DK)
        osq = ftake(512, HH, DK)
        hs0 = fr["at"]
        fr["at"] = work0 + 1536 + 512 * 2 + P
        s0 = ftake(NB * HH * DK, NB * HH, DK)
        vm = ftake(NB * 512, NB, 512)
        qep = view(mod_rows_at, 4 * NB * 36, 4, NB * 36)
        sb_ = ftake(7 * P, 7, HH, NS)
        kh_s = ftake(512)
        oh_s = view(mod_rows_at + 1280, 512, HH, DK)
        osq_s = view(mod_rows_at + 1792, 512, HH, DK)
        att_s = ftake(P, HH, NS)
        fr["at"] = work0
        wa = ftake(4 * D, 4, D)
        wb = ftake(4 * D, 4, D)
        mT = ftake(KD * 288, KD, 288)
        mrow = ftake(D)
        orow = ftake(D)
        scr = view(n_t + 3 * D, D)
        fr["at"] = work0
        lg = ftake(3 * E, 3, E)
        oneh = ftake(3 * 4 * E, 3, 4, E)
        mk = ftake(3 * E, 3, E)
        nchT = ftake(P)
        slotb = ftake(E)
        roww = ftake(E)
        wo = [view(n_t + IN_W + 4096 * i, 4096, 4, D) for i in range(2)]
        h2r = view(n_t, 3 * D, 3, D)
        h2T = mT
        xrow = view(n_t, D)
        xcT = view(n_t + D, 512, KD, SLOT)
        gt, up, sg, ac, aT, yc = (view(n_t + D + 512 * (1 + i), 512) for i in range(6))
        bias = view(mod_rows_at, 3 * D)
        ring_at = n_t + D + 512 * 7
        assert ring_at + 16 * 2 * D <= arena_w
        ring = [view(ring_at + 2 * D * i, 2 * D) for i in range(16)]
        gath = view(ring_at, 12 * D, 3, 4, D)
        accr = view(n_t, D)
        sqr = view(n_t + D, D)

        def by_parity(bank):
            return bank[:].rearrange("p (s k c) -> p s k c", s=2, k=2)

        cmp_pages = A["cache_cmp"][0].rearrange("n (p s) k g d -> n p (s k g d)", s=2)
        sel_pages = A["cache_sel"][0].rearrange("n p k g d -> n p k (g d)")
        n_pool = cmp_pages.shape[0]

        def load_pages(eng, units):
            eng.wait_ge(S("ld_ptab"), 16)

            def load(b, v):
                for half in range(2):
                    page = eng.value_load(ptab[0:1, bass.ds(b * NPG + 2 * v + half, 1)], min_val=0, max_val=n_pool - 1)
                    eng.dma_start(raw[v][64 * half:64 * half + 64], cmp_pages[bass.ds(page, 1)].squeeze(0)
                                  ).then_inc(S(f"ld_raw{v}"), 16)

            for v in units:
                load(0, v)
            with eng.Fori(1, NB) as b:
                for v in units:
                    eng.wait_ge(S("pair_ps"), 4 * b + (v - 3))
                    load(b, v)

        def load_selected(eng, first, name):
            for b in range(NB):
                eng.wait_ge(S("key_ps"), NB + b - 1)
                if b == 0:
                    eng.wait_ge(S("pv_ps"), 2)
                to = kst_at + D * (b % 2)
                apart = vpages_at + D * b - to
                start = min(to, arena_w - 2 * apart)
                both = arena[:, start:start + 2 * apart].rearrange("p (k c) -> p k c", k=2)[:, :, to - start:to - start + D]
                both = both.rearrange("p k (n c) -> p n k c", n=NPG)
                with eng.Fori(first, first + NPG // 2) as n:
                    page = eng.value_load(ptab[0:1, bass.ds(n + b * NPG, 1)], min_val=0, max_val=n_pool - 1)
                    eng.dma_start(both[:, bass.ds(n, 1)].squeeze(1), sel_pages[bass.ds(page, 1)].squeeze(0)
                                  ).then_inc(S(f"{name}{b % 2}"), 16)


        block = ctx.enter_context(nc.Block())

        @block.sync
        def _(sp):
            sp.dma_start(ctab, A["const"]).then_inc(S("ld_const"), 16)
            sp.dma_start(c9[0:1], A["c_prompt"]).then_inc(S("ld_c"), 16)
            sp.dma_start(c9[1:1 + NB], A["c_sample"]).then_inc(S("ld_c"), 16)

            def load_slab(m):
                if m >= 3:
                    if m - 3 < 12:
                        sp.wait_ge(S("mod_mm"), m - 2)
                    else:
                        sp.wait_ge(S("zin_mm"), m - 14)
                c0 = (m if m < 12 else m - 12) * 512
                src = w_ada if m < 12 else w_in
                w = min(512, src.shape[1] - c0)
                if m == 12:
                    for r in range(R):
                        for g in range(G):
                            c = DH * (R * g + r)
                            sp.dma_start(slabs[0][:, :, DH * (G * r + g):DH * (G * r + g) + DH],
                                         src[:, c:c + DH].rearrange("(k p) c -> p k c", p=P)).then_inc(S("ld_slab0"), 16)
                    return
                sp.dma_start(slabs[m % 3][:, :, 0:w], src[:, c0:c0 + w].rearrange("(k p) c -> p k c", p=P)
                             ).then_inc(S(f"ld_slab{m % 3}"), 16)

            load_slab(0)
            for j in range(4):
                src = A["b_ada"][0].rearrange("(n j c) -> j n c", j=4, c=P)[j]
                sp.dma_start(bada[32 * j:32 * j + 32], src.unsqueeze(0).broadcast_to([32, 12, P])).then_inc(S("ld_bada"), 16)
            load_slab(1)
            load_slab(2)
            sp.dma_start(ptab[0:1], A["page_table"].rearrange("(o b) n -> o (b n)", o=1)).then_inc(S("ld_ptab"), 16)
            for w, name in enumerate(("norm_mix_pre", "norm_mix_post", "norm_ffn_pre", "norm_ffn_post")):
                for j in range(4):
                    src = A[name][0].rearrange("(n j c) -> j n c", j=4, c=P)[j]
                    sp.dma_start(wn[32 * j:32 * j + 32, 2 * w:2 * w + 2], src.unsqueeze(0).broadcast_to([32, 2, P])
                                 ).then_inc(S("ld_wn"), 16)
            sp.dma_start(x[:, 0:2], A["x_prompt"][0].rearrange("(i p) d -> p i d", p=P)).then_inc(S("ld_x"), 16)
            sp.dma_start(x[0:NS, 2], A["x_sample"].rearrange("b t d -> (b t) d")).then_inc(S("ld_x"), 16)
            for m in range(3, 23):
                load_slab(m)
            sp.wait_ge(S("zin_mm"), 11)
            sp.dma_start(w1, A["cmp_w1"][0].rearrange("v (q p) h -> p v q h", p=P)).then_inc(S("ld_w1"), 16)
            sp.dma_start(w2, A["cmp_w2"][0].rearrange("v h d -> h v d")).then_inc(S("ld_w1"), 16)
            sp.dma_start(pe_rows[0:32], A["cmp_pe"][0].rearrange("v (q s) d -> (v q) (s d)", s=2)).then_inc(S("ld_w1"), 16)
            sp.wait_ge(S("zin_a"), 11)
            sp.wait_ge(S("zin_v"), 11)
            for n, (o_p, o_s) in enumerate(((2, 3), (4, 5), (6, 7))):
                c0 = 512 + 256 * n
                sp.dma_start(O[o_p][0, 0].rearrange("(i p) k g d -> p i (k g d)", p=P), z[:, 0:2, c0:c0 + 256]
                             ).then_inc(S("st_kv"), 16)
                if n < 2:
                    sp.dma_start(O[o_s][0].rearrange("b t k g d -> (b t) (k g d)"), z[0:NS, 2, c0:c0 + 256]
                                 ).then_inc(S("st_kv"), 16)
            for b in range(NB):
                sp.dma_start(O[7][0, b, WIN - TS:WIN].rearrange("t k g d -> t (k g d)"),
                             z[TS * b:TS * b + TS, 2, 1024:1280]).then_inc(S("st_kv"), 16)
            sp.dma_start(O[7][0, :, 0:WIN - TS].rearrange("b t k g d -> b (t k g d)"),
                         A["state_win"][0, :, TS:WIN].rearrange("b t k g d -> b (t k g d)")).then_inc(S("st_kv"), 16)
            load_pages(sp, (0, 1))
            sp.wait_ge(S("pair_ps"), 29)
            sp.wait_ge(S("st_kv"), 16 * 14)
            sp.dma_start(raw[0], O[2][0, 0].rearrange("(p s) k g d -> p (s k g d)", s=2)).then_inc(S("ld_raw0"), 16)
            sp.wait_ge(S("pre_ps"), 4)
            for b in range(NB):
                if b >= 2:
                    sp.wait_ge(S("key_ps"), b - 1)
                src = A["state_win"][0, b].rearrange("(n p) k g d -> p k n (g d)", p=P)
                sp.dma_start(kst[b % 2][:, 0:4], src[:, 0]).then_inc(S(f"ld_key{b % 2}"), 16)
                sp.dma_start(vpages[:, 4 * b:4 * b + 4], src[:, 1]).then_inc(S(f"ld_key{b % 2}"), 16)
            load_selected(sp, 0, "ld_key")
            sp.wait_ge(S("p_pv"), 6)
            sp.dma_start(lb, A["hg_lb_logits"][0:1].broadcast_to([P, 512])).then_inc(S("ld_hg"), 16)
            sp.dma_start(oml, A["hg_lb_logits"][1:2].broadcast_to([P, 512])).then_inc(S("ld_hg"), 16)
            sp.dma_start(hgn, A["hg_norm"][0:1].broadcast_to([P, P])).then_inc(S("ld_hg"), 16)
            sp.dma_start(wr, A["w_router"][0].rearrange("(k p) e -> p k e", p=P)).then_inc(S("ld_wr"), 16)
            sp.dma_start(br, A["b_router"][0:1].broadcast_to([P, E])).then_inc(S("ld_wr"), 16)
            sp.wait_ge(S("ohT_ps"), 2)
            sp.wait_ge(S("state"), 2)
            sp.dma_start(O[8][0, 0].rearrange("h k v -> k h v"), state).then_inc(S("st_state"), 16)
            sp.wait_ge(S("st_state"), 16)
            sp.dma_start(s0, A["state_hgrn"][0].rearrange("b h k v -> k (b h) v")).then_inc(S("ld_s0"), 16)
            sp.wait_ge(S("s_state"), 8)
            sp.dma_start(O[9][0].rearrange("b h k v -> k (b h) v"), s0).then_inc(S("st_state"), 16)
            sp.wait_ge(S("st_state"), 32)
            sp.wait_ge(S("ohT_ps"), 3)
            for g in range(G):
                sp.dma_start(wa[DH * g:DH * g + DH], A["w_branch_a"][0].rearrange("(g r d) n -> g d r n", g=G, r=R)[g]
                             ).then_inc(S("ld_wa"), 16)
            sp.dma_start(wb, A["w_branch_b"][0].rearrange("(h p) n -> p h n", p=P)).then_inc(S("ld_wa"), 16)
            sp.wait_ge(S("m_rows"), 3)
            for n in range(2):
                sp.dma_start(wo[n], A["w_out"][0][512 * n:512 * n + 512].rearrange("(k p) n -> p k n", p=P)).then_inc(S("ld_wo"), 16)
            w_up, w_down = A["w_up"][0], A["w_down"][0]
            sp.wait_ge(S("scattered"), 16 * 12)
            after(sp, "tab")
            last_of = lambda e: sp.value_load(tab[0:1, bass.ds(e, 1)], min_val=0, max_val=CMAX - 1)

            def load_expert(e, j, first):
                two_back = None if first and j < 2 else last_of(e + (2 * E - 2))
                back = None if first and j < 1 else last_of(e + (2 * E - 1))
                for q in range(12):
                    before, part = (two_back, q + 8) if q < 4 else (back, q - 4)
                    if before is not None:
                        sp.wait_ge(S("piece_used"), before * 12 + (part + 1))
                    pos = (12 * j + q) % 16
                    if q < 8:
                        src = w_up[bass.ds(e, 1)].squeeze(0)[P * q:P * q + P]
                        dst = ring[pos]
                    else:
                        src = w_down[bass.ds(e, 1)].squeeze(0)[2 * P * (q - 8):2 * P * (q - 7)].rearrange("(k p) n -> p k n", p=P)
                        dst = ring[pos].rearrange("p (k n) -> p k n", k=2)
                    sp.dma_start(dst, src).then_inc(S(f"ld_piece{pos}"), 16)
                    if q == 3:
                        at = 32 * (j % 2)
                        sp.dma_start(bias[at:at + 1, 0:2 * D], A["b_up"][0][bass.ds(e, 1)]).then_inc(S(f"ld_bias{j % 2}"), 16)
                        sp.dma_start(bias[at:at + 1, 2 * D:3 * D], A["b_down"][0][bass.ds(e, 1)]).then_inc(S(f"ld_bias{j % 2}"), 16)

            for j in range(4):
                load_expert(j, j, True)
            with sp.Fori(1, E // 4) as grp:
                for j in range(4):
                    load_expert(grp * 4 + j, j, False)
            sp.wait_ge(S("y2"), 2)
            sp.dma_start(O[0][0].rearrange("(i p) d -> p i d", p=P), x[:, 0:2]).then_inc(S("st_y2"), 16)
            sp.wait_ge(S("y2"), 3)
            sp.dma_start(O[1].rearrange("b t d -> (b t) d"), x[0:NS, 2]).then_inc(S("st_y2"), 16)
            sp.wait_ge(S("st_y2"), 32)
            sp.wait_ge(S("st_kv"), 16 * 14)
            sp.wait_ge(S("st_state"), 32)

        @block.tensor
        def _(pe):
            mm = nc.tensor.matmul
            pe.wait_ge(S("ld_const"), 16)
            after(pe, "silu_c")
            for k in range(KD):
                last = nc.tensor.transpose(banks[0][:, 32 * k:32 * k + 32], sc32[0:32, P * k:P * k + P], ident[0:32, 0:32])
            last.then_inc(S("sct_ps"), 1)
            after(pe, "sct")
            for n in range(12):
                pe.wait_ge(S(f"ld_slab{n % 3}"), 16 * (n // 3 + 1))
                if n >= 2:
                    pe.wait_ge(S("mod_v"), n - 1)
                for k in range(KD):
                    for j in range(4):
                        last = mm(banks[1 + n % 2][32 * j:32 * j + 32, 0:P], scT[:, k], slabs[n % 3][:, k, P * j:P * j + P],
                                  start=k == 0, stop=k == KD - 1)
                last.then_inc(S("mod_mm"), 1)

            def spread(q, n0):
                pe.wait_ge(S("bc"), q) if q else None
                for n in range(2):
                    for j in range(4):
                        mm(banks[3 + n][:, P * j:P * j + P], C("selp")[:, P * j:P * j + P], mod[:, n0 + n],
                           start=True, stop=True)
                        last = mm(banks[5 + n][0:32, P * j:P * j + P], C("sels")[:, 32 * j:32 * j + 32], mod[:, n0 + n],
                                  start=True, stop=True)
                last.then_inc(S("bc_ps"), 1)

            after(pe, "mod_w")
            spread(0, 2)
            spread(1, 0)
            spread(2, 4)

            def rows_to_hT(i, seq):
                pe.wait_ge(S("h_rows"), seq + 1)
                for k in range(KD):
                    last = nc.tensor.transpose(banks[(0, 7)[k // 4]][:, (k % 4) * P:(k % 4) * P + ROWS[i]],
                                               h_rows[0:ROWS[i], P * k:P * k + P], ident[0:ROWS[i], 0:ROWS[i]])
                last.then_inc(S("hT_ps"), 1)

            for i in range(3):
                if i:
                    pe.wait_ge(S("hT"), i)
                rows_to_hT(i, i)
            pe.wait_ge(S("hT"), 3)
            for n in range(11):
                m = 12 + n
                w = min(512, IN_W - 512 * n)
                b0, b1, b2 = (banks[1 + 3 * (n % 2) + v] for v in range(3))
                pe.wait_ge(S(f"ld_slab{m % 3}"), 16 * (m // 3 + 1 + (7 if m % 3 == 0 else 0)))
                if n == 0:
                    pe.wait_ge(S("bc"), 3)
                if n >= 2:
                    pe.wait_ge(S("zin_a"), n - 1)
                    pe.wait_ge(S("zin_v"), n - 1)
                slab = slabs[m % 3]
                for k in range(KD):
                    first, final = k == 0, k == KD - 1
                    mm(b0[:, 0:w], hT[:, k, 0:P], slab[:, k, 0:w], start=first, stop=final)
                    mm(b1[:, 0:w], hT[:, k, P:2 * P], slab[:, k, 0:w], start=first, stop=final)
                    for j in range(-(-w // P)):
                        wj = min(P, w - P * j)
                        last = mm(b2[32 * j:32 * j + 32, 0:wj], hT[:, k, 2 * P:2 * P + NS], slab[:, k, P * j:P * j + wj],
                                  start=first, stop=final)
                last.then_inc(S("zin_mm"), 1)
            pe.wait_ge(S("ld_w1"), 48)
            pe.wait_ge(S("zin_a"), 11)
            pe.wait_ge(S("zin_v"), 11)
            nc.tensor.transpose(banks[4][:, 0:32], pe_rows[0:32], ident[0:32, 0:32]).then_inc(S("peT_ps"), 1)

            def unit(v):
                for c in range(4):
                    last = nc.tensor.transpose(banks[v][:, P * c:P * c + P], raw[v][:, P * c:P * c + P], ident)
                last.then_inc(S("pair_ps"), 1)

            with pe.Fori(0, NB) as b:
                for v in range(4):
                    pe.wait_ge(S(f"ld_raw{v}"), 32 * b + 32)
                    pe.wait_ge(S(f"pair_out{v}"), b)
                    unit(v)
            pe.wait_ge(S("ld_raw0"), 32 * NB + 16)
            pe.wait_ge(S("pair_out0"), NB)
            unit(0)
            after(pe, "peT")
            for v in range(2):
                for q in range(16):
                    last = mm(banks[5][:, 64 + v:65 + v], w1[:, v, q], peT[:, 16 * v + q:16 * v + q + 1], start=q == 0, stop=q == 15)
            last.then_inc(S("pconst_ps"), 1)
            for v in range(4):
                pe.wait_ge(S(f"pair_out{v}"), NB + (v == 0))
            after(pe, "pconst")
            for vg in range(4):
                v, g = vg // 2, vg % 2
                src = pairT[:, v, g, 0:NB * 512].rearrange("p (b c) -> p b c", b=NB)
                own = pairT[:, v, g, NB * 512:UN * P]
                for q in range(16):
                    mm(banks[vg][:, 0:NB * NCMP], w1[:, v, q], src[:, :, q:q + 8 * NCMP - 7:8], start=q == 0, stop=q == 15)
                for q in range(16):
                    last = mm(banks[4 + vg][:, 0:NCMP_P], w1[:, v, q], own[:, q:q + 8 * NCMP_P - 7:8],
                              start=q == 0, stop=q == 15)
                last.then_inc(S("pre_ps"), 1)
            pe.wait_ge(S("gelu"), 4)
            for g in range(2):
                mm(banks[4][DH * g:DH * g + DH, 0:NB * NCMP], w2[:, 0], geT[:, 0, g, 0:NB * NCMP], start=True, stop=True)
            for g in range(2):
                last = mm(banks[6][DH * g:DH * g + DH, 0:NCMP_P], w2[:, 0], geT[:, 0, g, NB * NCMP:NC_ALL], start=True, stop=True)
            for b in range(NB + 1):
                n, at = (NCMP, P * (b % 4)) if b < NB else (NCMP_P, P)
                for g in range(2):
                    last = mm(banks[(0, 1, 5)[b // 4]][0:n, at + DH * g:at + DH * g + DH], geT[:, 1, g, NCMP * b:NCMP * b + n],
                              w2[:, 1], start=True, stop=True)
            last.then_inc(S("comp_ps"), 1)

            for r in range(R):
                nc.tensor.transpose(banks[7][:, NS * r:NS * r + NS], z[0:NS, 2, P * r:P * r + P], ident[0:NS, 0:NS])
            for n, name in enumerate(("ks", "kw")):
                last = nc.tensor.transpose(banks[7][:, P + NS * n:P + NS * n + NS], zc(2, name, P), ident[0:NS, 0:NS])
            last.then_inc(S("sq_ps"), 1)
            after(pe, "sg_gate")
            mm(banks[2][:, 0:24], C("expand", NS), sg_gate[0:NS, 2], start=True, stop=True).then_inc(S("sgate_ps"), 1)
            after(pe, "comp_a")
            after(pe, "comp_v")
            after(pe, "sq")
            qb = lambda g, b: qz[DH * g:DH * g + DH, 144 * b - 16 * b:144 * b - 16 * b + P]
            for g in range(G):
                for b in range(NB):
                    last = mm(banks[(1, 3)[g]][:, 0:NCMP], qb(g, b), kcT[DH * g:DH * g + DH, NCMP * b:NCMP * b + NCMP],
                              start=b == 0, stop=b == NB - 1)
            last.then_inc(S("score_ps"), 1)
            after(pe, "imp")
            mm(banks[5][:, 0:32], C("gsum"), imp, start=True, stop=True).then_inc(S("imp_ps"), 1)

            def probs_T(branch, tiles, new, seq):
                pe.wait_ge(S("probs"), branch + 1)
                for t in range(tiles + new):
                    n = P if t < tiles else NS
                    if branch == 0:
                        n = NCMP
                    if t % 2 == 0 and seq + t // 2 >= 2:
                        pe.wait_ge(S("pT"), seq + t // 2 - 1)
                    for g in range(G):
                        last = nc.tensor.transpose(banks[6 + (seq + t // 2) % 2][0:n, (t % 2) * 256 + P * g:(t % 2) * 256 + P * g + P],
                                                   sS[:, g, P * t:P * t + n], ident)
                    if t % 2 == 1 or t == tiles + new - 1:
                        last.then_inc(S("pT_ps"), 1)

            def values(branch, tiles, vname, seq_end):
                pe.wait_ge(S("pT"), seq_end)
                for b in range(NB):
                    for t in range(tiles):
                        if branch == 0:
                            last = mm(banks[0][:, 32 * b:32 * b + 32], vcb[0:NCMP, b], pTs[0:NCMP, 0, :, 16 * b:16 * b + 16],
                                      start=True, stop=True)
                        else:
                            mm(banks[0][:, 32 * b:32 * b + 32], vpages[:, tiles * b + t], pTs[:, t, :, 16 * b:16 * b + 16],
                               start=t == 0, stop=False)
                    if branch:
                        last = mm(banks[0][:, 32 * b:32 * b + 32], zc(2, vname, P), pTs[0:NS, tiles, :, 16 * b:16 * b + 16],
                                  start=False, stop=True)
                last.then_inc(S("pv_ps"), 1)

            def keys(branch, tiles):
                base = NB * (branch - 1)
                width = P * tiles

                def score(b):
                    pe.wait_ge(S("key_a"), base + b + 1)
                    pe.wait_ge(S("key_v"), base + b + 1)
                    for c in range(0, width, 512):
                        for g in range(G):
                            last = mm(banks[1 + 2 * g + c // 512][:], qb(g, b), kTb[b % 2][DH * g:DH * g + DH, c:c + 512],
                                      start=b == 0, stop=b == NB - 1)
                    last.then_inc(S("score_b"), 1)

                for b in range(NB):
                    pe.wait_ge(S(f"ld_key{b % 2}"), 32 * (b // 2 + 1) if branch == 1 else 128 + 64 * (b // 2 + 1))
                    if branch == 2:
                        pe.wait_ge(S(f"ld_key_p{b % 2}"), 64 * (b // 2 + 1))
                    if base + b:
                        pe.wait_ge(S("key_a"), base + b)
                        pe.wait_ge(S("key_v"), base + b)
                    for t in range(tiles):
                        last = nc.tensor.transpose(banks[6 + 2 * t // tiles][:, P * (t % (tiles // 2)):P * (t % (tiles // 2)) + P],
                                                   kst[b % 2][:, t], ident)
                    last.then_inc(S("key_ps"), 1)
                    if b:
                        score(b - 1)
                score(NB - 1)
                for g in range(G):
                    last = mm(banks[(5, 0)[g]][:, 0:NS], qf[DH * g:DH * g + DH].rearrange("p b r t -> p (b r t)"),
                              knT[DH * g:DH * g + DH, 2 - branch], start=True, stop=True)
                last.then_inc(S("score_ps"), 1)

            probs_T(0, 1, 0, 0)
            values(0, 1, None, 1)
            pe.wait_ge(S("oS"), 1)
            keys(1, 4)
            probs_T(1, 4, 1, 1)
            values(1, 4, "vw", 4)
            pe.wait_ge(S("oS"), 2)
            keys(2, 8)
            probs_T(2, 8, 1, 4)
            values(2, 8, "vs", 9)

            for i in range(2):
                pe.wait_ge(S("scores_in"), 3) if i == 0 else pe.wait_ge(S("pq"), 1)
                for r in range(R):
                    nc.tensor.transpose(banks[1][:, P * r:P * r + P], z[:, i, P * r:P * r + P], ident)
                for n, name in enumerate(("ks", "kw")):
                    last = nc.tensor.transpose(banks[2][:, P * n:P * n + P], zc(i, name, P), ident)
                last.then_inc(S("pq_ps"), 1)
            pe.wait_ge(S("pq"), 2)
            pe.wait_ge(S("oS"), 3)
            u = 0
            for i in range(2):
                for branch in range(3):
                    width = P * (i + 1) if branch else NCMP_P
                    if u:
                        pe.wait_ge(S("p_in"), u)
                    for h in range(H):
                        g, r = h // R, h % R
                        key = kT[DH * g:DH * g + DH, branch - 1, 0:width] if branch else \
                            kcT[DH * g:DH * g + DH, NB * NCMP:NC_ALL]
                        last = mm(banks[h // 2][:, 256 * (h % 2):256 * (h % 2) + width],
                                  qT[DH * g:DH * g + DH, r, P * i:P * i + P], key, start=True, stop=True)
                    last.then_inc(S("p_score"), 1)
                    pe.wait_ge(S("p_probs"), u + 1)
                    tiles = i + 1 if branch else 1
                    n = P if branch else NCMP_P
                    for t in range(tiles):
                        if t or u:
                            pe.wait_ge(S("ppT_a"), _ppt(i, branch) + t)
                            pe.wait_ge(S("ppT_v"), _ppt(i, branch) + t)
                        for h in range(H):
                            last = nc.tensor.transpose(banks[4 + h // 4][0:n, P * (h % 4):P * (h % 4) + P],
                                                       sP[:, h, P * t:P * t + n], ident)
                        last.then_inc(S("ppT_ps"), 1)
                    pe.wait_ge(S("ppT_a"), _ppt(i, branch) + tiles)
                    pe.wait_ge(S("ppT_v"), _ppt(i, branch) + tiles)
                    if u:
                        pe.wait_ge(S("on"), u)
                    for h in range(H):
                        g = h // R
                        for t in range(tiles):
                            if branch:
                                o = OFF[("vs", "vw")[branch - 1]] + DH * g
                                val = z[:, t, o:o + DH]
                            else:
                                val = vcb[0:NCMP_P, NB, DH * g:DH * g + DH]
                            c = P * (h % R) + DH * g
                            last = mm(banks[6][:, c:c + DH], pTp[0:n, t, h], val, start=t == 0, stop=t == tiles - 1)
                    last.then_inc(S("p_pv"), 1)
                    u += 1
            for i in range(2):
                if i:
                    pe.wait_ge(S("onT"), 1)
                else:
                    pe.wait_ge(S("on"), 6)
                for r in range(R):
                    last = nc.tensor.transpose(banks[0][:, P * r:P * r + P], on[:, i, P * r:P * r + P], ident)
                last.then_inc(S("onT_ps"), 1)
            def hgrn_inputs(i):
                r = ROWS[i]
                for h in range(HH):
                    c = slice(DK * h, DK * h + DK)
                    o = slice(r * h, r * h + r)
                    mm(banks[1][:, o], gl[0:r, i, c], C("tri") if i < 2 else C("bt32", NS), start=True, stop=True)
                    nc.tensor.transpose(banks[2][:, o], zc(i, "hq", 512)[:, c], ident[0:r, 0:r])
                    last = nc.tensor.transpose(banks[3][:, o], zc(i, "hf", 512)[:, c], ident[0:r, 0:r])
                last.then_inc(S("hg_ps"), 1)

            def hgrn_out(i, src):
                r = ROWS[i]
                pe.wait_ge(S("oh"), i + 1)
                if i:
                    pe.wait_ge(S("ohT"), i)
                for h in range(HH):
                    last = nc.tensor.transpose(banks[7][:, P * h:P * h + r], src[0:r, h], ident[0:r, 0:r])
                last.then_inc(S("ohT_ps"), 1)

            pe.wait_ge(S("onT"), 2)
            after(pe, "hk")
            after(pe, "gl")
            for i in range(2):
                if i:
                    pe.wait_ge(S("hg_cp"), i)
                hgrn_inputs(i)
                for h in range(HH):
                    c = slice(DK * h, DK * h + DK)
                    v = zc(i, "hi", 512)[:, c]
                    pe.wait_ge(S("hk_d"), HH * i + h + 1)
                    for s in range(8):
                        last = mm(banks[4][:, 16 * s:16 * s + 16], dk[:, s], dq[:, s], start=True, stop=True)
                    last.then_inc(S("att_ps"), 1)
                    pe.wait_ge(S("att"), HH * i + h + 1)
                    if h == 0 and i:
                        pe.wait_ge(S("oh_cp"), i)
                    last = mm(banks[5][:, c], att, v, start=True, stop=i == 0)
                    if i:
                        pe.wait_ge(S("state"), i)
                        last = mm(banks[5][:, c], qe[:, h], state[:, h], start=False, stop=True)
                    last.then_inc(S("o_ps"), 1)
                pe.wait_ge(S("kd"), i + 1)
                for h in range(HH):
                    last = nc.tensor.transpose(banks[6][:, P * h:P * h + P], dk[:, h], ident)
                last.then_inc(S("kh_ps"), 1)
                pe.wait_ge(S("kh"), i + 1)
                for h in range(HH):
                    c = slice(DK * h, DK * h + DK)
                    last = mm(banks[6][:, c], kh[:, c], zc(i, "hi", 512)[:, c], start=True, stop=True)
                last.then_inc(S("st_ps"), 1)
                hgrn_out(i, oh)
            pe.wait_ge(S("hg_cp"), 2)
            hgrn_inputs(2)
            after(pe, "s_kq")
            for h in range(HH):
                last = mm(banks[4][0:NS, NS * h:NS * h + NS], sb_[:, 5, h], sb_[:, 4, h], start=True, stop=True)
            last.then_inc(S("att_ps"), 1)
            for h in range(HH):
                last = nc.tensor.transpose(banks[6][0:NS, P * h:P * h + P], sb_[:, 6, h], ident)
            last.then_inc(S("kh_ps"), 1)
            pe.wait_ge(S("att"), 2 * HH + 1)
            pe.wait_ge(S("ld_s0"), 16)
            pe.wait_ge(S("oh_cp"), 2)
            for h in range(HH):
                c = slice(DK * h, DK * h + DK)
                mm(banks[5][0:NS, c], att_s[0:NS, h], zc(2, "hi", 512)[:, c], start=True, stop=False)
                for b in range(NB):
                    last = mm(banks[5][0:NS, c], qep[:, h, NS * b:NS * b + NS], s0[:, HH * b + h], start=False, stop=b == NB - 1)
            last.then_inc(S("o_ps"), 1)
            pe.wait_ge(S("kh"), 3)
            after(pe, "vm")
            for n in range(8):
                h, half = n // 2, n % 2
                if n >= 2:
                    pe.wait_ge(S("s_state"), n - 1)
                mm(banks[n % 2][:], kh_s[0:NS, DK * h:DK * h + DK], vm[0:NS, 4 * half:4 * half + 4, DK * h:DK * h + DK],
                   start=True, stop=True).then_inc(S("sst_ps"), 1)
            hgrn_out(2, oh_s)

            pe.wait_ge(S("ld_wa"), 48)
            after(pe, "onS")
            pe.wait_ge(S("ohT"), 3)
            pe.wait_ge(S("s_state"), 8)
            for i in range(3):
                t = slice(P * i, P * i + ROWS[i])
                if i:
                    pe.wait_ge(S("m_rows"), i)
                for n in range(2):
                    for k in range(4):
                        mm(banks[n][0:ROWS[i], :], onT[:, k, t], wa[:, k, 512 * n:512 * n + 512], start=k == 0, stop=k == 3)
                    for k in range(4):
                        last = mm(banks[2 + n][0:ROWS[i], :], ohT[:, k, t], wb[:, k, 512 * n:512 * n + 512], start=k == 0, stop=k == 3)
                last.then_inc(S("mrg_ps"), 1)
                pe.wait_ge(S("m_rows"), i + 1)
                if i:
                    pe.wait_ge(S("mT"), i)
                for k in range(KD):
                    last = nc.tensor.transpose(banks[4 + k // 4][:, (k % 4) * P:(k % 4) * P + ROWS[i]],
                                               mrow[0:ROWS[i], P * k:P * k + P], ident[0:ROWS[i], 0:ROWS[i]])
                last.then_inc(S("mT_ps"), 1)
            pe.wait_ge(S("ld_wo"), 32)
            pe.wait_ge(S("mT"), 3)
            for i in range(3):
                t = slice(P * i, P * i + ROWS[i])
                if i:
                    pe.wait_ge(S("out_cp"), i)
                for n in range(2):
                    for k in range(KD):
                        last = mm(banks[6 + n][0:ROWS[i], :], mT[:, k, t], wo[k // 4][:, k % 4, 512 * n:512 * n + 512],
                                  start=k == 0, stop=k == KD - 1)
                last.then_inc(S("out_ps"), 1)
            pe.wait_ge(S("out_cp"), 3)
            spread(3, 8)
            spread(4, 6)
            spread(5, 10)
            for i in range(3):
                pe.wait_ge(S("h2"), i + 1)
                if i:
                    pe.wait_ge(S("h2T"), i)
                for k in range(KD):
                    last = nc.tensor.transpose(banks[(0, 7)[k // 4]][:, (k % 4) * P:(k % 4) * P + ROWS[i]],
                                               h2r[0:ROWS[i], i, P * k:P * k + P], ident[0:ROWS[i], 0:ROWS[i]])
                last.then_inc(S("h2T_ps"), 1)
            pe.wait_ge(S("h2T"), 3)
            pe.wait_ge(S("ld_wr"), 32)
            for i in range(3):
                for k in range(KD):
                    last = mm(banks[1][0:ROWS[i], E * i:E * i + E], h2T[:, k, P * i:P * i + ROWS[i]], wr[:, k],
                              start=k == 0, stop=k == KD - 1)
            last.then_inc(S("lg_ps"), 1)
            pe.wait_ge(S("mk"), 3)
            for i in range(3):
                r = ROWS[i]
                o = slice(E * i, E * i + E)
                mm(banks[2][0:r, o], C("stri", r)[:, 0:r], mk[0:r, i], start=True, stop=i == 0)
                for v in range(i):
                    mm(banks[2][0:r, o], ones[:, 0:r], mk[:, v], start=False, stop=v == i - 1)
            for i in range(3):
                last = mm(banks[3][0:E, 0:P], mk[0:ROWS[i], i], ones[0:ROWS[i]], start=i == 0, stop=i == 2)
            last.then_inc(S("cnt_ps"), 1)
            after(pe, "nch")
            mm(banks[4][:, 0:E], nchT[0:E], C("stri", E)[:, 0:E], start=True, stop=True)
            mm(banks[4][:, E:2 * E], nchT[0:E], C("tri", E)[:, 0:E], start=True, stop=True).then_inc(S("base_ps"), 1)

            def chunk_T():
                for k in range(KD):
                    last = nc.tensor.transpose(banks[2][:, SLOT * k:SLOT * k + SLOT], xrow[0:SLOT, P * k:P * k + P],
                                               ident[0:SLOT, 0:SLOT])
                last.then_inc(S("xcT_ps"), 1)

            after(pe, "tab")
            pe.wait_ge(S("ld_x2"), 16)
            chunk_T()
            with pe.Fori(0, E // 4) as grp:
                for j in range(4):
                    before = pe.value_load(tab[0:1, bass.ds(grp * 4 + (E + j), 1)], min_val=0, max_val=CMAX)
                    upto = pe.value_load(tab[0:1, bass.ds(grp * 4 + j, 1)], min_val=1, max_val=CMAX)
                    with pe.Fori(before, upto) as c:
                        at = 32 * (j % 2)
                        pe.wait_ge(S("xcT"), c + 1)
                        pe.wait_ge(S(f"ld_bias{j % 2}"), grp * 64 + 32 * (j // 2) + 32)
                        one = ones[at:at + 1, 0:SLOT]
                        for part in range(2):
                            for s in range(2):
                                mm(banks[part][SLOT * s:SLOT * s + SLOT, :], one,
                                   bias[at:at + 1, D * part + 512 * s:D * part + 512 * s + 512], start=True, stop=False)
                        for q in range(8):
                            pos, use = (12 * j + q) % 16, (12 * j + q) // 16
                            pe.wait_ge(S(f"ld_piece{pos}"), grp * 48 + 16 * use + 16)
                            if q == 7:
                                pe.wait_ge(S("ld_x2"), c * 16 + 32)
                            for part in range(2):
                                for s in range(2):
                                    last = mm(banks[part][SLOT * s:SLOT * s + SLOT, :], xcT[:, q],
                                              ring[pos][:, D * part + 512 * s:D * part + 512 * s + 512], start=False, stop=q == 7)
                            last.then_inc(S("piece_used"), 1)
                        chunk_T()
                        pe.wait_ge(S("act"), c + 1)
                        for k in range(4):
                            last = nc.tensor.transpose(banks[3][:, P * k:P * k + P], ac[:, P * k:P * k + P], ident)
                        last.then_inc(S("aT_ps"), 1)
                        pe.wait_ge(S("yc"), c)
                        for s in range(2):
                            mm(banks[4][SLOT * s:SLOT * s + SLOT, :], one, bias[at:at + 1, 2 * D + 512 * s:2 * D + 512 * s + 512],
                               start=True, stop=False)
                        pe.wait_ge(S("aT"), c + 1)
                        for q in range(8, 12):
                            pos, use = (12 * j + q) % 16, (12 * j + q) // 16
                            pe.wait_ge(S(f"ld_piece{pos}"), grp * 48 + 16 * use + 16)
                            for v in range(2):
                                f = 2 * (q - 8) + v
                                lhs = aT[:, P * (f % 4) + SLOT * (f // 4):P * (f % 4) + SLOT * (f // 4) + SLOT]
                                for s in range(2):
                                    last = mm(banks[4][SLOT * s:SLOT * s + SLOT, :], lhs,
                                              ring[pos][:, D * v + 512 * s:D * v + 512 * s + 512], start=False, stop=f == 7)
                            last.then_inc(S("piece_used"), 1)

        @block.scalar
        def _(act):
            fn = nc.scalar.activation
            act.wait_ge(S("ld_c"), 32)
            after(act, "zeroed")
            fn(sc32[0:1 + NB], c9[0:1 + NB], ACT.Silu).then_inc(S("silu_c"), 1)

            def spread_out(q, dst):
                act.wait_ge(S("bc_ps"), q + 1)
                for n in range(2):
                    nc.scalar.copy(dst[:, 0, 512 * n:512 * n + 512], banks[3 + n][:])
                    last = nc.scalar.copy(dst[0:32, 1, 512 * n:512 * n + 512], banks[5 + n][0:32, :])
                last.then_inc(S("bc"), 1)

            spread_out(0, mod_rows[:, 0])
            spread_out(1, mod_rows[:, 1])
            spread_out(2, gate_rows)

            def root_mean_square(i, seq):
                r = ROWS[i]
                act.wait_ge(S("ss"), seq + 1)
                fn(rt_[0:r, i:i + 1], ss[0:r, i:i + 1], ACT.Sqrt, bias=eps_t[0:r], scale=1.0 / D).then_inc(S("rms"), 1)

            def hT_out(i, seq):
                act.wait_ge(S("hT_ps"), seq + 1)
                for v in range(2):
                    last = nc.scalar.copy(hT[:, 4 * v:4 * v + 4, P * i:P * i + ROWS[i]],
                                          banks[(0, 7)[v]][:].rearrange("p (k t) -> p k t", k=4)[:, :, 0:ROWS[i]])
                last.then_inc(S("hT"), 1)

            for i in range(3):
                root_mean_square(i, i)
                hT_out(i, i)
            for n in range(11):
                w = min(512, IN_W - 512 * n)
                b0, b1, b2 = (banks[1 + 3 * (n % 2) + v] for v in range(3))
                act.wait_ge(S("zin_mm"), n + 1)
                last = nc.scalar.copy(z[:, 0, 512 * n:512 * n + w], b0[:, 0:w])
                for j in range(0, -(-w // P), 2):
                    wj = min(P, w - P * j)
                    last = nc.scalar.copy(z[0:32, 2, 512 * n + P * j:512 * n + P * j + wj], b2[32 * j:32 * j + 32, 0:wj])
                last.then_inc(S("zin_a"), 1)
            act.wait_ge(S("zin_v"), 11)
            act.wait_ge(S("zin_a"), 11)
            fn(sg_gate[:, 0:2], z[:, 0:2, OFF["gn"]:OFF["gn"] + 24], ACT.Sigmoid)
            fn(sg_gate[0:NS, 2], zc(2, "gn", 24), ACT.Sigmoid).then_inc(S("sg_gate"), 1)

            with act.Fori(0, NB) as b:
                for v in (0, 2):
                    act.wait_ge(S("pair_ps"), 4 * b + v + 1)
                    for g in range(G):
                        for s in range(2):
                            last = nc.scalar.copy(pairT[DH * s:DH * s + DH, :, g, bass.ds((4 * b + v) * P, P)],
                                                  by_parity(banks[v])[DH * g:DH * g + DH, s])
                    last.then_inc(S(f"pair_out{v}"), 1)
            act.wait_ge(S("pair_ps"), 33)
            for g in range(G):
                for s in range(2):
                    last = nc.scalar.copy(pairT[DH * s:DH * s + DH, :, g, NB * 512:], by_parity(banks[0])[DH * g:DH * g + DH, s])
            last.then_inc(S("pair_out0"), 1)
            after(act, "pconst")
            for vg in range(4):
                v, g = vg // 2, vg % 2
                act.wait_ge(S("pre_ps"), vg + 1)
                fn(geT[:, v, g, 0:NB * NCMP], banks[vg][:, 0:NB * NCMP], ACT.Gelu_apprx_tanh, bias=pconst[:, v:v + 1])
                fn(geT[:, v, g, NB * NCMP:NC_ALL], banks[4 + vg][:, 0:NCMP_P], ACT.Gelu_apprx_tanh,
                   bias=pconst[:, v:v + 1]).then_inc(S("gelu"), 1)
            after(act, "comp_ps")
            nc.scalar.copy(kcT[:, 0:NB * NCMP], banks[4][:, 0:NB * NCMP])
            nc.scalar.copy(kcT[:, NB * NCMP:NC_ALL], banks[6][:, 0:NCMP_P]).then_inc(S("comp_a"), 1)

            def exps(branch, width):
                act.wait_ge(S("s_max"), branch + 1)
                for g in range(G):
                    last = fn(sS[:, g, 0:width], sS[:, g, 0:width], ACT.Exp, bias=sa_max[:, g:g + 1],
                              accum_out=sa_sum[:, g:g + 1])
                last.then_inc(S("s_exp"), 1)

            def probs_out(seq, n_banks, widths):
                for t in range(n_banks):
                    act.wait_ge(S("pT_ps"), seq + t + 1)
                    src = banks[6 + (seq + t) % 2][:].rearrange("p (t g r) -> p t g r", t=2, g=G)
                    for w in range(2):
                        if 2 * t + w < len(widths):
                            n = widths[2 * t + w]
                            last = nc.scalar.copy(pTs[0:n, 2 * t + w], src[0:n, w])
                    last.then_inc(S("pT"), 1)

            def keys_out(branch, tiles):
                for b in range(NB):
                    act.wait_ge(S("key_ps"), NB * (branch - 1) + b + 1)
                    if NB * (branch - 1) + b >= 2:
                        act.wait_ge(S("score_b"), NB * (branch - 1) + b - 1)
                    w = P * tiles // 2
                    nc.scalar.copy(kTb[b % 2][:, 0:w], banks[6][:, 0:w]).then_inc(S("key_a"), 1)

            exps(0, NCMP)
            probs_out(0, 1, [NCMP])
            keys_out(1, 4)
            exps(1, WIN_W)
            act.wait_ge(S("pv_ps"), 1)
            probs_out(1, 3, [P] * 4 + [NS])
            keys_out(2, 8)
            exps(2, SEL_W)
            act.wait_ge(S("pv_ps"), 2)
            probs_out(4, 5, [P] * 8 + [NS])

            for i in range(2):
                act.wait_ge(S("pq_ps"), i + 1)
                fn(qT[:, :, P * i:P * i + P], banks[1][:].rearrange("p (r t) -> p r t", r=R), ACT.Copy, scale=0.125)
                nc.scalar.copy(kT[:, :, P * i:P * i + P], banks[2][:, 0:256].rearrange("p (n t) -> p n t", n=2)
                               ).then_inc(S("pq"), 1)
            act.wait_ge(S("pv_ps"), 3)
            u, s = 0, 0
            for i in range(2):
                for branch in range(3):
                    width = P * (i + 1) if branch else NCMP_P
                    act.wait_ge(S("p_max"), u + 1)
                    for h in range(H):
                        last = fn(sP[:, h, 0:width], sP[:, h, 0:width], ACT.Exp, bias=pr_max[:, h:h + 1],
                                  accum_out=pr_sum[:, h:h + 1])
                    last.then_inc(S("p_exp"), 1)
                    tiles, n = (i + 1, P) if branch else (1, NCMP_P)
                    for t in range(tiles):
                        act.wait_ge(S("ppT_ps"), s + 1)
                        if u:
                            act.wait_ge(S("p_pv"), u)
                        nc.scalar.copy(pTp[0:n, t, 0:4], banks[4][0:n, :].rearrange("p (h t) -> p h t", h=4)
                                       ).then_inc(S("ppT_a"), 1)
                        s += 1
                    u += 1
            for i in range(2):
                act.wait_ge(S("onT_ps"), i + 1)
                nc.scalar.copy(onT[:, :, P * i:P * i + P], banks[0][:].rearrange("p (r t) -> p r t", r=R)).then_inc(S("onT"), 1)
            after(act, "lb_d")
            fn(lb, lb, ACT.Sigmoid).then_inc(S("lb"), 1)
            fn(z[:, 0:2, OFF["hf"]:OFF["hf"] + 512], z[:, 0:2, OFF["hf"]:OFF["hf"] + 512], ACT.Sigmoid)
            fn(zc(2, "hf", 512), zc(2, "hf", 512), ACT.Sigmoid).then_inc(S("hf_sig"), 1)
            fn(z[:, 0:2, OFF["ga"]:IN_W], z[:, 0:2, OFF["ga"]:IN_W], ACT.Sigmoid)
            fn(z[0:NS, 2, OFF["ga"]:IN_W], z[0:NS, 2, OFF["ga"]:IN_W], ACT.Sigmoid)
            for name in ("hq", "hg"):
                fn(z[:, 0:2, OFF[name]:OFF[name] + 512], z[:, 0:2, OFF[name]:OFF[name] + 512], ACT.Silu)
                fn(zc(2, name, 512), zc(2, name, 512), ACT.Silu)
            after(act, "f")
            fn(gl[:, 0:2], z[:, 0:2, OFF["hf"]:OFF["hf"] + 512], ACT.Ln)
            fn(gl[0:NS, 2], zc(2, "hf", 512), ACT.Ln).then_inc(S("gl"), 1)

            def hgrn_rms(i, src, sq):
                r = ROWS[i]
                act.wait_ge(S("hss"), i + 1)
                fn(hrt[0:r, 4 * i:4 * i + 4], hss[0:r, 4 * i:4 * i + 4], ACT.Sqrt, bias=eps_t[0:r], scale=1.0 / DK
                   ).then_inc(S("hrt"), 1)

            def hgrn_out_a(i):
                r = ROWS[i]
                act.wait_ge(S("ohT_ps"), i + 1)
                nc.scalar.copy(ohT[:, :, P * i:P * i + r], banks[7][:].rearrange("p (h t) -> p h t", h=HH)[:, :, 0:r]
                               ).then_inc(S("ohT"), 1)

            for i in range(2):
                act.wait_ge(S("hg_ps"), i + 1)
                if i:
                    act.wait_ge(S("kd"), i)
                    act.wait_ge(S("o_ps"), HH * i)
                    act.wait_ge(S("state"), i)
                nc.scalar.copy(bT, banks[1][:].rearrange("p (h t) -> p h t", h=HH))
                nc.scalar.copy(hqT, banks[2][:].rearrange("p (h t) -> p h t", h=HH))
                nc.scalar.copy(hkT, banks[3][:].rearrange("p (h t) -> p h t", h=HH)).then_inc(S("hg_cp"), 1)
                act.wait_ge(S("hg_cp"), i + 1)
                fn(ebT, bT, ACT.Exp).then_inc(S("ebT"), 1)
                for h in range(HH):
                    act.wait_ge(S("hd"), HH * i + h + 1)
                    fn(dk, dk, ACT.Exp)
                    fn(dq, dq, ACT.Exp).then_inc(S("he"), 1)
                act.wait_ge(S("kd_d"), i + 1)
                fn(dk[:, 0:4], dk[:, 0:4], ACT.Exp).then_inc(S("kd_e"), 1)
                act.wait_ge(S("kh_ps"), i + 1)
                nc.scalar.copy(kh, banks[6][:]).then_inc(S("kh"), 1)
                act.wait_ge(S("o_ps"), HH * (i + 1))
                if i:
                    act.wait_ge(S("ohT_ps"), i)
                nc.scalar.copy(oh, banks[5][:].rearrange("p (h v) -> p h v", h=HH)).then_inc(S("oh_cp"), 1)
                hgrn_rms(i, oh, osq)
                hgrn_out_a(i)
            act.wait_ge(S("hg_ps"), 3)
            after(act, "s_free")
            for n in range(3):
                last = nc.scalar.copy(sb_[:, n], banks[1 + n][:, 0:P].rearrange("p (h t) -> p h t", h=HH))
            last.then_inc(S("hg_cp"), 1)
            act.wait_ge(S("hg_cp"), 3)
            fn(sb_[:, 3], sb_[:, 0], ACT.Exp)
            fn(sb_[:, 5], sb_[:, 0], ACT.Exp, scale=-1.0).then_inc(S("ebT"), 1)
            act.wait_ge(S("kd_d"), 3)
            fn(sb_[:, 6], sb_[:, 6], ACT.Exp).then_inc(S("kd_e"), 1)
            act.wait_ge(S("kh_ps"), 3)
            nc.scalar.copy(kh_s[0:NS], banks[6][0:NS, :]).then_inc(S("kh"), 1)
            act.wait_ge(S("o_ps"), 2 * HH + 1)
            nc.scalar.copy(oh_s[0:NS], banks[5][0:NS, :].rearrange("p (h v) -> p h v", h=HH)).then_inc(S("oh_cp"), 1)
            hgrn_rms(2, oh_s, osq_s)
            hgrn_out_a(2)

            for i in range(3):
                act.wait_ge(S("mT_ps"), i + 1)
                for v in range(2):
                    last = nc.scalar.copy(mT[:, 4 * v:4 * v + 4, P * i:P * i + ROWS[i]],
                                          banks[4 + v][:].rearrange("p (k t) -> p k t", k=4)[:, :, 0:ROWS[i]])
                last.then_inc(S("mT"), 1)
            for i in range(3):
                r = ROWS[i]
                act.wait_ge(S("out_ps"), i + 1)
                if i:
                    act.wait_ge(S("y1"), i)
                for n in range(2):
                    last = nc.scalar.copy(orow[0:r, 512 * n:512 * n + 512], banks[6 + n][0:r, :])
                last.then_inc(S("out_cp"), 1)
                root_mean_square(i, 3 + i)
            act.wait_ge(S("y1"), 3)
            spread_out(3, mod_rows[:, 0])
            spread_out(4, mod_rows[:, 1])
            spread_out(5, gate_rows)
            for i in range(3):
                root_mean_square(i, 6 + i)
                act.wait_ge(S("h2T_ps"), i + 1)
                for v in range(2):
                    last = nc.scalar.copy(h2T[:, 4 * v:4 * v + 4, P * i:P * i + ROWS[i]],
                                          banks[(0, 7)[v]][:].rearrange("p (k t) -> p k t", k=4)[:, :, 0:ROWS[i]])
                last.then_inc(S("h2T"), 1)
            for i in range(3):
                r = ROWS[i]
                act.wait_ge(S("top"), i + 1)
                fn(wts[0:r, i], top8[0:r, 0:4], ACT.Exp, bias=negtop[0:r], accum_out=wsum[0:r]).then_inc(S("wexp"), 1)

            after(act, "tab")
            n_chunks = act.value_load(tab[0:1, E - 1:E], min_val=E, max_val=CMAX)
            act.wait_ge(S("xcT_ps"), 1)
            act.wait_ge(S("scattered"), 16 * 12)
            nc.scalar.copy(xcT, banks[2][:].rearrange("p (k s) -> p k s", s=SLOT)).then_inc(S("xcT"), 1)
            with act.Fori(0, n_chunks) as c:
                act.wait_ge(S("gate"), c + 1)
                fn(sg, gt, ACT.Sigmoid, scale=1.702).then_inc(S("sig"), 1)
                act.wait_ge(S("xcT_ps"), c + 2)
                nc.scalar.copy(xcT, banks[2][:].rearrange("p (k s) -> p k s", s=SLOT)).then_inc(S("xcT"), 1)
                act.wait_ge(S("piece_used"), c * 12 + 12)
                act.wait_ge(S("st_yc"), c * 32)
                nc.scalar.copy(yc, banks[4][:]).then_inc(S("yc"), 1)
            act.wait_ge(S("st_yc"), n_chunks * 32)
            nc.scalar.copy(gathered, eps_t).then_inc(S("all_out"), 1)
            for i in range(3):
                root_mean_square(i, 9 + i)

        @block.vector
        def _(dve):
            V = nc.vector
            V.memset(sc32[0:32], 0.0).then_inc(S("zeroed"), 1)
            V.memset(ones, 1.0)
            V.memset(eps_t, EPS)
            V.memset(zero_t, 0.0).then_inc(S("zero_t"), 1)
            after(dve, "sct_ps")
            V.tensor_copy(scT, banks[0][:, 0:KD * 32].rearrange("p (k r) -> p k r", r=32)).then_inc(S("sct"), 1)
            dve.wait_ge(S("ld_bada"), 64)
            for n in range(12):
                dve.wait_ge(S("mod_mm"), n + 1)
                V.tensor_tensor(mod[:, n], banks[1 + n % 2][:, 0:P], bada[:, n], ALU.add).then_inc(S("mod_v"), 1)
            dve.wait_ge(S("ld_wn"), 256)
            dve.wait_ge(S("mod_v"), 12)
            V.scalar_tensor_tensor(mod[:, 2:4], mod[:, 2:4], 1.0, wn[:, 0:2], ALU.add, ALU.mult)
            V.tensor_tensor(mod[:, 4:6], mod[:, 4:6], wn[:, 2:4], ALU.mult)
            V.scalar_tensor_tensor(mod[:, 8:10], mod[:, 8:10], 1.0, wn[:, 4:6], ALU.add, ALU.mult)
            V.tensor_tensor(mod[:, 10:12], mod[:, 10:12], wn[:, 6:8], ALU.mult).then_inc(S("mod_w"), 1)

            def normed_rows(i, seq, reuse):
                r, ps = ROWS[i], i // 2
                if reuse is not None:
                    dve.wait_ge(S("hT_ps"), reuse)
                link(dve, "dve", V.tensor_tensor_reduce(h_rows[0:r], x[0:r, i], x[0:r, i], 1.0, 0.0, ALU.mult, ALU.add,
                                                        ss[0:r, i:i + 1]))
                V.tensor_copy(ss[0:r, 3:4], ss[0:r, i:i + 1]).then_inc(S("ss"), 1)
                dve.wait_ge(S("rms"), seq + 1)
                link(dve, "dve", V.reciprocal(rstd[0:r, i:i + 1], rt_[0:r, i:i + 1]))
                link(dve, "dve", V.scalar_tensor_tensor(h_rows[0:r], x[0:r, i], rstd[0:r, i:i + 1], mod_rows[0:r, 0, ps],
                                                        ALU.mult, ALU.mult))
                V.tensor_tensor(h_rows[0:r], h_rows[0:r], mod_rows[0:r, 1, ps], ALU.add).then_inc(S("h_rows"), 1)

            dve.wait_ge(S("ld_x"), 32)
            dve.wait_ge(S("bc"), 2)
            for i in range(3):
                normed_rows(i, i, i if i else None)
            for n in range(11):
                w = min(512, IN_W - 512 * n)
                b0, b1, b2 = (banks[1 + 3 * (n % 2) + v] for v in range(3))
                dve.wait_ge(S("zin_mm"), n + 1)
                last = V.tensor_copy(z[:, 1, 512 * n:512 * n + w], b1[:, 0:w])
                for j in range(1, -(-w // P), 2):
                    wj = min(P, w - P * j)
                    last = V.tensor_copy(z[0:32, 2, 512 * n + P * j:512 * n + P * j + wj], b2[32 * j:32 * j + 32, 0:wj])
                last.then_inc(S("zin_v"), 1)
            after(dve, "peT_ps")
            V.tensor_copy(peT, banks[4][:, 0:32]).then_inc(S("peT"), 1)
            with dve.Fori(0, NB) as b:
                for v in (1, 3):
                    dve.wait_ge(S("pair_ps"), 4 * b + v + 1)
                    for g in range(G):
                        for s in range(2):
                            last = V.tensor_copy(pairT[DH * s:DH * s + DH, :, g, bass.ds((4 * b + v) * P, P)],
                                                 by_parity(banks[v])[DH * g:DH * g + DH, s])
                    last.then_inc(S(f"pair_out{v}"), 1)
            after(dve, "pconst_ps")
            V.tensor_copy(pconst, banks[5][:, 64:66]).then_inc(S("pconst"), 1)
            after(dve, "comp_ps")
            V.tensor_copy(vcb[0:NCMP, 0:4], banks[0][0:NCMP, :].rearrange("p (b c) -> p b c", b=4))
            V.tensor_copy(vcb[0:NCMP, 4:8], banks[1][0:NCMP, :].rearrange("p (b c) -> p b c", b=4))
            V.tensor_copy(vcb[0:NCMP_P, 8], banks[5][0:NCMP_P, P:2 * P]).then_inc(S("comp_v"), 1)

            V.memset(imp, 0.0)
            link(dve, "dve", V.memset(qz, 0.0))
            after(dve, "sq_ps")
            link(dve, "dve", V.tensor_scalar(qf.rearrange("p b r t -> p r b t"),
                                             banks[7][:, 0:P].rearrange("p (r b t) -> p r b t", r=R, b=NB), 0.125, None, ALU.mult))
            V.tensor_copy(qz.rearrange("p (b c) -> p b c", c=144)[:, :, 0:16], qf.rearrange("p b r t -> p b (r t)"))
            V.tensor_copy(knT, banks[7][:, P:P + 2 * NS].rearrange("p (n t) -> p n t", n=2)).then_inc(S("sq"), 1)
            after(dve, "sgate_ps")
            link(dve, "dve", V.tensor_tensor(sa_gate3.rearrange("p (a r) -> p a r", r=R),
                                             banks[2][:, 0:24].rearrange("p (a r) -> p a r", r=R),
                                             C("rdiag").unsqueeze(1).broadcast_to([P, 6, R]), ALU.mult))
            link(dve, "dve", V.tensor_reduce(sa_gate, sa_gate3.rearrange("p (a r) -> p a r", r=R), AX, ALU.add))

            def softmax(branch, width):
                link(dve, "dve", V.tensor_reduce(sa_coef, sS[:, :, 0:width], AX, ALU.max))
                V.tensor_scalar(sa_max, sa_coef, -1.0, None, ALU.mult).then_inc(S("s_max"), 1)
                dve.wait_ge(S("s_exp"), branch + 1)
                link(dve, "dve", V.reciprocal(sa_coef, sa_sum))
                if branch == 0:
                    for g in range(G):
                        link(dve, "dve", V.tensor_scalar(sS[:, g, 0:width], sS[:, g, 0:width], sa_coef[:, g:g + 1], None, ALU.mult))
                    imp3 = imp.rearrange("p (g j) -> p g j", g=G)
                    for g in range(G):
                        last = V.tensor_reduce(imp3[:, g, 0:14], sS[:, g, 4:60].rearrange("p (j s) -> p j s", s=4), AX, ALU.add)
                    link(dve, "dve", last)
                    V.tensor_tensor(imp3[:, :, 0:14], imp3[:, :, 0:14], sS[:, :, 3:56:4], ALU.add).then_inc(S("imp"), 1)
                    gates = sa_gate[:, 0:2]
                    after(dve, "imp")
                    for g in range(G):
                        last = V.tensor_scalar(sS[:, g, 0:width], sS[:, g, 0:width], gates[:, g:g + 1], None, ALU.mult)
                    last.then_inc(S("probs"), 1)
                else:
                    gates = sa_gate[:, 4:6] if branch == 1 else sa_gate[:, 2:4]
                    link(dve, "dve", V.tensor_tensor(sa_coef, sa_coef, gates, ALU.mult))
                    for g in range(G):
                        last = V.tensor_scalar(sS[:, g, 0:width], sS[:, g, 0:width], sa_coef[:, g:g + 1], None, ALU.mult)
                    last.then_inc(S("probs"), 1)

            def keys_out_v(branch, tiles):
                for b in range(NB):
                    dve.wait_ge(S("key_ps"), NB * (branch - 1) + b + 1)
                    if NB * (branch - 1) + b >= 2:
                        dve.wait_ge(S("score_b"), NB * (branch - 1) + b - 1)
                    w = P * tiles // 2
                    V.tensor_copy(kTb[b % 2][:, w:2 * w], banks[7][:, 0:w]).then_inc(S("key_v"), 1)

            def biased(g, c, w, bank, nd):
                return V.scalar_tensor_tensor(sS[:, g, c:c + w], nd, C("slope")[:, g:g + 1], bank[:, 0:w], ALU.mult, ALU.add)

            dve.wait_ge(S("score_ps"), 1)
            biased(0, 0, NCMP, banks[1], C("ndcs")[:, 0:NCMP])
            link(dve, "dve", biased(1, 0, NCMP, banks[3], C("ndcs")[:, 0:NCMP]))
            softmax(0, NCMP)
            after(dve, "imp_ps")
            impg3 = impg.rearrange("p (g j) -> p g j", g=G)
            cand3 = cand.rearrange("p (g j) -> p g j", g=G)
            link(dve, "dve", V.tensor_copy(impg, banks[5][:, 0:32]))
            link(dve, "dve", V.tensor_reduce(lowest, impg3[:, :, 0:14], AX, ALU.min))
            for g in range(G):
                last = V.scalar_tensor_tensor(cand3[:, g, 0:14], impg3[:, g, 0:14], lowest[:, g:g + 1], C("jp1")[:, 1:15],
                                              ALU.is_equal, ALU.mult)
            link(dve, "dve", last)
            link(dve, "dve", V.tensor_reduce(dropj, cand3[:, :, 0:14], AX, ALU.max))
            for g in range(G):
                last = V.tensor_scalar(dmask[:, 16 * g:16 * g + 16], C("jp1"), dropj[:, g:g + 1], -1e30, ALU.is_equal, ALU.mult)
            link(dve, "dve", last)
            dve.wait_ge(S("pv_ps"), 1)
            V.tensor_copy(oS, banks[0][:, 0:256]).then_inc(S("oS"), 1)
            keys_out_v(1, 4)
            dve.wait_ge(S("score_ps"), 2)
            for g in range(G):
                biased(g, 0, WIN, banks[1 + 2 * g], C("ndwin")[:, 0:WIN])
                last = biased(g, WIN, NS, banks[(5, 0)[g]], C("ndwin")[:, WIN:])
            last.then_inc(S("scores_in"), 2)
            dve.wait_ge(S("scores_in"), 2)
            softmax(1, WIN_W)
            dve.wait_ge(S("pv_ps"), 2)
            V.tensor_tensor(oS, oS, banks[0][:, 0:256], ALU.add).then_inc(S("oS"), 1)
            keys_out_v(2, 8)
            dve.wait_ge(S("score_ps"), 3)
            for g in range(G):
                for c in range(2):
                    biased(g, 512 * c, 512, banks[1 + 2 * g + c], C("ndsel")[:, 512 * c:512 * c + 512])
                last = biased(g, PAST, NS, banks[(5, 0)[g]], C("ndsel")[:, PAST:])
            last.then_inc(S("scores_in"), 1)
            dve.wait_ge(S("scores_in"), 3)
            for g in range(G):
                blocks = sS[:, g, 0:PAST].rearrange("p (j s) -> p j s", s=64)
                last = V.tensor_tensor(blocks, blocks, dmask[:, 16 * g:16 * g + 16].unsqueeze(2).broadcast_to([P, 16, 64]), ALU.add)
            link(dve, "dve", last)
            softmax(2, SEL_W)
            dve.wait_ge(S("pv_ps"), 3)
            dve.wait_ge(S("oS"), 2)
            V.tensor_tensor(oS, oS, banks[0][:, 0:256], ALU.add).then_inc(S("oS"), 1)
            dve.wait_ge(S("oS"), 3)
            for g in range(G):
                V.tensor_copy(onT[DH * g:DH * g + DH, :, 256:288].rearrange("p r (b t) -> p r b t", t=TS),
                              oS[DH * g:DH * g + DH].rearrange("p (b g r t) -> p g r b t", b=NB, g=G, r=R)[:, g])

            u, s = 0, 0
            after(dve, "sg_gate")
            for i in range(2):
                for branch in range(3):
                    width = P * (i + 1) if branch else NCMP_P
                    nd = C(f"ndc{i}")[:, 0:NCMP_P] if branch == 0 else C("nd")[:, P:] if i == 0 else C("nd")
                    dve.wait_ge(S("p_score"), u + 1)
                    if u:
                        dve.wait_ge(S("ppT_ps"), s)
                    for h in range(H):
                        last = V.scalar_tensor_tensor(sP[:, h, 0:width], nd, 2.0 ** -(h + 1),
                                                      banks[h // 2][:, 256 * (h % 2):256 * (h % 2) + width], ALU.mult, ALU.add)
                    last.then_inc(S("p_in"), 1)
                    dve.wait_ge(S("p_in"), u + 1)
                    link(dve, "dve", V.tensor_reduce(pr_coef, sP[:, :, 0:width], AX, ALU.max))
                    V.tensor_scalar(pr_max, pr_coef, -1.0, None, ALU.mult).then_inc(S("p_max"), 1)
                    dve.wait_ge(S("p_exp"), u + 1)
                    link(dve, "dve", V.reciprocal(pr_coef, pr_sum))
                    link(dve, "dve", V.tensor_tensor(pr_coef, pr_coef, sg_gate[:, i, 8 * branch:8 * branch + 8], ALU.mult))
                    if branch == 0:
                        link(dve, "dve", V.tensor_scalar(pr_coef, pr_coef, C("rowv")[:, i:i + 1], None, ALU.mult))
                    V.tensor_tensor(sP[:, :, 0:width], sP[:, :, 0:width], pr_coef.unsqueeze(2).broadcast_to([P, H, width]),
                                    ALU.mult).then_inc(S("p_probs"), 1)
                    tiles, n = (i + 1, P) if branch else (1, NCMP_P)
                    for t in range(tiles):
                        dve.wait_ge(S("ppT_ps"), s + 1)
                        if u:
                            dve.wait_ge(S("p_pv"), u)
                        V.tensor_copy(pTp[0:n, t, 4:8], banks[5][0:n, :].rearrange("p (h t) -> p h t", h=4)
                                      ).then_inc(S("ppT_v"), 1)
                        s += 1
                    dve.wait_ge(S("p_pv"), u + 1)
                    if branch == 0:
                        V.tensor_copy(on[:, i], banks[6][:]).then_inc(S("on"), 1)
                    else:
                        dve.wait_ge(S("on"), u)
                        V.tensor_tensor(on[:, i], on[:, i], banks[6][:], ALU.add).then_inc(S("on"), 1)
                    u += 1
            dve.wait_ge(S("ld_hg"), 48)
            V.tensor_tensor(lb, lb, oml, ALU.subtract).then_inc(S("lb_d"), 1)
            after(dve, "lb")
            link(dve, "dve", V.tensor_scalar(oml, lb, -1.0, 1.0, ALU.mult, ALU.add))
            after(dve, "hf_sig")
            hf01, hf2 = z[:, 0:2, OFF["hf"]:OFF["hf"] + 512], zc(2, "hf", 512)
            V.tensor_tensor(hf01, hf01, oml.unsqueeze(1).broadcast_to([P, 2, 512]), ALU.mult)
            link(dve, "dve", V.tensor_tensor(hf2, hf2, oml[0:NS], ALU.mult))
            V.tensor_tensor(hf01, hf01, lb.unsqueeze(1).broadcast_to([P, 2, 512]), ALU.add)
            V.tensor_tensor(hf2, hf2, lb[0:NS], ALU.add).then_inc(S("f"), 1)
            after(dve, "gl")
            V.tensor_scalar(hf01, hf01, -1.0, 1.0, ALU.mult, ALU.add)
            V.tensor_scalar(hf2, hf2, -1.0, 1.0, ALU.mult, ALU.add).then_inc(S("hk"), 1)

            def hgrn_norm(i, src, sq):
                r = ROWS[i]
                dve.wait_ge(S("oh_cp"), i + 1)
                link(dve, "dve", V.tensor_tensor(sq[0:r], src[0:r], src[0:r], ALU.mult))
                V.tensor_reduce(hss[0:r, 4 * i:4 * i + 4], sq[0:r], AX, ALU.add).then_inc(S("hss"), 1)
                dve.wait_ge(S("hrt"), i + 1)
                link(dve, "dve", V.reciprocal(hrs[0:r, 4 * i:4 * i + 4], hrt[0:r, 4 * i:4 * i + 4]))
                link(dve, "dve", V.tensor_tensor(src[0:r], src[0:r], hrs[0:r, 4 * i:4 * i + 4].unsqueeze(2).broadcast_to([r, HH, DK]),
                                                 ALU.mult))
                link(dve, "dve", V.tensor_tensor(src[0:r], src[0:r], hgn[0:r].unsqueeze(1).broadcast_to([r, HH, DK]), ALU.mult))
                V.tensor_tensor(src[0:r], src[0:r], zc(i, "hg", 512).rearrange("p (h v) -> p h v", h=HH), ALU.mult
                                ).then_inc(S("oh"), 1)

            for i in range(2):
                dve.wait_ge(S("ebT"), i + 1)
                V.tensor_tensor(qe, hqT, ebT, ALU.mult)
                for h in range(HH):
                    sub = bT[:, h].rearrange("p (s t) -> p s t", t=16)
                    if h or i:
                        dve.wait_ge(S("att_ps"), HH * i + h)
                    if h == 0 and i:
                        dve.wait_ge(S("kh_ps"), i)
                    V.tensor_tensor(dk, sub[:, :, 7:8].broadcast_to([P, 8, P]), bT[:, h].unsqueeze(1).broadcast_to([P, 8, P]),
                                    ALU.subtract)
                    link(dve, "dve", V.tensor_tensor(dq, sub, sub[:, :, 7:8].broadcast_to([P, 8, 16]), ALU.subtract))
                    V.tensor_scalar(dk, dk, TOP, None, ALU.min)
                    V.tensor_scalar(dq, dq, TOP, None, ALU.min).then_inc(S("hd"), 1)
                    dve.wait_ge(S("he"), HH * i + h + 1)
                    V.tensor_tensor(dk, dk, hkT[:, h].unsqueeze(1).broadcast_to([P, 8, P]), ALU.mult)
                    V.tensor_tensor(dq, dq, hqT[:, h].rearrange("p (s t) -> p s t", t=16), ALU.mult).then_inc(S("hk_d"), 1)
                    dve.wait_ge(S("att_ps"), HH * i + h + 1)
                    if h or i:
                        dve.wait_ge(S("o_ps"), HH * i + h)
                    V.tensor_tensor(att, banks[4][:, 0:P], C("tri"), ALU.mult).then_inc(S("att"), 1)
                V.tensor_tensor(dk[:, 0:4], bT[:, :, P - 1:P].broadcast_to([P, HH, P]), bT, ALU.subtract).then_inc(S("kd_d"), 1)
                dve.wait_ge(S("kd_e"), i + 1)
                V.tensor_tensor(dk[:, 0:4], dk[:, 0:4], hkT, ALU.mult).then_inc(S("kd"), 1)
                dve.wait_ge(S("st_ps"), i + 1)
                new = banks[6][:].rearrange("p (h v) -> p h v", h=HH)
                if i == 0:
                    V.tensor_copy(state, new).then_inc(S("state"), 1)
                else:
                    dve.wait_ge(S("o_ps"), HH * (i + 1))
                    link(dve, "dve", V.tensor_tensor(state, state, ebT[:, :, P - 1:P].broadcast_to([P, HH, DK]), ALU.mult))
                    V.tensor_tensor(state, state, new, ALU.add).then_inc(S("state"), 1)
                hgrn_norm(i, oh, osq)
            dve.wait_ge(S("ohT_ps"), 2)
            dve.wait_ge(S("st_state"), 16)
            V.tensor_tensor(vm[0:NS], zc(2, "hi", 512).unsqueeze(1).broadcast_to([NS, NB, 512]),
                            C("bmask", NS).unsqueeze(2).broadcast_to([NS, NB, 512]), ALU.mult).then_inc(S("vm"), 1)
            link(dve, "dve", V.memset(qep, 0.0))
            V.tensor_copy(ss[:, 3:4], eps_t).then_inc(S("s_free"), 1)
            dve.wait_ge(S("ebT"), 3)
            ends = sb_[:, 0].rearrange("p h (b t) -> p (h b) t", t=TS)
            V.tensor_tensor(sb_[:, 6].rearrange("p h (b t) -> p (h b) t", t=TS), ends[:, :, TS - 1:TS].broadcast_to([P, HH * NB, TS]),
                            ends, ALU.subtract).then_inc(S("kd_d"), 1)
            link(dve, "dve", V.tensor_tensor(sb_[:, 4], sb_[:, 1], sb_[:, 3], ALU.mult))
            V.tensor_copy(qep.rearrange("p h (b c) -> p h b c", c=36)[:, :, :, 0:TS], sb_[:, 4].rearrange("p h (b t) -> p h b t", t=TS))
            V.scalar_tensor_tensor(sb_[:, 5], sb_[:, 5], CLIP, sb_[:, 2], ALU.min, ALU.mult)
            dve.wait_ge(S("kd_e"), 3)
            V.tensor_tensor(sb_[:, 6], sb_[:, 6], sb_[:, 2], ALU.mult).then_inc(S("s_kq"), 1)
            dve.wait_ge(S("att_ps"), 2 * HH + 1)
            V.tensor_tensor(att_s[0:NS], banks[4][0:NS, 0:P].rearrange("p (h t) -> p h t", h=HH),
                            C("bt32", NS).unsqueeze(1).broadcast_to([NS, HH, NS]), ALU.mult).then_inc(S("att"), 1)
            dve.wait_ge(S("o_ps"), 2 * HH + 1)
            eb_end = sb_[:, 3].rearrange("p h (b t) -> p b h t", t=TS)[:, :, :, TS - 1]
            s0v = s0.rearrange("p (b h) v -> p b h v", h=HH)
            for b in range(NB):
                last = V.tensor_tensor(s0v[:, b], s0v[:, b], eb_end[:, b].unsqueeze(2).broadcast_to([P, HH, DK]), ALU.mult)
            link(dve, "dve", last)
            for n in range(8):
                h, half = n // 2, n % 2
                dve.wait_ge(S("sst_ps"), n + 1)
                V.tensor_tensor(s0v[:, 4 * half:4 * half + 4, h], s0v[:, 4 * half:4 * half + 4, h],
                                banks[n % 2][:].rearrange("p (b v) -> p b v", b=4), ALU.add).then_inc(S("s_state"), 1)
            hgrn_norm(2, oh_s, osq_s)

            V.tensor_copy(ss[:, 3:4], eps_t).then_inc(S("onS"), 1)
            for i in range(3):
                r = ROWS[i]
                dve.wait_ge(S("mrg_ps"), i + 1)
                for n in range(2):
                    for name, bank in (("ga", banks[n]), ("gb", banks[2 + n])):
                        v = zc(i, name, D)[:, 512 * n:512 * n + 512]
                        last = V.tensor_tensor(v, v, bank[0:r, :], ALU.mult)
                link(dve, "dve", last)
                if i:
                    dve.wait_ge(S("mT_ps"), i)
                V.tensor_tensor(mrow[0:r], zc(i, "ga", D), zc(i, "gb", D), ALU.add).then_inc(S("m_rows"), 1)

            def residual(i, src, seq, name):
                r, ps = ROWS[i], i // 2
                link(dve, "dve", V.tensor_tensor_reduce(scr[0:r], src[0:r], src[0:r], 1.0, 0.0, ALU.mult, ALU.add, ss[0:r, i:i + 1]))
                V.tensor_copy(ss[0:r, 3:4], ss[0:r, i:i + 1]).then_inc(S("ss"), 1)
                dve.wait_ge(S("rms"), seq + 1)
                link(dve, "dve", V.reciprocal(rstd[0:r, i:i + 1], rt_[0:r, i:i + 1]))
                link(dve, "dve", V.scalar_tensor_tensor(src[0:r], src[0:r], rstd[0:r, i:i + 1], gate_rows[0:r, ps], ALU.mult, ALU.mult))
                V.tensor_tensor(x[0:r, i], x[0:r, i], src[0:r], ALU.add).then_inc(S(name), 1)

            for i in range(3):
                dve.wait_ge(S("out_cp"), i + 1)
                residual(i, orow, 3 + i, "y1")

            dve.wait_ge(S("bc"), 6)
            for i in range(3):
                r, ps = ROWS[i], i // 2
                link(dve, "dve", V.tensor_tensor_reduce(scr[0:r], x[0:r, i], x[0:r, i], 1.0, 0.0, ALU.mult, ALU.add, ss[0:r, i:i + 1]))
                V.tensor_copy(ss[0:r, 3:4], ss[0:r, i:i + 1]).then_inc(S("ss"), 1)
                dve.wait_ge(S("rms"), 7 + i)
                link(dve, "dve", V.reciprocal(rstd[0:r, i:i + 1], rt_[0:r, i:i + 1]))
                link(dve, "dve", V.scalar_tensor_tensor(h2r[0:r, i], x[0:r, i], rstd[0:r, i:i + 1], mod_rows[0:r, 0, ps],
                                                        ALU.mult, ALU.mult))
                V.tensor_tensor(h2r[0:r, i], h2r[0:r, i], mod_rows[0:r, 1, ps], ALU.add).then_inc(S("h2"), 1)
            after(dve, "lg_ps")
            for i in range(3):
                r = ROWS[i]
                link(dve, "dve", V.tensor_tensor(lg[0:r, i], banks[1][0:r, E * i:E * i + E], br[0:r], ALU.add))
                link(dve, "dve", V.max(top8[0:r], lg[0:r, i]))
                link(dve, "dve", V.max_index(top8i[0:r].bitcast(U32), top8[0:r], lg[0:r, i]))
                V.tensor_copy(idxf[0:r], top8i[0:r, 0:4].bitcast(U32))
                V.tensor_scalar(negtop[0:r], top8[0:r, 0:1], -1.0, None, ALU.mult).then_inc(S("top"), 1)
                dve.wait_ge(S("top"), i + 1)
                for k in range(4):
                    last = V.tensor_scalar(oneh[0:r, i, k], C("iota")[0:r], idxf[0:r, k:k + 1], None, ALU.is_equal)
                link(dve, "dve", last)
                V.tensor_reduce(mk[0:r, i], oneh[0:r, i].rearrange("p k e -> p e k"), AX, ALU.add).then_inc(S("mk"), 1)
                dve.wait_ge(S("wexp"), i + 1)
                link(dve, "dve", V.reciprocal(wrec[0:r], wsum[0:r]))
                link(dve, "dve", V.tensor_scalar(wts[0:r, i], wts[0:r, i], wrec[0:r], None, ALU.mult))
            after(dve, "cnt_ps")
            link(dve, "dve", V.tensor_scalar(nchT[0:E], banks[3][0:E, 0:P], float(SLOT), 1.0, ALU.is_gt, ALU.add))
            for v in range(2, JMAX):
                ins = V.scalar_tensor_tensor(nchT[0:E], banks[3][0:E, 0:P], float(SLOT * v), nchT[0:E], ALU.is_gt, ALU.add)
                if v < JMAX - 1:
                    link(dve, "dve", ins)
            ins.then_inc(S("nch"), 1)
            after(dve, "base_ps")
            V.tensor_copy(tab[0:1, 0:E], banks[4][0:1, E:2 * E])
            V.tensor_scalar(tab[0:1, 2 * E:3 * E], banks[4][0:1, E:2 * E], -1.0, None, ALU.add)
            V.tensor_copy(tab[0:1, E:2 * E], banks[4][0:1, 0:E]).then_inc(S("tab"), 1)
            link(dve, "dve", V.tensor_scalar(slotb, banks[4][:, 0:E], float(SLOT), None, ALU.mult))
            for i in range(3):
                r = ROWS[i]
                link(dve, "dve", V.tensor_tensor(roww[0:r], banks[2][0:r, E * i:E * i + E], slotb[0:r], ALU.add))
                for k in range(4):
                    link(dve, "dve", V.tensor_tensor_reduce(oneh[0:r, i, k], oneh[0:r, i, k], roww[0:r], 1.0, 0.0, ALU.mult, ALU.add,
                                                            rowf[0:r, 4 * i + k:4 * i + k + 1]))
                V.tensor_copy(rowu[0:r, 4 * i:4 * i + 4], rowf[0:r, 4 * i:4 * i + 4]).then_inc(S("rows"), 1)

            dve.wait_ge(S("scattered"), 16 * 12)
            after(dve, "tab")
            n_chunks = dve.value_load(tab[0:1, E - 1:E], min_val=E, max_val=CMAX)
            with dve.Fori(0, n_chunks) as c:
                dve.wait_ge(S("piece_used"), c * 12 + 8)
                V.tensor_scalar(gt, banks[0][:], 7.0, None, ALU.min).then_inc(S("gate"), 1)
                V.tensor_scalar(up, banks[1][:], -7.0, 7.0, ALU.max, ALU.min).then_inc(S("up"), 1)
                dve.wait_ge(S("gate"), c + 1)
                dve.wait_ge(S("up"), c + 1)
                V.scalar_tensor_tensor(up, up, 1.0, gt, ALU.add, ALU.mult).then_inc(S("prod"), 1)
                dve.wait_ge(S("prod"), c + 1)
                dve.wait_ge(S("sig"), c + 1)
                V.tensor_tensor(ac, up, sg, ALU.mult).then_inc(S("act"), 1)
                dve.wait_ge(S("aT_ps"), c + 1)
                V.tensor_copy(aT, banks[3][:]).then_inc(S("aT"), 1)
            for i in range(3):
                r = ROWS[i]
                dve.wait_ge(S(f"ld_gath{i}"), 64)
                link(dve, "dve", V.tensor_scalar(accr[0:r], gath[0:r, i, 0], wts[0:r, i, 0:1], None, ALU.mult))
                for k in range(1, 4):
                    link(dve, "dve", V.scalar_tensor_tensor(accr[0:r], gath[0:r, i, k], wts[0:r, i, k:k + 1], accr[0:r],
                                                            ALU.mult, ALU.add))
                link(dve, "dve", V.tensor_tensor_reduce(sqr[0:r], accr[0:r], accr[0:r], 1.0, 0.0, ALU.mult, ALU.add, ss[0:r, i:i + 1]))
                V.tensor_copy(ss[0:r, 3:4], ss[0:r, i:i + 1]).then_inc(S("ss"), 1)
                dve.wait_ge(S("rms"), 10 + i)
                link(dve, "dve", V.reciprocal(rstd[0:r, i:i + 1], rt_[0:r, i:i + 1]))
                link(dve, "dve", V.scalar_tensor_tensor(accr[0:r], accr[0:r], rstd[0:r, i:i + 1], gate_rows[0:r, i // 2],
                                                        ALU.mult, ALU.mult))
                link(dve, "dve", V.tensor_tensor(x[0:r, i], x[0:r, i], accr[0:r], ALU.add))
                V.tensor_copy(ss[0:r, 3:4], ss[0:r, i:i + 1]).then_inc(S("y2"), 1)

        @block.gpsimd
        def _(pool):
            after(pool, "zero_t")
            rows = slots.rearrange("(p a) (b c) -> p (a b) c", p=P, c=P)
            half = rows.shape[1] // 2
            for n in range(2):
                pool.wait_ge(S("zin_mm"), 3 * n + 1)
                if n:
                    pool.wait_ge(S("zero_slots"), 16)
                pool.dma_start(rows[:, half * n:half * n + half], zero_t.unsqueeze(1).broadcast_to([P, half, P])
                               ).then_inc(S("zero_slots"), 16)
            pool.wait_ge(S("zero_slots"), 32)
            load_pages(pool, (2, 3))
            pool.wait_ge(S("pre_ps"), 4)
            load_selected(pool, NPG // 2, "ld_key_p")

            for i in range(3):
                pool.wait_ge(S("rows"), i + 1)
                for k in range(4):
                    pool.indirect_dma_start(
                        out=slots, out_offset=bass.IndirectOffsetOnAxis(ap=rowu[0:ROWS[i], 4 * i + k:4 * i + k + 1], axis=0),
                        in_=h2r[0:ROWS[i], i], in_offset=None).then_inc(S("scattered"), 16)
            pool.wait_ge(S("scattered"), 16 * 12)
            after(pool, "tab")
            n_chunks = pool.value_load(tab[0:1, E - 1:E], min_val=E, max_val=CMAX)
            pool.dma_start(xrow[0:SLOT], slots[0:SLOT]).then_inc(S("ld_x2"), 16)
            with pool.Fori(0, n_chunks) as c:
                pool.wait_ge(S("xcT_ps"), c + 1)
                pool.dma_start(xrow[0:SLOT], slots[bass.ds(c * SLOT + SLOT, SLOT)]).then_inc(S("ld_x2"), 16)
                pool.wait_ge(S("yc"), c + 1)
                for s in range(2):
                    pool.dma_start(slots[bass.ds(c * SLOT, SLOT), 512 * s:512 * s + 512], yc[SLOT * s:SLOT * s + SLOT]
                                   ).then_inc(S("st_yc"), 16)
            after(pool, "all_out")
            for i in range(3):
                for k in range(4):
                    pool.indirect_dma_start(
                        out=gath[0:ROWS[i], i, k], out_offset=None, in_=slots,
                        in_offset=bass.IndirectOffsetOnAxis(ap=rowu[0:ROWS[i], 4 * i + k:4 * i + k + 1], axis=0)
                    ).then_inc(S(f"ld_gath{i}"), 16)


_INS = ["x_prompt", "x_sample", "c_prompt", "c_sample", "cache_cmp", "cache_sel", "state_win", "state_hgrn", "page_table",
        "w_ada", "b_ada", "norm_mix_pre", "norm_mix_post", "norm_ffn_pre", "norm_ffn_post", "w_in", "cmp_pe", "cmp_w1",
        "cmp_w2", "hg_lb_logits", "hg_norm", "w_branch_a", "w_branch_b", "w_out", "w_router", "b_router", "w_up", "b_up",
        "w_down", "b_down"]
_OUTS = [(1, TP, D), (NB, TS, D), (1, 1, TP, 2, G, DH), (1, NB, TS, 2, G, DH), (1, 1, TP, 2, G, DH), (1, NB, TS, 2, G, DH),
         (1, 1, TP, 2, G, DH), (1, NB, WIN, 2, G, DH), (1, 1, HH, DK, DK), (1, NB, HH, DK, DK)]


def kernel(**inputs):
    import numpy as _np
    import concourse.bacc as _bacc
    from concourse.bass_utils import run_bass_kernel_spmd as _run

    nc = _bacc.Bacc("TRN2", target_bir_lowering=False, num_devices=1)
    arrays, args = {}, {}
    for name in _INS:
        a = _np.ascontiguousarray(inputs[name])
        arrays[f"in_{name}"] = a
        args[name] = nc.dram_tensor(f"in_{name}", a.shape, mybir.dt.from_np(a.dtype), kind="ExternalInput").ap()
    arrays["in_const"] = CONST
    args["const"] = nc.dram_tensor("in_const", CONST.shape, F32, kind="ExternalInput").ap()
    outs = [nc.dram_tensor(f"out_{i}", s, F32, kind="ExternalOutput").ap() for i, s in enumerate(_OUTS)]
    build(nc, args, outs)
    r = _run(nc, [arrays], core_ids=[0])
    return tuple(r.results[0][f"out_{i}"] for i in range(len(_OUTS)))
```

```python
from contextlib import ExitStack

import numpy as np

import concourse.bass as bass
from concourse import mybir

F32 = mybir.dt.float32
I32 = mybir.dt.int32
U32 = mybir.dt.uint32
ALU = mybir.AluOpType
ACT = mybir.ActivationFunctionType
AX = mybir.AxisListType.X

P = 128
D = 1024
KD = D // P
TP, NB, TS = 256, 8, 4
NS = NB * TS
PAST, PAGE = 1024, 128
NPG = PAST // PAGE
G, R, DH, H = 2, 4, 64, 8
WIN = 512
NCMP = PAST // 16 - 1
NCMP_P = TP // 16 - 1
HH, DK = 4, 128
E, TOPK = 32, 4
EPS = 1e-6
OFF = {}
IN_W = 0
for _n, _w in (("q", 512), ("kc", 128), ("vc", 128), ("ks", 128), ("vs", 128), ("kw", 128), ("vw", 128), ("gn", 24),
               ("hq", 512), ("hf", 512), ("hi", 512), ("hg", 512), ("ga", 1024), ("gb", 1024)):
    OFF[_n] = IN_W
    IN_W += _w
ROWS = (P, P, NS)
SLOT = 64
CMAX = E + (TOPK * (TP + NS) - E) // SLOT
NCHUNK = CMAX + 1
JMAX = -(-(TP + NS) // SLOT)
SEL_W = PAST + NS
WIN_W = WIN + NS
FAR = -1e33
CLIP = 1e18
TOP = 41.0

CONSTS = {}
_cat = []


def _put(name, a):
    t = np.zeros((P, a.shape[1]), np.float32)
    t[:a.shape[0]] = a
    CONSTS[name] = (sum(x.shape[1] for x in _cat), a.shape[1])
    _cat.append(t)


def const_table():
    _cat.clear()
    p = np.arange(P)
    _put("ident", np.eye(P))
    _put("tri", (p[:, None] <= p[None, :]) * 1.0)
    _put("stri", (p[:, None] < p[None, :]) * 1.0)
    dist = P + p[:, None] - np.arange(2 * P)[None, :]
    _put("nd", np.where(dist >= 0, -dist, FAR))
    for i in range(2):
        dist = i * P + p[:, None] - (16 * np.arange(16)[None, :] + 31)
        _put(f"ndc{i}", np.where(dist >= 0, -dist, FAR))
    _put("rowv", np.stack([(p >= 31) * 1.0, np.ones(P)], 1))
    b32 = np.arange(NS) // TS
    same = b32[:, None] == b32[None, :]
    _put("bt32", (same & (np.arange(NS)[:, None] <= np.arange(NS)[None, :])) * 1.0)
    _put("bmask", (b32[:, None] == np.arange(NB)[None, :]) * 1.0)
    _put("jp1", np.broadcast_to(np.arange(1, 17), (P, 16)))
    _put("iota", np.broadcast_to(np.arange(E), (P, E)))
    _put("selp", np.repeat(p[:, None] == 32 * np.arange(4)[None, :], P, 1) * 1.0)
    _put("sels", np.concatenate([p[:, None] == 32 * j + 1 + b32[None, :] for j in range(4)], 1) * 1.0)
    rb, rr, rt = p // 16, (p // 4) % 4, p % 4
    _put("rdiag", (rr[:, None] == np.arange(4)[None, :]) * 1.0)
    _put("expand", (np.arange(NS)[:, None] == (rb * TS + rt)[None, :]) * 1.0)
    _put("gsum", ((rb[:, None] == rb[None, :]) & (rt[:, None] == rt[None, :])) * 1.0)
    _put("slope", np.stack([2.0 ** -(g * R + rr + 1.0) for g in range(G)], 1))
    qpos = PAST + rt
    nb, nt = np.arange(NS) // TS, np.arange(NS) % TS
    new = np.where((nb[None, :] == rb[:, None]) & (nt[None, :] <= rt[:, None]),
                   -(rt[:, None] - nt[None, :]).astype(np.float64), FAR)
    _put("ndsel", np.concatenate([-(qpos[:, None] - np.arange(PAST)[None, :]), new], 1))
    d = qpos[:, None] - (PAST - WIN + np.arange(WIN)[None, :])
    _put("ndwin", np.concatenate([np.where(d < WIN, -d, FAR), new], 1))
    _put("ndcs", -(qpos[:, None] - (16 * np.arange(64)[None, :] + 31)))
    return np.concatenate(_cat, 1).astype(np.float32)


CONST = const_table()


STEPS = {
    "pe_step": ('sct_ps', 'peT_ps', 'pconst_ps', 'comp_ps', 'sq_ps', 'sgate_ps', 'imp_ps', 'lg_ps', 'cnt_ps', 'base_ps'),
    "act_step": ('silu_c', 'sg_gate', 'hf_sig', 'comp_a', 'lb', 'gl', 'all_out'),
    "dve_step": ('zeroed', 'zero_t', 'sct', 'mod_w', 'peT', 'pconst', 'comp_v', 'sq', 'imp', 'lb_d', 'f', 'hk', 'vm', 's_free', 's_kq', 'onS', 'nch', 'tab'),
}
STEP_OF = {name: (sem, n + 1) for sem, names in STEPS.items() for n, name in enumerate(names)}


UNITS = [(i, branch, g) for i in range(2) for branch in range(3) for g in range(G)]


def _tiles_before(u):
    return sum((i + 1 if branch else 1) for i, branch, _ in UNITS[:u])


def prompt_steps():
    todo = {}

    def step(engine, us, name, args, *after_):
        before = [s for s in after_ if s in todo]
        same = [s for s in todo if s[0] == name]
        todo[(name, args)] = (engine, us, before + same[-1:])

    for u, (i, branch, g) in enumerate(UNITS):
        wide = i + 1 if branch else 0.3
        tiles = max(1, int(wide))
        step("pe", 1.0 + 0.5 * wide, "scores", (u,), ("biased", (u - 1,)))
        step("dve", 1.0 + 0.9 * wide, "biased", (u,), ("scores", (u,)), ("probs_T", (u - 2, UNITS[u - 2][0] if UNITS[u - 2][1] else 0)))
        step("act", 0.8 + 0.5 * wide, "exps", (u,), ("biased", (u,)))
        step("dve", 0.6 + 0.6 * wide, "probs", (u,), ("exps", (u,)))
        for t in range(tiles):
            step("pe", 1.0, "probs_T", (u, t), ("probs", (u,)), ("probs_out", (u, t - 1)),
                 ("probs_out", (u - 1, UNITS[u - 1][0] if UNITS[u - 1][1] else 0)))
            step("act", 0.6, "probs_out", (u, t), ("probs_T", (u, t)), ("values", (u - 2,)))
        step("pe", 0.5 * 4 * tiles, "values", (u,), ("probs_out", (u, tiles - 1)), ("add", (u - 1,)))
        step("dve", 0.4, "add", (u,), ("values", (u,)), ("add", (u - 2,)))
    for i in range(2):
        step("pe", 3.2, "inputs", (i,), ("result", (i - 1,)), ("head_masked", (i - 1, HH - 1)), ("new_state", (i - 1,)))
        step("act", 2.4, "inputs_out", (i,), ("inputs", (i,)), ("end_keys", (i - 1,)), ("head", (i - 1, HH - 1)), ("new_state", (i - 1,)))
        for h in range(HH):
            last = ("attention", (i, h - 2)) if h > 1 else ("keys_back", (i - 1,))
            step("dve", 2.6, "distances", (i, h), ("inputs_out", (i,)), last, ("head", (i - 1, HH - 1)))
            step("act", 1.2, "decays", (i, h), ("distances", (i, h)))
            step("dve", 1.3, "factors", (i, h), ("decays", (i, h)))
            step("pe", 0.6, "attention", (i, h), ("factors", (i, h)), ("head_masked", (i, h - 1)), ("inputs_out", (i,)))
            step("dve", 0.3, "head_masked", (i, h), ("attention", (i, h)), ("head", (i, h - 1)))
            step("pe", 0.5, "head", (i, h), ("head_masked", (i, h)), ("result", (i - 1,)), ("new_state", (i - 1,)))
        step("dve", 0.6, "to_end", (i,), ("attention", (i, HH - 1)))
        step("act", 0.6, "end_decays", (i,), ("to_end", (i,)))
        step("dve", 0.6, "end_keys", (i,), ("end_decays", (i,)))
        step("pe", 1.0, "keys_back", (i,), ("end_keys", (i,)), ("inputs_out", (i,)))
        step("act", 0.5, "keys_out", (i,), ("keys_back", (i,)))
        step("pe", 1.0, "state", (i,), ("keys_out", (i,)))
        step("dve", 1.0, "new_state", (i,), ("state", (i,)), ("head", (i, HH - 1)))
        step("act", 0.5, "result", (i,), ("head", (i, HH - 1)), ("out", (i - 1,)))
        step("dve", 1.2, "squares", (i,), ("result", (i,)))
        step("act", 0.3, "rms", (i,), ("squares", (i,)))
        step("dve", 2.0, "gated", (i,), ("rms", (i,)))
        step("pe", 1.0, "out", (i,), ("gated", (i,)), ("out_T", (i - 1,)))
        step("act", 0.5, "out_T", (i,), ("out", (i,)))
    free, done, order = {"pe": 0.0, "act": 0.0, "dve": 0.0}, {}, []
    while todo:
        ready = []
        for n, (s, (engine, us, before)) in enumerate(todo.items()):
            if all(b in done for b in before):
                ready.append((max([free[engine]] + [done[b] + 0.25 for b in before]), n, s))
        begin, _, s = min(ready)
        engine, us, _ = todo.pop(s)
        done[s] = free[engine] = begin + us
        order.append(s)
    return order


PROMPT_STEPS = prompt_steps()


def build(nc, A, O):
    with ExitStack() as ctx:
        arena_w = 53200
        arena = ctx.enter_context(nc.sbuf_tensor("arena", [P, arena_w], F32))
        banks = [ctx.enter_context(nc.psum_tensor(f"bank{i}", [P, 512], F32)) for i in range(8)]
        sems = {}

        def S(name):
            name = STEP_OF[name][0] if name in STEP_OF else name
            if name not in sems:
                sems[name] = ctx.enter_context(nc.semaphore(name))
            return sems[name]

        def after(eng, name):
            eng.wait_ge(S(name), STEP_OF[name][1])

        place = {"at": 0}

        def take(n, *shape):
            a = place["at"]
            place["at"] = a + n
            assert place["at"] <= arena_w, place["at"]
            return view(a, n, *shape)

        def view(a, n, *shape):
            v = arena[:, a:a + n]
            if len(shape) == 2:
                v = v.rearrange("p (a b) -> p a b", b=shape[1])
            elif len(shape) == 3:
                v = v.rearrange("p (a b c) -> p a b c", b=shape[1], c=shape[2])
            elif len(shape) == 4:
                v = v.rearrange("p (a b c d) -> p a b c d", b=shape[1], c=shape[2], d=shape[3])
            return v

        ctab = take(CONST.shape[1])

        def C(name, rows=P, r0=0):
            o, w = CONSTS[name]
            return ctab[r0:r0 + rows, o:o + w]

        ident = C("ident")
        x = take(3 * D, 3, D)
        mod = take(12 * P, 12, P)
        gate_rows = take(2 * D, 2, D)
        mod_rows_at = place["at"]
        mod_rows = take(4 * D, 2, 2, D)
        ones = take(P)
        wr = take(KD * E, KD, E)
        br = take(E)
        tab = take(3 * E).bitcast(I32)
        rowu = take(12).bitcast(U32)
        zero_t = take(P)
        ptab = take(NB * NPG).bitcast(I32)
        small = take(768)
        sm = {"at": 0}

        def tiny(n):
            a = sm["at"]
            sm["at"] = a + n
            assert sm["at"] <= 768
            return small[:, a:a + n]

        eps_t = tiny(1)
        ss = tiny(4)
        rt_ = tiny(4)
        rstd = tiny(4)
        pr_max, pr_sum, pr_coef = tiny(8), tiny(8), tiny(8)
        sg_gate = tiny(3 * 24).rearrange("p (a b) -> p a b", b=24)
        sa_gate3 = tiny(24)
        sa_gate = tiny(6)
        sa_max, sa_sum, sa_coef = tiny(2), tiny(2), tiny(2)
        imp, impg, cand = tiny(32), tiny(32), tiny(32)
        lowest, dropj = tiny(2), tiny(2)
        dmask = tiny(32)
        pconst = tiny(2)
        hss, hrt, hrs = tiny(12), tiny(12), tiny(12)
        top8 = tiny(8)
        top8i = tiny(8)
        idxf = tiny(4)
        wts = tiny(12).rearrange("p (a b) -> p a b", b=4)
        wsum, wrec, negtop = tiny(1), tiny(1), tiny(1)
        rowf = tiny(12)
        gathered = tiny(1)
        n_t = place["at"]

        z = take(3 * IN_W, 3, IN_W)
        free0 = place["at"]
        h_rows = view(free0 + 3 * 4096 + 2304, D)
        hT = view(free0 + 3 * 4096, KD * (TP + NS), KD, TP + NS)
        slabs = [view(free0 + 4096 * i, 4096, KD, 512) for i in range(3)]
        bada = view(n_t, 12 * P, 12, P)
        wn = view(n_t + 12 * P, 8 * P, 8, P)
        c9 = view(n_t + 20 * P, D)
        sc32 = view(n_t + 20 * P + D, D)
        scT = view(n_t + 20 * P + 2 * D, KD * 32, KD, 32)

        dram = {}

        def internal(name, shape):
            dram[name] = nc.dram_tensor(name, shape, F32, kind="Internal").ap()
            return dram[name]

        slots = internal("slots", (NCHUNK * SLOT, D))

        w_in = A["w_in"][0]
        w_ada = A["w_ada"][0]
        zc = lambda i, name, w, r=None: z[0:ROWS[i], i, OFF[name]:OFF[name] + w]

        order = {"act": 0, "dve": 0, "pool": 0}

        def link(eng, key, ins):
            order[key] += 1
            ins.then_inc(S(f"own_{key}"), 1)
            eng.wait_ge(S(f"own_{key}"), order[key])


        fr = {"at": free0}

        def ftake(n, *shape):
            a = fr["at"]
            fr["at"] = a + n
            assert fr["at"] <= arena_w, fr["at"] - arena_w
            return view(a, n, *shape)

        NC_ALL = NB * NCMP + NCMP_P
        kcT = ftake(520)
        vcb = ftake(9 * P, 9, P)
        w2 = ftake(2 * DH, 2, DH)
        pe_rows = ftake(P)
        peT = ftake(32)
        attn0 = fr["at"]
        raw_at = arena_w - 2080
        raw = [view(raw_at + 512 * v, 512) for v in range(4)]
        geT = view(raw_at, 4 * 520, 2, 2, 520)
        UN = NB * 4 + 1
        pairT = ftake(4 * UN * P, 2, 2, UN * P)
        w1 = view(mod_rows_at, 4 * D, 2, 16, P)

        fr["at"] = attn0
        qT = view(mod_rows_at, 4 * TP, 4, TP)
        kT = ftake(2 * TP, 2, TP)
        qf = ftake(P, NB, R, TS)
        qz_at = fr["at"]
        qz = ftake(NB * 144)
        knT = ftake(2 * NS, 2, NS)
        onT = ftake(4 * 288, 4, 288)
        ohT = ftake(4 * 288, 4, 288)
        on = view(mod_rows_at + D, 2 * 512, 2, 512)
        oS = ftake(256)
        work0 = fr["at"]
        kst_at = fr["at"]
        kst = [ftake(D, 8, P) for _ in range(2)]
        vpages_at = fr["at"]
        vpages = ftake(NB * NPG * P, NB * NPG, P)
        sS = ftake(2 * SEL_W, 2, SEL_W)
        pTs = ftake(9 * 256, 9, 2, P)
        kTb = [view(mod_rows_at + D * (2 + i), D) for i in range(2)]
        fr["at"] = work0
        gl = ftake(3 * 512, 3, 512)
        lb = ftake(512)
        oml = ftake(512)
        hgn = ftake(P)
        state = ftake(512, HH, DK)
        bT = ftake(512, HH, P)
        hqT = ftake(512, HH, P)
        hkT = ftake(512, HH, P)
        ebT = ftake(512, HH, P)
        qe = ftake(512, HH, P)
        dks = [ftake(D, 8, P) for _ in range(2)]
        dqs = [ftake(P, 8, 16) for _ in range(2)]
        att = ftake(P)
        kh = ftake(512)
        oh = ftake(512, HH, DK)
        osq = ftake(512, HH, DK)
        sP = [ftake(4 * 256, 4, 256) for _ in range(2)]
        pTp = [ftake(2 * 4 * P, 2, 4, P) for _ in range(2)]
        fr["at"] = work0 + 1536 + 512 * 2 + P
        s0 = ftake(NB * HH * DK, NB * HH, DK)
        vm = ftake(NB * 512, NB, 512)
        qep = view(mod_rows_at, 4 * NB * 36, 4, NB * 36)
        sb_ = ftake(7 * P, 7, HH, NS)
        kh_s = ftake(512)
        oh_s = view(mod_rows_at + 1280, 512, HH, DK)
        osq_s = view(mod_rows_at + 1792, 512, HH, DK)
        att_s = ftake(P, HH, NS)
        fr["at"] = work0
        wo_at = fr["at"]
        ftake(8 * D)
        wo = [view(wo_at + D * k, D) for k in range(KD)]
        wbr = [view(n_t + IN_W * (k // 3) + D * (k % 3), D) for k in range(6)] + [view(arena_w - D * (2 - k), D) for k in range(2)]
        mT = ftake(KD * 288, KD, 288)
        mrow = ftake(D)
        orow = ftake(D)
        fr["at"] = n_t + 3 * D
        lg = ftake(3 * E, 3, E)
        oneh = ftake(3 * 4 * E, 3, 4, E)
        mk = ftake(3 * E, 3, E)
        nchT = ftake(P)
        slotb = ftake(E)
        roww = ftake(E)
        scr = ftake(D)
        h2r = view(n_t, 3 * D, 3, D)
        h2T = mT
        xrow = view(n_t, D)
        xcT = view(n_t + D, 512, KD, SLOT)
        gt, up, sg, ac, aT, yc = (view(n_t + D + 512 * (1 + i), 512) for i in range(6))
        bias = view(mod_rows_at, 3 * D)
        ring_at = fr["at"]
        assert ring_at + 16 * 2 * D <= arena_w
        ring = [view(ring_at + 2 * D * i, 2 * D) for i in range(16)]
        gath = view(ring_at, 12 * D, 3, 4, D)
        accr = view(n_t, D)
        sqr = view(n_t + D, D)

        def by_parity(bank):
            return bank[:].rearrange("p (s k c) -> p s k c", s=2, k=2)

        cmp_pages = A["cache_cmp"][0].rearrange("n (p s) k g d -> n p (s k g d)", s=2)
        sel_pages = A["cache_sel"][0].rearrange("n p k g d -> n p k (g d)")
        n_pool = cmp_pages.shape[0]

        def load_pages(eng, units):
            eng.wait_ge(S("ld_ptab"), 16)

            def load(b, v):
                for half in range(2):
                    page = eng.value_load(ptab[0:1, bass.ds(b * NPG + 2 * v + half, 1)], min_val=0, max_val=n_pool - 1)
                    eng.dma_start(raw[v][64 * half:64 * half + 64], cmp_pages[bass.ds(page, 1)].squeeze(0)
                                  ).then_inc(S(f"ld_raw{v}"), 16)

            for v in units:
                load(0, v)
            with eng.Fori(1, NB) as b:
                for v in units:
                    eng.wait_ge(S("pair_ps"), 4 * b + (v - 3))
                    load(b, v)

        def load_selected(eng, first, name):
            for b in range(NB):
                eng.wait_ge(S("key_ps"), NB + b - 1)
                if b == 0:
                    eng.wait_ge(S("pv_ps"), 2)
                to = kst_at + D * (b % 2)
                apart = vpages_at + D * b - to
                start = min(to, arena_w - 2 * apart)
                both = arena[:, start:start + 2 * apart].rearrange("p (k c) -> p k c", k=2)[:, :, to - start:to - start + D]
                both = both.rearrange("p k (n c) -> p n k c", n=NPG)
                with eng.Fori(first, first + NPG // 2) as n:
                    page = eng.value_load(ptab[0:1, bass.ds(n + b * NPG, 1)], min_val=0, max_val=n_pool - 1)
                    eng.dma_start(both[:, bass.ds(n, 1)].squeeze(1), sel_pages[bass.ds(page, 1)].squeeze(0)
                                  ).then_inc(S(f"{name}{b % 2}"), 16)


        block = ctx.enter_context(nc.Block())

        @block.sync
        def _(sp):
            sp.dma_start(ctab, A["const"]).then_inc(S("ld_const"), 16)
            sp.dma_start(c9[0:1], A["c_prompt"]).then_inc(S("ld_c"), 16)
            sp.dma_start(c9[1:1 + NB], A["c_sample"]).then_inc(S("ld_c"), 16)

            def load_slab(m):
                if m >= 3:
                    if m - 3 < 12:
                        sp.wait_ge(S("mod_mm"), m - 2)
                    else:
                        sp.wait_ge(S("zin_mm"), m - 14)
                c0 = (m if m < 12 else m - 12) * 512
                src = w_ada if m < 12 else w_in
                w = min(512, src.shape[1] - c0)
                if m == 12:
                    for r in range(R):
                        for g in range(G):
                            c = DH * (R * g + r)
                            sp.dma_start(slabs[0][:, :, DH * (G * r + g):DH * (G * r + g) + DH],
                                         src[:, c:c + DH].rearrange("(k p) c -> p k c", p=P)).then_inc(S("ld_slab0"), 16)
                    return
                sp.dma_start(slabs[m % 3][:, :, 0:w], src[:, c0:c0 + w].rearrange("(k p) c -> p k c", p=P)
                             ).then_inc(S(f"ld_slab{m % 3}"), 16)

            load_slab(0)
            for j in range(4):
                src = A["b_ada"][0].rearrange("(n j c) -> j n c", j=4, c=P)[j]
                sp.dma_start(bada[32 * j:32 * j + 32], src.unsqueeze(0).broadcast_to([32, 12, P])).then_inc(S("ld_bada"), 16)
            load_slab(1)
            load_slab(2)
            sp.dma_start(ptab[0:1], A["page_table"].rearrange("(o b) n -> o (b n)", o=1)).then_inc(S("ld_ptab"), 16)
            for w, name in enumerate(("norm_mix_pre", "norm_mix_post", "norm_ffn_pre", "norm_ffn_post")):
                for j in range(4):
                    src = A[name][0].rearrange("(n j c) -> j n c", j=4, c=P)[j]
                    sp.dma_start(wn[32 * j:32 * j + 32, 2 * w:2 * w + 2], src.unsqueeze(0).broadcast_to([32, 2, P])
                                 ).then_inc(S("ld_wn"), 16)
            sp.dma_start(x[:, 0:2], A["x_prompt"][0].rearrange("(i p) d -> p i d", p=P)).then_inc(S("ld_x"), 16)
            sp.dma_start(x[0:NS, 2], A["x_sample"].rearrange("b t d -> (b t) d")).then_inc(S("ld_x"), 16)
            for m in range(3, 23):
                load_slab(m)
            sp.wait_ge(S("zin_mm"), 11)
            sp.dma_start(w1, A["cmp_w1"][0].rearrange("v (q p) h -> p v q h", p=P)).then_inc(S("ld_w1"), 16)
            sp.dma_start(w2, A["cmp_w2"][0].rearrange("v h d -> h v d")).then_inc(S("ld_w1"), 16)
            sp.dma_start(pe_rows[0:32], A["cmp_pe"][0].rearrange("v (q s) d -> (v q) (s d)", s=2)).then_inc(S("ld_w1"), 16)
            sp.wait_ge(S("zin_a"), 11)
            sp.wait_ge(S("zin_v"), 11)
            for n, (o_p, o_s) in enumerate(((2, 3), (4, 5), (6, 7))):
                c0 = 512 + 256 * n
                sp.dma_start(O[o_p][0, 0].rearrange("(i p) k g d -> p i (k g d)", p=P), z[:, 0:2, c0:c0 + 256]
                             ).then_inc(S("st_kv"), 16)
                if n < 2:
                    sp.dma_start(O[o_s][0].rearrange("b t k g d -> (b t) (k g d)"), z[0:NS, 2, c0:c0 + 256]
                                 ).then_inc(S("st_kv"), 16)
            for b in range(NB):
                sp.dma_start(O[7][0, b, WIN - TS:WIN].rearrange("t k g d -> t (k g d)"),
                             z[TS * b:TS * b + TS, 2, 1024:1280]).then_inc(S("st_kv"), 16)
            sp.dma_start(O[7][0, :, 0:WIN - TS].rearrange("b t k g d -> b (t k g d)"),
                         A["state_win"][0, :, TS:WIN].rearrange("b t k g d -> b (t k g d)")).then_inc(S("st_kv"), 16)
            load_pages(sp, (0, 1))
            sp.wait_ge(S("pair_ps"), 29)
            sp.wait_ge(S("st_kv"), 16 * 14)
            sp.dma_start(raw[0], O[2][0, 0].rearrange("(p s) k g d -> p (s k g d)", s=2)).then_inc(S("ld_raw0"), 16)
            sp.wait_ge(S("pre_ps"), 4)
            for b in range(NB):
                if b >= 2:
                    sp.wait_ge(S("key_ps"), b - 1)
                src = A["state_win"][0, b].rearrange("(n p) k g d -> p k n (g d)", p=P)
                sp.dma_start(kst[b % 2][:, 0:4], src[:, 0]).then_inc(S(f"ld_key{b % 2}"), 16)
                sp.dma_start(vpages[:, 4 * b:4 * b + 4], src[:, 1]).then_inc(S(f"ld_key{b % 2}"), 16)
            load_selected(sp, 0, "ld_key")
            sp.wait_ge(S("pv_ps"), 3)
            sp.dma_start(lb, A["hg_lb_logits"][0:1].broadcast_to([P, 512])).then_inc(S("ld_hg"), 16)
            sp.dma_start(oml, A["hg_lb_logits"][1:2].broadcast_to([P, 512])).then_inc(S("ld_hg"), 16)
            sp.dma_start(hgn, A["hg_norm"][0:1].broadcast_to([P, P])).then_inc(S("ld_hg"), 16)
            sp.dma_start(wr, A["w_router"][0].rearrange("(k p) e -> p k e", p=P)).then_inc(S("ld_wr"), 16)
            sp.dma_start(br, A["b_router"][0:1].broadcast_to([P, E])).then_inc(S("ld_wr"), 16)
            sp.wait_ge(S("ohT_ps"), 2)
            sp.wait_ge(S("state"), 2)
            sp.dma_start(O[8][0, 0].rearrange("h k v -> k h v"), state).then_inc(S("st_state"), 16)
            sp.wait_ge(S("st_state"), 16)
            sp.wait_ge(S("p_pv"), len(UNITS))
            sp.dma_start(s0, A["state_hgrn"][0].rearrange("b h k v -> k (b h) v")).then_inc(S("ld_s0"), 16)
            for k in range(8):
                if k < 4:
                    for g in range(G):
                        sp.dma_start(wbr[k][DH * g:DH * g + DH], A["w_branch_a"][0, DH * (R * g + k):DH * (R * g + k) + DH]
                                     ).then_inc(S("ld_wa"), 16)
                else:
                    sp.dma_start(wbr[k], A["w_branch_b"][0, P * (k - 4):P * (k - 4) + P]).then_inc(S("ld_wa"), 16)
            sp.wait_ge(S("s_state"), 8)
            sp.dma_start(O[9][0].rearrange("b h k v -> k (b h) v"), s0).then_inc(S("st_state"), 16)
            sp.wait_ge(S("st_state"), 32)
            sp.wait_ge(S("ohT_ps"), 3)
            sp.dma_start(arena[:, wo_at:wo_at + 8 * D].rearrange("p (k n) -> p k n", n=D),
                         A["w_out"][0].rearrange("(k p) n -> p k n", p=P)).then_inc(S("ld_wo"), 16)
            w_up, w_down = A["w_up"][0], A["w_down"][0]
            last_of = lambda e: sp.value_load(tab[0:1, bass.ds(e, 1)], min_val=0, max_val=CMAX - 1)

            def load_piece(e, j, q):
                pos = (12 * j + q) % 16
                if q < 8:
                    src = w_up[bass.ds(e, 1)].squeeze(0)[P * q:P * q + P]
                    dst = ring[pos]
                else:
                    src = w_down[bass.ds(e, 1)].squeeze(0)[2 * P * (q - 8):2 * P * (q - 7)].rearrange("(k p) n -> p k n", p=P)
                    dst = ring[pos].rearrange("p (k n) -> p k n", k=2)
                sp.dma_start(dst, src).then_inc(S(f"ld_piece{pos}"), 16)

            def load_bias(e, j):
                at = 32 * (j % 2)
                sp.dma_start(bias[at:at + 1, 0:2 * D], A["b_up"][0][bass.ds(e, 1)]).then_inc(S(f"ld_bias{j % 2}"), 16)
                sp.dma_start(bias[at:at + 1, 2 * D:3 * D], A["b_down"][0][bass.ds(e, 1)]).then_inc(S(f"ld_bias{j % 2}"), 16)

            def load_expert(e, j, first):
                two_back = None if first and j < 2 else last_of(e + (2 * E - 2))
                back = last_of(e + (2 * E - 1))
                for q in range(4 if two_back is None else 0, 12):
                    before, part = (two_back, q + 8) if q < 4 else (back, q - 4)
                    sp.wait_ge(S("piece_used"), before * 12 + (part + 1))
                    load_piece(e, j, q)
                    if q == 3:
                        load_bias(e, j)

            sp.wait_ge(S("m_rows"), 3)
            for n in range(16):
                if n == 8:
                    sp.wait_ge(S("out_ps"), 3)
                if n == 12:
                    sp.wait_ge(S("y1"), 3)
                    after(sp, "lg_ps")
                load_piece(n // 12, n // 12, n % 12)
            sp.wait_ge(S("h2"), 3)
            load_bias(0, 0)
            load_bias(1, 1)
            after(sp, "tab")
            for j in range(1, 4):
                load_expert(j, j, True)
            with sp.Fori(1, E // 4) as grp:
                for j in range(4):
                    load_expert(grp * 4 + j, j, False)
            sp.wait_ge(S("y2"), 2)
            sp.dma_start(O[0][0].rearrange("(i p) d -> p i d", p=P), x[:, 0:2]).then_inc(S("st_y2"), 16)
            sp.wait_ge(S("y2"), 3)
            sp.dma_start(O[1].rearrange("b t d -> (b t) d"), x[0:NS, 2]).then_inc(S("st_y2"), 16)
            sp.wait_ge(S("st_y2"), 32)
            sp.wait_ge(S("st_kv"), 16 * 14)
            sp.wait_ge(S("st_state"), 32)

        @block.tensor
        def _(pe):
            mm = nc.tensor.matmul
            pe.wait_ge(S("ld_const"), 16)
            after(pe, "silu_c")
            for k in range(KD):
                last = nc.tensor.transpose(banks[0][:, 32 * k:32 * k + 32], sc32[0:32, P * k:P * k + P], ident[0:32, 0:32])
            last.then_inc(S("sct_ps"), 1)
            after(pe, "sct")
            for n in range(12):
                pe.wait_ge(S(f"ld_slab{n % 3}"), 16 * (n // 3 + 1))
                if n >= 2:
                    pe.wait_ge(S("mod_v"), n - 1)
                for k in range(KD):
                    for j in range(4):
                        last = mm(banks[1 + n % 2][32 * j:32 * j + 32, 0:P], scT[:, k], slabs[n % 3][:, k, P * j:P * j + P],
                                  start=k == 0, stop=k == KD - 1)
                last.then_inc(S("mod_mm"), 1)

            def spread(q, n0):
                pe.wait_ge(S("bc"), q) if q else None
                for n in range(2):
                    for j in range(4):
                        mm(banks[3 + n][:, P * j:P * j + P], C("selp")[:, P * j:P * j + P], mod[:, n0 + n],
                           start=True, stop=True)
                        last = mm(banks[5 + n][0:32, P * j:P * j + P], C("sels")[:, 32 * j:32 * j + 32], mod[:, n0 + n],
                                  start=True, stop=True)
                last.then_inc(S("bc_ps"), 1)

            after(pe, "mod_w")
            spread(0, 2)
            spread(1, 0)
            spread(2, 4)

            def rows_to_hT(i, seq):
                pe.wait_ge(S("h_rows"), seq + 1)
                for k in range(KD):
                    last = nc.tensor.transpose(banks[(0, 7)[k // 4]][:, (k % 4) * P:(k % 4) * P + ROWS[i]],
                                               h_rows[0:ROWS[i], P * k:P * k + P], ident[0:ROWS[i], 0:ROWS[i]])
                last.then_inc(S("hT_ps"), 1)

            for i in range(3):
                if i:
                    pe.wait_ge(S("hT"), i)
                rows_to_hT(i, i)
            pe.wait_ge(S("hT"), 3)
            for n in range(11):
                m = 12 + n
                w = min(512, IN_W - 512 * n)
                b0, b1, b2 = (banks[1 + 3 * (n % 2) + v] for v in range(3))
                pe.wait_ge(S(f"ld_slab{m % 3}"), 16 * (m // 3 + 1 + (7 if m % 3 == 0 else 0)))
                if n == 0:
                    pe.wait_ge(S("bc"), 3)
                if n >= 2:
                    pe.wait_ge(S("zin_a"), n - 1)
                    pe.wait_ge(S("zin_v"), n - 1)
                slab = slabs[m % 3]
                for k in range(KD):
                    first, final = k == 0, k == KD - 1
                    mm(b0[:, 0:w], hT[:, k, 0:P], slab[:, k, 0:w], start=first, stop=final)
                    mm(b1[:, 0:w], hT[:, k, P:2 * P], slab[:, k, 0:w], start=first, stop=final)
                    for j in range(-(-w // P)):
                        wj = min(P, w - P * j)
                        last = mm(b2[32 * j:32 * j + 32, 0:wj], hT[:, k, 2 * P:2 * P + NS], slab[:, k, P * j:P * j + wj],
                                  start=first, stop=final)
                last.then_inc(S("zin_mm"), 1)
            pe.wait_ge(S("ld_w1"), 48)
            pe.wait_ge(S("zin_a"), 11)
            pe.wait_ge(S("zin_v"), 11)
            nc.tensor.transpose(banks[4][:, 0:32], pe_rows[0:32], ident[0:32, 0:32]).then_inc(S("peT_ps"), 1)

            def unit(v):
                for c in range(4):
                    last = nc.tensor.transpose(banks[v][:, P * c:P * c + P], raw[v][:, P * c:P * c + P], ident)
                last.then_inc(S("pair_ps"), 1)

            with pe.Fori(0, NB) as b:
                for v in range(4):
                    pe.wait_ge(S(f"ld_raw{v}"), 32 * b + 32)
                    pe.wait_ge(S(f"pair_out{v}"), b)
                    unit(v)
            pe.wait_ge(S("ld_raw0"), 32 * NB + 16)
            pe.wait_ge(S("pair_out0"), NB)
            unit(0)
            after(pe, "peT")
            for v in range(2):
                for q in range(16):
                    last = mm(banks[5][:, 64 + v:65 + v], w1[:, v, q], peT[:, 16 * v + q:16 * v + q + 1], start=q == 0, stop=q == 15)
            last.then_inc(S("pconst_ps"), 1)
            for v in range(4):
                pe.wait_ge(S(f"pair_out{v}"), NB + (v == 0))
            after(pe, "pconst")
            for vg in range(4):
                v, g = vg // 2, vg % 2
                src = pairT[:, v, g, 0:NB * 512].rearrange("p (b c) -> p b c", b=NB)
                own = pairT[:, v, g, NB * 512:UN * P]
                for q in range(16):
                    mm(banks[vg][:, 0:NB * NCMP], w1[:, v, q], src[:, :, q:q + 8 * NCMP - 7:8], start=q == 0, stop=q == 15)
                for q in range(16):
                    last = mm(banks[4 + vg][:, 0:NCMP_P], w1[:, v, q], own[:, q:q + 8 * NCMP_P - 7:8],
                              start=q == 0, stop=q == 15)
                last.then_inc(S("pre_ps"), 1)
            pe.wait_ge(S("gelu"), 4)
            for g in range(2):
                mm(banks[4][DH * g:DH * g + DH, 0:NB * NCMP], w2[:, 0], geT[:, 0, g, 0:NB * NCMP], start=True, stop=True)
            for g in range(2):
                last = mm(banks[6][DH * g:DH * g + DH, 0:NCMP_P], w2[:, 0], geT[:, 0, g, NB * NCMP:NC_ALL], start=True, stop=True)
            for b in range(NB + 1):
                n, at = (NCMP, P * (b % 4)) if b < NB else (NCMP_P, P)
                for g in range(2):
                    last = mm(banks[(0, 1, 5)[b // 4]][0:n, at + DH * g:at + DH * g + DH], geT[:, 1, g, NCMP * b:NCMP * b + n],
                              w2[:, 1], start=True, stop=True)
            last.then_inc(S("comp_ps"), 1)

            for r in range(R):
                nc.tensor.transpose(banks[7][:, NS * r:NS * r + NS], z[0:NS, 2, P * r:P * r + P], ident[0:NS, 0:NS])
            for n, name in enumerate(("ks", "kw")):
                last = nc.tensor.transpose(banks[7][:, P + NS * n:P + NS * n + NS], zc(2, name, P), ident[0:NS, 0:NS])
            last.then_inc(S("sq_ps"), 1)
            after(pe, "sg_gate")
            mm(banks[2][:, 0:24], C("expand", NS), sg_gate[0:NS, 2], start=True, stop=True).then_inc(S("sgate_ps"), 1)
            after(pe, "comp_a")
            after(pe, "comp_v")
            after(pe, "sq")
            qb = lambda g, b: qz[DH * g:DH * g + DH, 144 * b - 16 * b:144 * b - 16 * b + P]
            for g in range(G):
                for b in range(NB):
                    last = mm(banks[(1, 3)[g]][:, 0:NCMP], qb(g, b), kcT[DH * g:DH * g + DH, NCMP * b:NCMP * b + NCMP],
                              start=b == 0, stop=b == NB - 1)
            last.then_inc(S("score_ps"), 1)
            after(pe, "imp")
            mm(banks[5][:, 0:32], C("gsum"), imp, start=True, stop=True).then_inc(S("imp_ps"), 1)

            def probs_T(branch, tiles, new, seq):
                pe.wait_ge(S("probs"), branch + 1)
                for t in range(tiles + new):
                    n = P if t < tiles else NS
                    if branch == 0:
                        n = NCMP
                    if t % 2 == 0 and seq + t // 2 >= 2:
                        pe.wait_ge(S("pT"), seq + t // 2 - 1)
                    for g in range(G):
                        last = nc.tensor.transpose(banks[6 + (seq + t // 2) % 2][0:n, (t % 2) * 256 + P * g:(t % 2) * 256 + P * g + P],
                                                   sS[:, g, P * t:P * t + n], ident)
                    if t % 2 == 1 or t == tiles + new - 1:
                        last.then_inc(S("pT_ps"), 1)

            def values(branch, tiles, vname, seq_end):
                pe.wait_ge(S("pT"), seq_end)
                for b in range(NB):
                    for t in range(tiles):
                        if branch == 0:
                            last = mm(banks[0][:, 32 * b:32 * b + 32], vcb[0:NCMP, b], pTs[0:NCMP, 0, :, 16 * b:16 * b + 16],
                                      start=True, stop=True)
                        else:
                            mm(banks[0][:, 32 * b:32 * b + 32], vpages[:, tiles * b + t], pTs[:, t, :, 16 * b:16 * b + 16],
                               start=t == 0, stop=False)
                    if branch:
                        last = mm(banks[0][:, 32 * b:32 * b + 32], zc(2, vname, P), pTs[0:NS, tiles, :, 16 * b:16 * b + 16],
                                  start=False, stop=True)
                last.then_inc(S("pv_ps"), 1)

            def keys(branch, tiles):
                base = NB * (branch - 1)
                width = P * tiles

                def score(b):
                    pe.wait_ge(S("key_a"), base + b + 1)
                    pe.wait_ge(S("key_v"), base + b + 1)
                    for c in range(0, width, 512):
                        for g in range(G):
                            last = mm(banks[1 + 2 * g + c // 512][:], qb(g, b), kTb[b % 2][DH * g:DH * g + DH, c:c + 512],
                                      start=b == 0, stop=b == NB - 1)
                    last.then_inc(S("score_b"), 1)

                for b in range(NB):
                    pe.wait_ge(S(f"ld_key{b % 2}"), 32 * (b // 2 + 1) if branch == 1 else 128 + 64 * (b // 2 + 1))
                    if branch == 2:
                        pe.wait_ge(S(f"ld_key_p{b % 2}"), 64 * (b // 2 + 1))
                    if base + b:
                        pe.wait_ge(S("key_a"), base + b)
                        pe.wait_ge(S("key_v"), base + b)
                    for t in range(tiles):
                        last = nc.tensor.transpose(banks[6 + 2 * t // tiles][:, P * (t % (tiles // 2)):P * (t % (tiles // 2)) + P],
                                                   kst[b % 2][:, t], ident)
                    last.then_inc(S("key_ps"), 1)
                    if b:
                        score(b - 1)
                score(NB - 1)
                for g in range(G):
                    last = mm(banks[(5, 0)[g]][:, 0:NS], qf[DH * g:DH * g + DH].rearrange("p b r t -> p (b r t)"),
                              knT[DH * g:DH * g + DH, 2 - branch], start=True, stop=True)
                last.then_inc(S("score_ps"), 1)

            probs_T(0, 1, 0, 0)
            values(0, 1, None, 1)
            pe.wait_ge(S("oS"), 1)
            keys(1, 4)
            probs_T(1, 4, 1, 1)
            values(1, 4, "vw", 4)
            pe.wait_ge(S("oS"), 2)
            keys(2, 8)
            probs_T(2, 8, 1, 4)
            values(2, 8, "vs", 9)

            for i in range(2):
                pe.wait_ge(S("scores_in"), 3) if i == 0 else pe.wait_ge(S("pq"), 1)
                for r in range(R):
                    nc.tensor.transpose(banks[1][:, P * r:P * r + P], z[:, i, P * r:P * r + P], ident)
                for n, name in enumerate(("ks", "kw")):
                    last = nc.tensor.transpose(banks[2][:, P * n:P * n + P], zc(i, name, P), ident)
                last.then_inc(S("pq_ps"), 1)
            pe.wait_ge(S("pq"), 2)
            pe.wait_ge(S("oS"), 3)

            def scores(u):
                i, branch, g = UNITS[u]
                width = P * (i + 1) if branch else NCMP_P
                if u:
                    pe.wait_ge(S("p_in"), u)
                for r in range(R):
                    key = kT[DH * g:DH * g + DH, branch - 1, 0:width] if branch else kcT[DH * g:DH * g + DH, NB * NCMP:NC_ALL]
                    last = mm(banks[r // 2][:, 256 * (r % 2):256 * (r % 2) + width], qT[DH * g:DH * g + DH, r, P * i:P * i + P],
                              key, start=True, stop=True)
                last.then_inc(S("p_score"), 1)

            def probabilities_T(u, t):
                n = P if UNITS[u][1] else NCMP_P
                pe.wait_ge(S("p_probs"), u + 1)
                if _tiles_before(u) + t:
                    pe.wait_ge(S("ppT"), _tiles_before(u) + t)
                for r in range(R):
                    last = nc.tensor.transpose(banks[2][0:n, P * r:P * r + P], sP[u % 2][:, r, P * t:P * t + n], ident)
                last.then_inc(S("ppT_ps"), 1)

            def values_of(u):
                i, branch, g = UNITS[u]
                tiles, n = (i + 1, P) if branch else (1, NCMP_P)
                pe.wait_ge(S("ppT"), _tiles_before(u) + tiles)
                if u:
                    pe.wait_ge(S("on"), u)
                for r in range(R):
                    for t in range(tiles):
                        if branch:
                            o = OFF[("vs", "vw")[branch - 1]] + DH * g
                            val = z[:, t, o:o + DH]
                        else:
                            val = vcb[0:NCMP_P, NB, DH * g:DH * g + DH]
                        last = mm(banks[3][:, DH * r:DH * r + DH], pTp[u % 2][0:n, t, r], val, start=t == 0, stop=t == tiles - 1)
                last.then_inc(S("p_pv"), 1)

            def transposed_output():
                for i in range(2):
                    if i:
                        pe.wait_ge(S("onT"), 1)
                    else:
                        pe.wait_ge(S("on"), len(UNITS))
                    for r in range(R):
                        last = nc.tensor.transpose(banks[0][:, P * r:P * r + P], on[:, i, P * r:P * r + P], ident)
                    last.then_inc(S("onT_ps"), 1)
            def hgrn_inputs(i):
                r = ROWS[i]
                b0, b1, b2 = banks[4:7] if i < 2 else banks[1:4]
                if i == 0:
                    after(pe, "hk")
                    after(pe, "gl")
                if i == 1:
                    pe.wait_ge(S("oh_cp"), i)
                    pe.wait_ge(S("att"), HH * i)
                    pe.wait_ge(S("state"), i)
                for h in range(HH):
                    c = slice(DK * h, DK * h + DK)
                    o = slice(r * h, r * h + r)
                    mm(b0[:, o], gl[0:r, i, c], C("tri") if i < 2 else C("bt32", NS), start=True, stop=True)
                    nc.tensor.transpose(b1[:, o], zc(i, "hq", 512)[:, c], ident[0:r, 0:r])
                    last = nc.tensor.transpose(b2[:, o], zc(i, "hf", 512)[:, c], ident[0:r, 0:r])
                last.then_inc(S("hg_ps"), 1)

            def hgrn_attention(i, h):
                if h == 0:
                    pe.wait_ge(S("hg_cp"), i + 1)
                if h:
                    pe.wait_ge(S("att"), HH * i + h)
                pe.wait_ge(S("hk_d"), HH * i + h + 1)
                for s in range(8):
                    last = mm(banks[4][:, 16 * s:16 * s + 16], dks[h % 2][:, s], dqs[h % 2][:, s], start=True, stop=True)
                last.then_inc(S("att_ps"), 1)

            def hgrn_values(i, h):
                c = slice(DK * h, DK * h + DK)
                pe.wait_ge(S("att"), HH * i + h + 1)
                last = mm(banks[5][:, c], att, zc(i, "hi", 512)[:, c], start=True, stop=i == 0)
                if i:
                    last = mm(banks[5][:, c], qe[:, h], state[:, h], start=False, stop=True)
                last.then_inc(S("o_ps"), 1)

            def hgrn_keys_back(i):
                pe.wait_ge(S("kd"), i + 1)
                for h in range(HH):
                    last = nc.tensor.transpose(banks[6][:, P * h:P * h + P], dks[0][:, h], ident)
                last.then_inc(S("kh_ps"), 1)

            def hgrn_state(i):
                pe.wait_ge(S("kh"), i + 1)
                for h in range(HH):
                    c = slice(DK * h, DK * h + DK)
                    last = mm(banks[6][:, c], kh[:, c], zc(i, "hi", 512)[:, c], start=True, stop=True)
                last.then_inc(S("st_ps"), 1)

            def hgrn_out(i, src):
                r = ROWS[i]
                pe.wait_ge(S("oh"), i + 1)
                if i:
                    pe.wait_ge(S("ohT"), i)
                for h in range(HH):
                    last = nc.tensor.transpose(banks[7][:, P * h:P * h + r], src[0:r, h], ident[0:r, 0:r])
                last.then_inc(S("ohT_ps"), 1)

            steps = {"scores": scores, "probs_T": probabilities_T, "values": values_of, "inputs": hgrn_inputs,
                     "attention": hgrn_attention, "head": hgrn_values, "keys_back": hgrn_keys_back, "state": hgrn_state,
                     "out": lambda i: hgrn_out(i, oh)}
            for name, args in PROMPT_STEPS:
                if name in steps:
                    steps[name](*args)
            transposed_output()
            pe.wait_ge(S("hg_cp"), 2)
            hgrn_inputs(2)
            after(pe, "s_kq")
            for h in range(HH):
                last = mm(banks[4][0:NS, NS * h:NS * h + NS], sb_[:, 5, h], sb_[:, 4, h], start=True, stop=True)
            last.then_inc(S("att_ps"), 1)
            for h in range(HH):
                last = nc.tensor.transpose(banks[6][0:NS, P * h:P * h + P], sb_[:, 6, h], ident)
            last.then_inc(S("kh_ps"), 1)
            pe.wait_ge(S("att"), 2 * HH + 1)
            pe.wait_ge(S("ld_s0"), 16)
            pe.wait_ge(S("oh_cp"), 2)
            for h in range(HH):
                c = slice(DK * h, DK * h + DK)
                mm(banks[5][0:NS, c], att_s[0:NS, h], zc(2, "hi", 512)[:, c], start=True, stop=False)
                for b in range(NB):
                    last = mm(banks[5][0:NS, c], qep[:, h, NS * b:NS * b + NS], s0[:, HH * b + h], start=False, stop=b == NB - 1)
            last.then_inc(S("o_ps"), 1)
            pe.wait_ge(S("kh"), 3)
            after(pe, "vm")
            for n in range(8):
                h, half = n // 2, n % 2
                if n >= 2:
                    pe.wait_ge(S("s_state"), n - 1)
                mm(banks[n % 2][:], kh_s[0:NS, DK * h:DK * h + DK], vm[0:NS, 4 * half:4 * half + 4, DK * h:DK * h + DK],
                   start=True, stop=True).then_inc(S("sst_ps"), 1)
            hgrn_out(2, oh_s)

            spread(3, 8)
            spread(4, 6)
            pe.wait_ge(S("bc"), 5)

            pe.wait_ge(S("ld_wa"), 192)
            after(pe, "onS")
            pe.wait_ge(S("ohT"), 3)
            pe.wait_ge(S("s_state"), 8)
            for i in range(3):
                t = slice(P * i, P * i + ROWS[i])
                if i:
                    pe.wait_ge(S("m_rows"), i)
                for n in range(2):
                    for k in range(4):
                        mm(banks[n][0:ROWS[i], :], onT[:, k, t], wbr[k][:, 512 * n:512 * n + 512], start=k == 0, stop=k == 3)
                    for k in range(4):
                        last = mm(banks[2 + n][0:ROWS[i], :], ohT[:, k, t], wbr[4 + k][:, 512 * n:512 * n + 512], start=k == 0, stop=k == 3)
                last.then_inc(S("mrg_ps"), 1)
                pe.wait_ge(S("m_rows"), i + 1)
                if i:
                    pe.wait_ge(S("mT"), i)
                for k in range(KD):
                    last = nc.tensor.transpose(banks[4 + k // 4][:, (k % 4) * P:(k % 4) * P + ROWS[i]],
                                               mrow[0:ROWS[i], P * k:P * k + P], ident[0:ROWS[i], 0:ROWS[i]])
                last.then_inc(S("mT_ps"), 1)
            pe.wait_ge(S("ld_wo"), 16)
            pe.wait_ge(S("mT"), 3)
            for i in range(3):
                t = slice(P * i, P * i + ROWS[i])
                if i:
                    pe.wait_ge(S("out_cp"), i)
                for n in range(2):
                    for k in range(KD):
                        last = mm(banks[6 + n][0:ROWS[i], :], mT[:, k, t], wo[k][:, 512 * n:512 * n + 512],
                                  start=k == 0, stop=k == KD - 1)
                last.then_inc(S("out_ps"), 1)
            for i in range(3):
                pe.wait_ge(S("h2"), i + 1)
                if i:
                    pe.wait_ge(S("h2T"), i)
                for k in range(KD):
                    last = nc.tensor.transpose(banks[(0, 7)[k // 4]][:, (k % 4) * P:(k % 4) * P + ROWS[i]],
                                               h2r[0:ROWS[i], i, P * k:P * k + P], ident[0:ROWS[i], 0:ROWS[i]])
                last.then_inc(S("h2T_ps"), 1)
            pe.wait_ge(S("h2T"), 3)
            pe.wait_ge(S("ld_wr"), 32)
            for i in range(3):
                for k in range(KD):
                    last = mm(banks[1][0:ROWS[i], E * i:E * i + E], h2T[:, k, P * i:P * i + ROWS[i]], wr[:, k],
                              start=k == 0, stop=k == KD - 1)
            last.then_inc(S("lg_ps"), 1)
            pe.wait_ge(S("out_cp"), 3)
            spread(5, 10)
            pe.wait_ge(S("bc"), 6)
            pe.wait_ge(S("mk"), 3)
            for i in range(3):
                r = ROWS[i]
                o = slice(E * i, E * i + E)
                mm(banks[2][0:r, o], C("stri", r)[:, 0:r], mk[0:r, i], start=True, stop=i == 0)
                for v in range(i):
                    mm(banks[2][0:r, o], ones[:, 0:r], mk[:, v], start=False, stop=v == i - 1)
            for i in range(3):
                last = mm(banks[3][0:E, 0:P], mk[0:ROWS[i], i], ones[0:ROWS[i]], start=i == 0, stop=i == 2)
            last.then_inc(S("cnt_ps"), 1)
            after(pe, "nch")
            mm(banks[4][:, 0:E], nchT[0:E], C("stri", E)[:, 0:E], start=True, stop=True)
            mm(banks[4][:, E:2 * E], nchT[0:E], C("tri", E)[:, 0:E], start=True, stop=True).then_inc(S("base_ps"), 1)

            def chunk_T():
                for k in range(KD):
                    last = nc.tensor.transpose(banks[2][:, SLOT * k:SLOT * k + SLOT], xrow[0:SLOT, P * k:P * k + P],
                                               ident[0:SLOT, 0:SLOT])
                last.then_inc(S("xcT_ps"), 1)

            after(pe, "tab")
            pe.wait_ge(S("ld_x2"), 16)
            chunk_T()
            with pe.Fori(0, E // 4) as grp:
                for j in range(4):
                    before = pe.value_load(tab[0:1, bass.ds(grp * 4 + (E + j), 1)], min_val=0, max_val=CMAX)
                    upto = pe.value_load(tab[0:1, bass.ds(grp * 4 + j, 1)], min_val=1, max_val=CMAX)
                    with pe.Fori(before, upto) as c:
                        at = 32 * (j % 2)
                        pe.wait_ge(S("xcT"), c + 1)
                        pe.wait_ge(S(f"ld_bias{j % 2}"), grp * 64 + 32 * (j // 2) + 32)
                        one = ones[at:at + 1, 0:SLOT]
                        for part in range(2):
                            for s in range(2):
                                mm(banks[part][SLOT * s:SLOT * s + SLOT, :], one,
                                   bias[at:at + 1, D * part + 512 * s:D * part + 512 * s + 512], start=True, stop=False)
                        for q in range(8):
                            pos, use = (12 * j + q) % 16, (12 * j + q) // 16
                            pe.wait_ge(S(f"ld_piece{pos}"), grp * 48 + 16 * use + 16)
                            if q == 7:
                                pe.wait_ge(S("ld_x2"), c * 16 + 32)
                            for part in range(2):
                                for s in range(2):
                                    last = mm(banks[part][SLOT * s:SLOT * s + SLOT, :], xcT[:, q],
                                              ring[pos][:, D * part + 512 * s:D * part + 512 * s + 512], start=False, stop=q == 7)
                            last.then_inc(S("piece_used"), 1)
                        chunk_T()
                        pe.wait_ge(S("act"), c + 1)
                        for k in range(4):
                            last = nc.tensor.transpose(banks[3][:, P * k:P * k + P], ac[:, P * k:P * k + P], ident)
                        last.then_inc(S("aT_ps"), 1)
                        pe.wait_ge(S("yc"), c)
                        for s in range(2):
                            mm(banks[4][SLOT * s:SLOT * s + SLOT, :], one, bias[at:at + 1, 2 * D + 512 * s:2 * D + 512 * s + 512],
                               start=True, stop=False)
                        pe.wait_ge(S("aT"), c + 1)
                        for q in range(8, 12):
                            pos, use = (12 * j + q) % 16, (12 * j + q) // 16
                            pe.wait_ge(S(f"ld_piece{pos}"), grp * 48 + 16 * use + 16)
                            for v in range(2):
                                f = 2 * (q - 8) + v
                                lhs = aT[:, P * (f % 4) + SLOT * (f // 4):P * (f % 4) + SLOT * (f // 4) + SLOT]
                                for s in range(2):
                                    last = mm(banks[4][SLOT * s:SLOT * s + SLOT, :], lhs,
                                              ring[pos][:, D * v + 512 * s:D * v + 512 * s + 512], start=False, stop=f == 7)
                            last.then_inc(S("piece_used"), 1)

        @block.scalar
        def _(act):
            fn = nc.scalar.activation
            act.wait_ge(S("ld_c"), 32)
            after(act, "zeroed")
            fn(sc32[0:1 + NB], c9[0:1 + NB], ACT.Silu).then_inc(S("silu_c"), 1)

            def spread_out(q, dst):
                act.wait_ge(S("bc_ps"), q + 1)
                for n in range(2):
                    nc.scalar.copy(dst[:, 0, 512 * n:512 * n + 512], banks[3 + n][:])
                    last = nc.scalar.copy(dst[0:32, 1, 512 * n:512 * n + 512], banks[5 + n][0:32, :])
                last.then_inc(S("bc"), 1)

            spread_out(0, mod_rows[:, 0])
            spread_out(1, mod_rows[:, 1])
            spread_out(2, gate_rows)

            def root_mean_square(i, seq):
                r = ROWS[i]
                act.wait_ge(S("ss"), seq + 1)
                fn(rt_[0:r, i:i + 1], ss[0:r, i:i + 1], ACT.Sqrt, bias=eps_t[0:r], scale=1.0 / D).then_inc(S("rms"), 1)

            def hT_out(i, seq):
                act.wait_ge(S("hT_ps"), seq + 1)
                for v in range(2):
                    last = nc.scalar.copy(hT[:, 4 * v:4 * v + 4, P * i:P * i + ROWS[i]],
                                          banks[(0, 7)[v]][:].rearrange("p (k t) -> p k t", k=4)[:, :, 0:ROWS[i]])
                last.then_inc(S("hT"), 1)

            for i in range(3):
                root_mean_square(i, i)
                hT_out(i, i)
            for n in range(11):
                w = min(512, IN_W - 512 * n)
                b0, b1, b2 = (banks[1 + 3 * (n % 2) + v] for v in range(3))
                act.wait_ge(S("zin_mm"), n + 1)
                last = nc.scalar.copy(z[:, 0, 512 * n:512 * n + w], b0[:, 0:w])
                for j in range(0, -(-w // P), 2):
                    wj = min(P, w - P * j)
                    last = nc.scalar.copy(z[0:32, 2, 512 * n + P * j:512 * n + P * j + wj], b2[32 * j:32 * j + 32, 0:wj])
                last.then_inc(S("zin_a"), 1)
            act.wait_ge(S("zin_v"), 11)
            act.wait_ge(S("zin_a"), 11)
            fn(sg_gate[:, 0:2], z[:, 0:2, OFF["gn"]:OFF["gn"] + 24], ACT.Sigmoid)
            fn(sg_gate[0:NS, 2], zc(2, "gn", 24), ACT.Sigmoid).then_inc(S("sg_gate"), 1)

            with act.Fori(0, NB) as b:
                for v in (0, 2):
                    act.wait_ge(S("pair_ps"), 4 * b + v + 1)
                    for g in range(G):
                        for s in range(2):
                            last = nc.scalar.copy(pairT[DH * s:DH * s + DH, :, g, bass.ds((4 * b + v) * P, P)],
                                                  by_parity(banks[v])[DH * g:DH * g + DH, s])
                    last.then_inc(S(f"pair_out{v}"), 1)
            act.wait_ge(S("pair_ps"), 33)
            for g in range(G):
                for s in range(2):
                    last = nc.scalar.copy(pairT[DH * s:DH * s + DH, :, g, NB * 512:], by_parity(banks[0])[DH * g:DH * g + DH, s])
            last.then_inc(S("pair_out0"), 1)
            fn(z[:, 0:2, OFF["hf"]:OFF["hf"] + 512], z[:, 0:2, OFF["hf"]:OFF["hf"] + 512], ACT.Sigmoid)
            fn(zc(2, "hf", 512), zc(2, "hf", 512), ACT.Sigmoid).then_inc(S("hf_sig"), 1)
            fn(z[:, 0:2, OFF["ga"]:IN_W], z[:, 0:2, OFF["ga"]:IN_W], ACT.Sigmoid)
            fn(z[0:NS, 2, OFF["ga"]:IN_W], z[0:NS, 2, OFF["ga"]:IN_W], ACT.Sigmoid)
            for name in ("hq", "hg"):
                fn(z[:, 0:2, OFF[name]:OFF[name] + 512], z[:, 0:2, OFF[name]:OFF[name] + 512], ACT.Silu)
                fn(zc(2, name, 512), zc(2, name, 512), ACT.Silu)
            after(act, "pconst")
            for vg in range(4):
                v, g = vg // 2, vg % 2
                act.wait_ge(S("pre_ps"), vg + 1)
                fn(geT[:, v, g, 0:NB * NCMP], banks[vg][:, 0:NB * NCMP], ACT.Gelu_apprx_tanh, bias=pconst[:, v:v + 1])
                fn(geT[:, v, g, NB * NCMP:NC_ALL], banks[4 + vg][:, 0:NCMP_P], ACT.Gelu_apprx_tanh,
                   bias=pconst[:, v:v + 1]).then_inc(S("gelu"), 1)
            after(act, "comp_ps")
            nc.scalar.copy(kcT[:, 0:NB * NCMP], banks[4][:, 0:NB * NCMP])
            nc.scalar.copy(kcT[:, NB * NCMP:NC_ALL], banks[6][:, 0:NCMP_P]).then_inc(S("comp_a"), 1)

            def exps(branch, width):
                act.wait_ge(S("s_max"), branch + 1)
                for g in range(G):
                    last = fn(sS[:, g, 0:width], sS[:, g, 0:width], ACT.Exp, bias=sa_max[:, g:g + 1],
                              accum_out=sa_sum[:, g:g + 1])
                last.then_inc(S("s_exp"), 1)

            def probs_out(seq, n_banks, widths):
                for t in range(n_banks):
                    act.wait_ge(S("pT_ps"), seq + t + 1)
                    src = banks[6 + (seq + t) % 2][:].rearrange("p (t g r) -> p t g r", t=2, g=G)
                    for w in range(2):
                        if 2 * t + w < len(widths):
                            n = widths[2 * t + w]
                            last = nc.scalar.copy(pTs[0:n, 2 * t + w], src[0:n, w])
                    last.then_inc(S("pT"), 1)

            def keys_out(branch, tiles):
                for b in range(NB):
                    act.wait_ge(S("key_ps"), NB * (branch - 1) + b + 1)
                    if NB * (branch - 1) + b >= 2:
                        act.wait_ge(S("score_b"), NB * (branch - 1) + b - 1)
                    w = P * tiles // 2
                    nc.scalar.copy(kTb[b % 2][:, 0:w], banks[6][:, 0:w]).then_inc(S("key_a"), 1)

            exps(0, NCMP)
            probs_out(0, 1, [NCMP])
            keys_out(1, 4)
            exps(1, WIN_W)
            act.wait_ge(S("pv_ps"), 1)
            probs_out(1, 3, [P] * 4 + [NS])
            keys_out(2, 8)
            exps(2, SEL_W)
            act.wait_ge(S("pv_ps"), 2)
            probs_out(4, 5, [P] * 8 + [NS])

            for i in range(2):
                act.wait_ge(S("pq_ps"), i + 1)
                fn(qT[:, :, P * i:P * i + P], banks[1][:].rearrange("p (r t) -> p r t", r=R), ACT.Copy, scale=0.125)
                nc.scalar.copy(kT[:, :, P * i:P * i + P], banks[2][:, 0:256].rearrange("p (n t) -> p n t", n=2)
                               ).then_inc(S("pq"), 1)
            act.wait_ge(S("pv_ps"), 3)

            def exps_of(u):
                i, branch, g = UNITS[u]
                width = P * (i + 1) if branch else NCMP_P
                act.wait_ge(S("p_max"), u + 1)
                for r in range(R):
                    at = R * (u % 2) + r
                    last = fn(sP[u % 2][:, r, 0:width], sP[u % 2][:, r, 0:width], ACT.Exp, bias=pr_max[:, at:at + 1],
                              accum_out=pr_sum[:, at:at + 1])
                last.then_inc(S("p_exp"), 1)

            def probs_T_out(u, t):
                n = P if UNITS[u][1] else NCMP_P
                act.wait_ge(S("ppT_ps"), _tiles_before(u) + t + 1)
                if u >= 2:
                    act.wait_ge(S("p_pv"), u - 1)
                nc.scalar.copy(pTp[u % 2][0:n, t], banks[2][0:n, :].rearrange("p (r t) -> p r t", r=R)).then_inc(S("ppT"), 1)

            def output_T_out():
                for i in range(2):
                    act.wait_ge(S("onT_ps"), i + 1)
                    nc.scalar.copy(onT[:, :, P * i:P * i + P], banks[0][:].rearrange("p (r t) -> p r t", r=R)
                                   ).then_inc(S("onT"), 1)
            after(act, "lb_d")
            fn(lb, lb, ACT.Sigmoid).then_inc(S("lb"), 1)
            after(act, "f")
            fn(gl[:, 0:2], z[:, 0:2, OFF["hf"]:OFF["hf"] + 512], ACT.Ln)
            fn(gl[0:NS, 2], zc(2, "hf", 512), ACT.Ln).then_inc(S("gl"), 1)

            def hgrn_rms(i, src, sq):
                r = ROWS[i]
                act.wait_ge(S("hss"), i + 1)
                fn(hrt[0:r, 4 * i:4 * i + 4], hss[0:r, 4 * i:4 * i + 4], ACT.Sqrt, bias=eps_t[0:r], scale=1.0 / DK
                   ).then_inc(S("hrt"), 1)

            def hgrn_out_a(i):
                r = ROWS[i]
                act.wait_ge(S("ohT_ps"), i + 1)
                nc.scalar.copy(ohT[:, :, P * i:P * i + r], banks[7][:].rearrange("p (h t) -> p h t", h=HH)[:, :, 0:r]
                               ).then_inc(S("ohT"), 1)

            def hgrn_inputs_out(i):
                act.wait_ge(S("hg_ps"), i + 1)
                if i:
                    act.wait_ge(S("kd"), i)
                    act.wait_ge(S("o_ps"), HH * i)
                    act.wait_ge(S("state"), i)
                nc.scalar.copy(bT, banks[4][:].rearrange("p (h t) -> p h t", h=HH))
                nc.scalar.copy(hqT, banks[5][:].rearrange("p (h t) -> p h t", h=HH))
                nc.scalar.copy(hkT, banks[6][:].rearrange("p (h t) -> p h t", h=HH)).then_inc(S("hg_cp"), 1)
                act.wait_ge(S("hg_cp"), i + 1)
                fn(ebT, bT, ACT.Exp).then_inc(S("ebT"), 1)

            def hgrn_decays(i, h):
                act.wait_ge(S("hd"), HH * i + h + 1)
                fn(dks[h % 2], dks[h % 2], ACT.Exp)
                fn(dqs[h % 2], dqs[h % 2], ACT.Exp).then_inc(S("he"), 1)

            def hgrn_end_decays(i):
                act.wait_ge(S("kd_d"), i + 1)
                fn(dks[0][:, 0:4], dks[0][:, 0:4], ACT.Exp).then_inc(S("kd_e"), 1)

            def hgrn_keys_out(i):
                act.wait_ge(S("kh_ps"), i + 1)
                nc.scalar.copy(kh, banks[6][:]).then_inc(S("kh"), 1)

            def hgrn_result_out(i):
                act.wait_ge(S("o_ps"), HH * (i + 1))
                if i:
                    act.wait_ge(S("ohT_ps"), i)
                nc.scalar.copy(oh, banks[5][:].rearrange("p (h v) -> p h v", h=HH)).then_inc(S("oh_cp"), 1)

            steps = {"exps": exps_of, "probs_out": probs_T_out, "inputs_out": hgrn_inputs_out, "decays": hgrn_decays,
                     "end_decays": hgrn_end_decays, "keys_out": hgrn_keys_out, "result": hgrn_result_out,
                     "rms": lambda i: hgrn_rms(i, oh, osq), "out_T": hgrn_out_a}
            for name, args in PROMPT_STEPS:
                if name in steps:
                    steps[name](*args)
            output_T_out()
            act.wait_ge(S("hg_ps"), 3)
            after(act, "s_free")
            for n in range(3):
                last = nc.scalar.copy(sb_[:, n], banks[1 + n][:, 0:P].rearrange("p (h t) -> p h t", h=HH))
            last.then_inc(S("hg_cp"), 1)
            act.wait_ge(S("hg_cp"), 3)
            fn(sb_[:, 3], sb_[:, 0], ACT.Exp)
            fn(sb_[:, 5], sb_[:, 0], ACT.Exp, scale=-1.0).then_inc(S("ebT"), 1)
            act.wait_ge(S("kd_d"), 3)
            fn(sb_[:, 6], sb_[:, 6], ACT.Exp).then_inc(S("kd_e"), 1)
            act.wait_ge(S("kh_ps"), 3)
            nc.scalar.copy(kh_s[0:NS], banks[6][0:NS, :]).then_inc(S("kh"), 1)
            act.wait_ge(S("o_ps"), 2 * HH + 1)
            nc.scalar.copy(oh_s[0:NS], banks[5][0:NS, :].rearrange("p (h v) -> p h v", h=HH)).then_inc(S("oh_cp"), 1)
            hgrn_rms(2, oh_s, osq_s)
            hgrn_out_a(2)
            spread_out(3, mod_rows[:, 0])
            spread_out(4, mod_rows[:, 1])

            for i in range(3):
                act.wait_ge(S("mT_ps"), i + 1)
                for v in range(2):
                    last = nc.scalar.copy(mT[:, 4 * v:4 * v + 4, P * i:P * i + ROWS[i]],
                                          banks[4 + v][:].rearrange("p (k t) -> p k t", k=4)[:, :, 0:ROWS[i]])
                last.then_inc(S("mT"), 1)
            for i in range(3):
                r = ROWS[i]
                act.wait_ge(S("out_ps"), i + 1)
                if i:
                    act.wait_ge(S("y1"), i)
                for n in range(2):
                    last = nc.scalar.copy(orow[0:r, 512 * n:512 * n + 512], banks[6 + n][0:r, :])
                last.then_inc(S("out_cp"), 1)
                root_mean_square(i, 3 + i)
            for i in range(3):
                root_mean_square(i, 6 + i)
                act.wait_ge(S("h2T_ps"), i + 1)
                for v in range(2):
                    last = nc.scalar.copy(h2T[:, 4 * v:4 * v + 4, P * i:P * i + ROWS[i]],
                                          banks[(0, 7)[v]][:].rearrange("p (k t) -> p k t", k=4)[:, :, 0:ROWS[i]])
                last.then_inc(S("h2T"), 1)
            act.wait_ge(S("y1"), 3)
            spread_out(5, gate_rows)
            for i in range(3):
                r = ROWS[i]
                act.wait_ge(S("top"), i + 1)
                fn(wts[0:r, i], top8[0:r, 0:4], ACT.Exp, bias=negtop[0:r], accum_out=wsum[0:r]).then_inc(S("wexp"), 1)

            after(act, "tab")
            n_chunks = act.value_load(tab[0:1, E - 1:E], min_val=E, max_val=CMAX)
            act.wait_ge(S("xcT_ps"), 1)
            act.wait_ge(S("scattered"), 16 * 12)
            nc.scalar.copy(xcT, banks[2][:].rearrange("p (k s) -> p k s", s=SLOT)).then_inc(S("xcT"), 1)
            with act.Fori(0, n_chunks) as c:
                act.wait_ge(S("gate"), c + 1)
                fn(sg, gt, ACT.Sigmoid, scale=1.702).then_inc(S("sig"), 1)
                act.wait_ge(S("xcT_ps"), c + 2)
                nc.scalar.copy(xcT, banks[2][:].rearrange("p (k s) -> p k s", s=SLOT)).then_inc(S("xcT"), 1)
                act.wait_ge(S("piece_used"), c * 12 + 12)
                act.wait_ge(S("st_yc"), c * 32)
                nc.scalar.copy(yc, banks[4][:]).then_inc(S("yc"), 1)
            act.wait_ge(S("st_yc"), n_chunks * 32)
            nc.scalar.copy(gathered, eps_t).then_inc(S("all_out"), 1)
            for i in range(3):
                root_mean_square(i, 9 + i)

        @block.vector
        def _(dve):
            V = nc.vector
            V.memset(sc32[0:32], 0.0).then_inc(S("zeroed"), 1)
            V.memset(ones, 1.0)
            V.memset(eps_t, EPS)
            V.memset(zero_t, 0.0).then_inc(S("zero_t"), 1)
            after(dve, "sct_ps")
            V.tensor_copy(scT, banks[0][:, 0:KD * 32].rearrange("p (k r) -> p k r", r=32)).then_inc(S("sct"), 1)
            dve.wait_ge(S("ld_bada"), 64)
            for n in range(12):
                dve.wait_ge(S("mod_mm"), n + 1)
                V.tensor_tensor(mod[:, n], banks[1 + n % 2][:, 0:P], bada[:, n], ALU.add).then_inc(S("mod_v"), 1)
            dve.wait_ge(S("ld_wn"), 256)
            dve.wait_ge(S("mod_v"), 12)
            V.scalar_tensor_tensor(mod[:, 2:4], mod[:, 2:4], 1.0, wn[:, 0:2], ALU.add, ALU.mult)
            V.tensor_tensor(mod[:, 4:6], mod[:, 4:6], wn[:, 2:4], ALU.mult)
            V.scalar_tensor_tensor(mod[:, 8:10], mod[:, 8:10], 1.0, wn[:, 4:6], ALU.add, ALU.mult)
            V.tensor_tensor(mod[:, 10:12], mod[:, 10:12], wn[:, 6:8], ALU.mult).then_inc(S("mod_w"), 1)

            def normed_rows(i, seq, reuse):
                r, ps = ROWS[i], i // 2
                if reuse is not None:
                    dve.wait_ge(S("hT_ps"), reuse)
                link(dve, "dve", V.tensor_tensor_reduce(h_rows[0:r], x[0:r, i], x[0:r, i], 1.0, 0.0, ALU.mult, ALU.add,
                                                        ss[0:r, i:i + 1]))
                V.tensor_copy(ss[0:r, 3:4], ss[0:r, i:i + 1]).then_inc(S("ss"), 1)
                dve.wait_ge(S("rms"), seq + 1)
                link(dve, "dve", V.reciprocal(rstd[0:r, i:i + 1], rt_[0:r, i:i + 1]))
                link(dve, "dve", V.scalar_tensor_tensor(h_rows[0:r], x[0:r, i], rstd[0:r, i:i + 1], mod_rows[0:r, 0, ps],
                                                        ALU.mult, ALU.mult))
                V.tensor_tensor(h_rows[0:r], h_rows[0:r], mod_rows[0:r, 1, ps], ALU.add).then_inc(S("h_rows"), 1)

            dve.wait_ge(S("ld_x"), 32)
            dve.wait_ge(S("bc"), 2)
            for i in range(3):
                normed_rows(i, i, i if i else None)
            for n in range(11):
                w = min(512, IN_W - 512 * n)
                b0, b1, b2 = (banks[1 + 3 * (n % 2) + v] for v in range(3))
                dve.wait_ge(S("zin_mm"), n + 1)
                last = V.tensor_copy(z[:, 1, 512 * n:512 * n + w], b1[:, 0:w])
                for j in range(1, -(-w // P), 2):
                    wj = min(P, w - P * j)
                    last = V.tensor_copy(z[0:32, 2, 512 * n + P * j:512 * n + P * j + wj], b2[32 * j:32 * j + 32, 0:wj])
                last.then_inc(S("zin_v"), 1)
            after(dve, "peT_ps")
            V.tensor_copy(peT, banks[4][:, 0:32]).then_inc(S("peT"), 1)
            with dve.Fori(0, NB) as b:
                for v in (1, 3):
                    dve.wait_ge(S("pair_ps"), 4 * b + v + 1)
                    for g in range(G):
                        for s in range(2):
                            last = V.tensor_copy(pairT[DH * s:DH * s + DH, :, g, bass.ds((4 * b + v) * P, P)],
                                                 by_parity(banks[v])[DH * g:DH * g + DH, s])
                    last.then_inc(S(f"pair_out{v}"), 1)
            after(dve, "pconst_ps")
            V.tensor_copy(pconst, banks[5][:, 64:66]).then_inc(S("pconst"), 1)
            after(dve, "comp_ps")
            V.tensor_copy(vcb[0:NCMP, 0:4], banks[0][0:NCMP, :].rearrange("p (b c) -> p b c", b=4))
            V.tensor_copy(vcb[0:NCMP, 4:8], banks[1][0:NCMP, :].rearrange("p (b c) -> p b c", b=4))
            V.tensor_copy(vcb[0:NCMP_P, 8], banks[5][0:NCMP_P, P:2 * P]).then_inc(S("comp_v"), 1)

            V.memset(imp, 0.0)
            link(dve, "dve", V.memset(qz, 0.0))
            after(dve, "sq_ps")
            link(dve, "dve", V.tensor_scalar(qf.rearrange("p b r t -> p r b t"),
                                             banks[7][:, 0:P].rearrange("p (r b t) -> p r b t", r=R, b=NB), 0.125, None, ALU.mult))
            V.tensor_copy(qz.rearrange("p (b c) -> p b c", c=144)[:, :, 0:16], qf.rearrange("p b r t -> p b (r t)"))
            V.tensor_copy(knT, banks[7][:, P:P + 2 * NS].rearrange("p (n t) -> p n t", n=2)).then_inc(S("sq"), 1)
            after(dve, "sgate_ps")
            link(dve, "dve", V.tensor_tensor(sa_gate3.rearrange("p (a r) -> p a r", r=R),
                                             banks[2][:, 0:24].rearrange("p (a r) -> p a r", r=R),
                                             C("rdiag").unsqueeze(1).broadcast_to([P, 6, R]), ALU.mult))
            link(dve, "dve", V.tensor_reduce(sa_gate, sa_gate3.rearrange("p (a r) -> p a r", r=R), AX, ALU.add))

            def softmax(branch, width):
                link(dve, "dve", V.tensor_reduce(sa_coef, sS[:, :, 0:width], AX, ALU.max))
                V.tensor_scalar(sa_max, sa_coef, -1.0, None, ALU.mult).then_inc(S("s_max"), 1)
                dve.wait_ge(S("s_exp"), branch + 1)
                link(dve, "dve", V.reciprocal(sa_coef, sa_sum))
                if branch == 0:
                    for g in range(G):
                        link(dve, "dve", V.tensor_scalar(sS[:, g, 0:width], sS[:, g, 0:width], sa_coef[:, g:g + 1], None, ALU.mult))
                    imp3 = imp.rearrange("p (g j) -> p g j", g=G)
                    for g in range(G):
                        last = V.tensor_reduce(imp3[:, g, 0:14], sS[:, g, 4:60].rearrange("p (j s) -> p j s", s=4), AX, ALU.add)
                    link(dve, "dve", last)
                    V.tensor_tensor(imp3[:, :, 0:14], imp3[:, :, 0:14], sS[:, :, 3:56:4], ALU.add).then_inc(S("imp"), 1)
                    gates = sa_gate[:, 0:2]
                    after(dve, "imp")
                    for g in range(G):
                        last = V.tensor_scalar(sS[:, g, 0:width], sS[:, g, 0:width], gates[:, g:g + 1], None, ALU.mult)
                    last.then_inc(S("probs"), 1)
                else:
                    gates = sa_gate[:, 4:6] if branch == 1 else sa_gate[:, 2:4]
                    link(dve, "dve", V.tensor_tensor(sa_coef, sa_coef, gates, ALU.mult))
                    for g in range(G):
                        last = V.tensor_scalar(sS[:, g, 0:width], sS[:, g, 0:width], sa_coef[:, g:g + 1], None, ALU.mult)
                    last.then_inc(S("probs"), 1)

            def keys_out_v(branch, tiles):
                for b in range(NB):
                    dve.wait_ge(S("key_ps"), NB * (branch - 1) + b + 1)
                    if NB * (branch - 1) + b >= 2:
                        dve.wait_ge(S("score_b"), NB * (branch - 1) + b - 1)
                    w = P * tiles // 2
                    V.tensor_copy(kTb[b % 2][:, w:2 * w], banks[7][:, 0:w]).then_inc(S("key_v"), 1)

            def biased(g, c, w, bank, nd):
                return V.scalar_tensor_tensor(sS[:, g, c:c + w], nd, C("slope")[:, g:g + 1], bank[:, 0:w], ALU.mult, ALU.add)

            dve.wait_ge(S("score_ps"), 1)
            biased(0, 0, NCMP, banks[1], C("ndcs")[:, 0:NCMP])
            link(dve, "dve", biased(1, 0, NCMP, banks[3], C("ndcs")[:, 0:NCMP]))
            softmax(0, NCMP)
            after(dve, "imp_ps")
            impg3 = impg.rearrange("p (g j) -> p g j", g=G)
            cand3 = cand.rearrange("p (g j) -> p g j", g=G)
            link(dve, "dve", V.tensor_copy(impg, banks[5][:, 0:32]))
            link(dve, "dve", V.tensor_reduce(lowest, impg3[:, :, 0:14], AX, ALU.min))
            for g in range(G):
                last = V.scalar_tensor_tensor(cand3[:, g, 0:14], impg3[:, g, 0:14], lowest[:, g:g + 1], C("jp1")[:, 1:15],
                                              ALU.is_equal, ALU.mult)
            link(dve, "dve", last)
            link(dve, "dve", V.tensor_reduce(dropj, cand3[:, :, 0:14], AX, ALU.max))
            for g in range(G):
                last = V.tensor_scalar(dmask[:, 16 * g:16 * g + 16], C("jp1"), dropj[:, g:g + 1], -1e30, ALU.is_equal, ALU.mult)
            link(dve, "dve", last)
            dve.wait_ge(S("pv_ps"), 1)
            V.tensor_copy(oS, banks[0][:, 0:256]).then_inc(S("oS"), 1)
            keys_out_v(1, 4)
            dve.wait_ge(S("score_ps"), 2)
            for g in range(G):
                biased(g, 0, WIN, banks[1 + 2 * g], C("ndwin")[:, 0:WIN])
                last = biased(g, WIN, NS, banks[(5, 0)[g]], C("ndwin")[:, WIN:])
            last.then_inc(S("scores_in"), 2)
            dve.wait_ge(S("scores_in"), 2)
            softmax(1, WIN_W)
            dve.wait_ge(S("pv_ps"), 2)
            V.tensor_tensor(oS, oS, banks[0][:, 0:256], ALU.add).then_inc(S("oS"), 1)
            keys_out_v(2, 8)
            dve.wait_ge(S("score_ps"), 3)
            for g in range(G):
                for c in range(2):
                    biased(g, 512 * c, 512, banks[1 + 2 * g + c], C("ndsel")[:, 512 * c:512 * c + 512])
                last = biased(g, PAST, NS, banks[(5, 0)[g]], C("ndsel")[:, PAST:])
            last.then_inc(S("scores_in"), 1)
            dve.wait_ge(S("scores_in"), 3)
            for g in range(G):
                blocks = sS[:, g, 0:PAST].rearrange("p (j s) -> p j s", s=64)
                last = V.tensor_tensor(blocks, blocks, dmask[:, 16 * g:16 * g + 16].unsqueeze(2).broadcast_to([P, 16, 64]), ALU.add)
            link(dve, "dve", last)
            softmax(2, SEL_W)
            dve.wait_ge(S("pv_ps"), 3)
            dve.wait_ge(S("oS"), 2)
            V.tensor_tensor(oS, oS, banks[0][:, 0:256], ALU.add).then_inc(S("oS"), 1)
            dve.wait_ge(S("oS"), 3)
            for g in range(G):
                V.tensor_copy(onT[DH * g:DH * g + DH, :, 256:288].rearrange("p r (b t) -> p r b t", t=TS),
                              oS[DH * g:DH * g + DH].rearrange("p (b g r t) -> p g r b t", b=NB, g=G, r=R)[:, g])

            after(dve, "sg_gate")

            def biased_scores(u):
                i, branch, g = UNITS[u]
                width = P * (i + 1) if branch else NCMP_P
                nd = C(f"ndc{i}")[:, 0:NCMP_P] if branch == 0 else C("nd")[:, P:] if i == 0 else C("nd")
                four = slice(R * (u % 2), R * (u % 2) + R)
                dve.wait_ge(S("p_score"), u + 1)
                if u >= 2:
                    dve.wait_ge(S("ppT_ps"), _tiles_before(u - 1))
                for r in range(R):
                    last = V.scalar_tensor_tensor(sP[u % 2][:, r, 0:width], nd, 2.0 ** -(R * g + r + 1),
                                                  banks[r // 2][:, 256 * (r % 2):256 * (r % 2) + width], ALU.mult, ALU.add)
                last.then_inc(S("p_in"), 1)
                dve.wait_ge(S("p_in"), u + 1)
                link(dve, "dve", V.tensor_reduce(pr_coef[:, four], sP[u % 2][:, :, 0:width], AX, ALU.max))
                V.tensor_scalar(pr_max[:, four], pr_coef[:, four], -1.0, None, ALU.mult).then_inc(S("p_max"), 1)

            def probabilities(u):
                i, branch, g = UNITS[u]
                width = P * (i + 1) if branch else NCMP_P
                four = slice(R * (u % 2), R * (u % 2) + R)
                dve.wait_ge(S("p_exp"), u + 1)
                link(dve, "dve", V.reciprocal(pr_coef[:, four], pr_sum[:, four]))
                at = 8 * branch + R * g
                link(dve, "dve", V.tensor_tensor(pr_coef[:, four], pr_coef[:, four], sg_gate[:, i, at:at + R], ALU.mult))
                if branch == 0:
                    link(dve, "dve", V.tensor_scalar(pr_coef[:, four], pr_coef[:, four], C("rowv")[:, i:i + 1], None, ALU.mult))
                V.tensor_tensor(sP[u % 2][:, :, 0:width], sP[u % 2][:, :, 0:width],
                                pr_coef[:, four].unsqueeze(2).broadcast_to([P, R, width]), ALU.mult).then_inc(S("p_probs"), 1)

            def add_output(u):
                i, branch, g = UNITS[u]
                to = on[:, i].rearrange("p (r g d) -> p g r d", r=R, g=G)[:, g]
                new = banks[3][:, 0:R * DH].rearrange("p (r d) -> p r d", r=R)
                dve.wait_ge(S("p_pv"), u + 1)
                if branch == 0:
                    V.tensor_copy(to, new).then_inc(S("on"), 1)
                else:
                    dve.wait_ge(S("on"), u - 1)
                    V.tensor_tensor(to, to, new, ALU.add).then_inc(S("on"), 1)
            dve.wait_ge(S("ld_hg"), 48)
            V.tensor_tensor(lb, lb, oml, ALU.subtract).then_inc(S("lb_d"), 1)
            after(dve, "lb")
            link(dve, "dve", V.tensor_scalar(oml, lb, -1.0, 1.0, ALU.mult, ALU.add))
            after(dve, "hf_sig")
            hf01, hf2 = z[:, 0:2, OFF["hf"]:OFF["hf"] + 512], zc(2, "hf", 512)
            V.tensor_tensor(hf01, hf01, oml.unsqueeze(1).broadcast_to([P, 2, 512]), ALU.mult)
            link(dve, "dve", V.tensor_tensor(hf2, hf2, oml[0:NS], ALU.mult))
            V.tensor_tensor(hf01, hf01, lb.unsqueeze(1).broadcast_to([P, 2, 512]), ALU.add)
            V.tensor_tensor(hf2, hf2, lb[0:NS], ALU.add).then_inc(S("f"), 1)
            after(dve, "gl")
            V.tensor_scalar(hf01, hf01, -1.0, 1.0, ALU.mult, ALU.add)
            V.tensor_scalar(hf2, hf2, -1.0, 1.0, ALU.mult, ALU.add).then_inc(S("hk"), 1)

            def hgrn_squares(i, src, sq):
                r = ROWS[i]
                dve.wait_ge(S("oh_cp"), i + 1)
                link(dve, "dve", V.tensor_tensor(sq[0:r], src[0:r], src[0:r], ALU.mult))
                V.tensor_reduce(hss[0:r, 4 * i:4 * i + 4], sq[0:r], AX, ALU.add).then_inc(S("hss"), 1)

            def hgrn_gated(i, src):
                r = ROWS[i]
                dve.wait_ge(S("hrt"), i + 1)
                link(dve, "dve", V.reciprocal(hrs[0:r, 4 * i:4 * i + 4], hrt[0:r, 4 * i:4 * i + 4]))
                link(dve, "dve", V.tensor_tensor(src[0:r], src[0:r], hrs[0:r, 4 * i:4 * i + 4].unsqueeze(2).broadcast_to([r, HH, DK]),
                                                 ALU.mult))
                link(dve, "dve", V.tensor_tensor(src[0:r], src[0:r], hgn[0:r].unsqueeze(1).broadcast_to([r, HH, DK]), ALU.mult))
                V.tensor_tensor(src[0:r], src[0:r], zc(i, "hg", 512).rearrange("p (h v) -> p h v", h=HH), ALU.mult
                                ).then_inc(S("oh"), 1)

            def hgrn_norm(i, src, sq):
                hgrn_squares(i, src, sq)
                hgrn_gated(i, src)

            def hgrn_distances(i, h):
                if h == 0:
                    dve.wait_ge(S("ebT"), i + 1)
                    V.tensor_tensor(qe, hqT, ebT, ALU.mult)
                sub = bT[:, h].rearrange("p (s t) -> p s t", t=16)
                dk, dq = dks[h % 2], dqs[h % 2]
                if h > 1:
                    dve.wait_ge(S("att_ps"), HH * i + h - 1)
                elif i:
                    dve.wait_ge(S("kh_ps"), i)
                V.tensor_tensor(dk, sub[:, :, 7:8].broadcast_to([P, 8, P]), bT[:, h].unsqueeze(1).broadcast_to([P, 8, P]),
                                ALU.subtract)
                link(dve, "dve", V.tensor_tensor(dq, sub, sub[:, :, 7:8].broadcast_to([P, 8, 16]), ALU.subtract))
                V.tensor_scalar(dk, dk, TOP, None, ALU.min)
                V.tensor_scalar(dq, dq, TOP, None, ALU.min).then_inc(S("hd"), 1)

            def hgrn_factors(i, h):
                dk, dq = dks[h % 2], dqs[h % 2]
                dve.wait_ge(S("he"), HH * i + h + 1)
                V.tensor_tensor(dk, dk, hkT[:, h].unsqueeze(1).broadcast_to([P, 8, P]), ALU.mult)
                V.tensor_tensor(dq, dq, hqT[:, h].rearrange("p (s t) -> p s t", t=16), ALU.mult).then_inc(S("hk_d"), 1)

            def hgrn_masked(i, h):
                dve.wait_ge(S("att_ps"), HH * i + h + 1)
                if h or i:
                    dve.wait_ge(S("o_ps"), HH * i + h)
                V.tensor_tensor(att, banks[4][:, 0:P], C("tri"), ALU.mult).then_inc(S("att"), 1)

            def hgrn_to_end(i):
                dve.wait_ge(S("att_ps"), HH * (i + 1))
                dk = dks[0]
                V.tensor_tensor(dk[:, 0:4], bT[:, :, P - 1:P].broadcast_to([P, HH, P]), bT, ALU.subtract).then_inc(S("kd_d"), 1)

            def hgrn_end_keys(i):
                dk = dks[0]
                dve.wait_ge(S("kd_e"), i + 1)
                V.tensor_tensor(dk[:, 0:4], dk[:, 0:4], hkT, ALU.mult).then_inc(S("kd"), 1)

            def hgrn_new_state(i):
                dve.wait_ge(S("st_ps"), i + 1)
                new = banks[6][:].rearrange("p (h v) -> p h v", h=HH)
                if i == 0:
                    V.tensor_copy(state, new).then_inc(S("state"), 1)
                else:
                    dve.wait_ge(S("o_ps"), HH * (i + 1))
                    link(dve, "dve", V.tensor_tensor(state, state, ebT[:, :, P - 1:P].broadcast_to([P, HH, DK]), ALU.mult))
                    V.tensor_tensor(state, state, new, ALU.add).then_inc(S("state"), 1)

            steps = {"biased": biased_scores, "probs": probabilities, "add": add_output, "distances": hgrn_distances,
                     "factors": hgrn_factors, "head_masked": hgrn_masked, "to_end": hgrn_to_end, "end_keys": hgrn_end_keys,
                     "new_state": hgrn_new_state, "squares": lambda i: hgrn_squares(i, oh, osq),
                     "gated": lambda i: hgrn_gated(i, oh)}
            for name, args in PROMPT_STEPS:
                if name in steps:
                    steps[name](*args)
            dve.wait_ge(S("ohT_ps"), 2)
            dve.wait_ge(S("onT_ps"), 2)
            dve.wait_ge(S("st_state"), 16)
            V.tensor_tensor(vm[0:NS], zc(2, "hi", 512).unsqueeze(1).broadcast_to([NS, NB, 512]),
                            C("bmask", NS).unsqueeze(2).broadcast_to([NS, NB, 512]), ALU.mult).then_inc(S("vm"), 1)
            link(dve, "dve", V.memset(qep, 0.0))
            V.tensor_copy(ss[:, 3:4], eps_t).then_inc(S("s_free"), 1)
            dve.wait_ge(S("ebT"), 3)
            ends = sb_[:, 0].rearrange("p h (b t) -> p (h b) t", t=TS)
            V.tensor_tensor(sb_[:, 6].rearrange("p h (b t) -> p (h b) t", t=TS), ends[:, :, TS - 1:TS].broadcast_to([P, HH * NB, TS]),
                            ends, ALU.subtract).then_inc(S("kd_d"), 1)
            link(dve, "dve", V.tensor_tensor(sb_[:, 4], sb_[:, 1], sb_[:, 3], ALU.mult))
            V.tensor_copy(qep.rearrange("p h (b c) -> p h b c", c=36)[:, :, :, 0:TS], sb_[:, 4].rearrange("p h (b t) -> p h b t", t=TS))
            V.scalar_tensor_tensor(sb_[:, 5], sb_[:, 5], CLIP, sb_[:, 2], ALU.min, ALU.mult)
            dve.wait_ge(S("kd_e"), 3)
            V.tensor_tensor(sb_[:, 6], sb_[:, 6], sb_[:, 2], ALU.mult).then_inc(S("s_kq"), 1)
            dve.wait_ge(S("att_ps"), 2 * HH + 1)
            V.tensor_tensor(att_s[0:NS], banks[4][0:NS, 0:P].rearrange("p (h t) -> p h t", h=HH),
                            C("bt32", NS).unsqueeze(1).broadcast_to([NS, HH, NS]), ALU.mult).then_inc(S("att"), 1)
            dve.wait_ge(S("o_ps"), 2 * HH + 1)
            eb_end = sb_[:, 3].rearrange("p h (b t) -> p b h t", t=TS)[:, :, :, TS - 1]
            s0v = s0.rearrange("p (b h) v -> p b h v", h=HH)
            for b in range(NB):
                last = V.tensor_tensor(s0v[:, b], s0v[:, b], eb_end[:, b].unsqueeze(2).broadcast_to([P, HH, DK]), ALU.mult)
            link(dve, "dve", last)
            for n in range(8):
                h, half = n // 2, n % 2
                dve.wait_ge(S("sst_ps"), n + 1)
                V.tensor_tensor(s0v[:, 4 * half:4 * half + 4, h], s0v[:, 4 * half:4 * half + 4, h],
                                banks[n % 2][:].rearrange("p (b v) -> p b v", b=4), ALU.add).then_inc(S("s_state"), 1)
            hgrn_norm(2, oh_s, osq_s)

            V.tensor_copy(ss[:, 3:4], eps_t).then_inc(S("onS"), 1)
            for i in range(3):
                r = ROWS[i]
                dve.wait_ge(S("mrg_ps"), i + 1)
                for n in range(2):
                    for name, bank in (("ga", banks[n]), ("gb", banks[2 + n])):
                        v = zc(i, name, D)[:, 512 * n:512 * n + 512]
                        last = V.tensor_tensor(v, v, bank[0:r, :], ALU.mult)
                link(dve, "dve", last)
                if i:
                    dve.wait_ge(S("mT_ps"), i)
                V.tensor_tensor(mrow[0:r], zc(i, "ga", D), zc(i, "gb", D), ALU.add).then_inc(S("m_rows"), 1)

            def residual(i, src, seq, name):
                r, ps = ROWS[i], i // 2
                link(dve, "dve", V.tensor_tensor_reduce(scr[0:r], src[0:r], src[0:r], 1.0, 0.0, ALU.mult, ALU.add, ss[0:r, i:i + 1]))
                V.tensor_copy(ss[0:r, 3:4], ss[0:r, i:i + 1]).then_inc(S("ss"), 1)
                dve.wait_ge(S("rms"), seq + 1)
                link(dve, "dve", V.reciprocal(rstd[0:r, i:i + 1], rt_[0:r, i:i + 1]))
                link(dve, "dve", V.scalar_tensor_tensor(src[0:r], src[0:r], rstd[0:r, i:i + 1], gate_rows[0:r, ps], ALU.mult, ALU.mult))
                V.tensor_tensor(x[0:r, i], x[0:r, i], src[0:r], ALU.add).then_inc(S(name), 1)

            for i in range(3):
                dve.wait_ge(S("out_cp"), i + 1)
                residual(i, orow, 3 + i, "y1")

            dve.wait_ge(S("bc"), 5)
            for i in range(3):
                r, ps = ROWS[i], i // 2
                link(dve, "dve", V.tensor_tensor_reduce(scr[0:r], x[0:r, i], x[0:r, i], 1.0, 0.0, ALU.mult, ALU.add, ss[0:r, i:i + 1]))
                V.tensor_copy(ss[0:r, 3:4], ss[0:r, i:i + 1]).then_inc(S("ss"), 1)
                dve.wait_ge(S("rms"), 7 + i)
                link(dve, "dve", V.reciprocal(rstd[0:r, i:i + 1], rt_[0:r, i:i + 1]))
                link(dve, "dve", V.scalar_tensor_tensor(h2r[0:r, i], x[0:r, i], rstd[0:r, i:i + 1], mod_rows[0:r, 0, ps],
                                                        ALU.mult, ALU.mult))
                V.tensor_tensor(h2r[0:r, i], h2r[0:r, i], mod_rows[0:r, 1, ps], ALU.add).then_inc(S("h2"), 1)
            after(dve, "lg_ps")
            for i in range(3):
                r = ROWS[i]
                link(dve, "dve", V.tensor_tensor(lg[0:r, i], banks[1][0:r, E * i:E * i + E], br[0:r], ALU.add))
                link(dve, "dve", V.max(top8[0:r], lg[0:r, i]))
                link(dve, "dve", V.max_index(top8i[0:r].bitcast(U32), top8[0:r], lg[0:r, i]))
                V.tensor_copy(idxf[0:r], top8i[0:r, 0:4].bitcast(U32))
                V.tensor_scalar(negtop[0:r], top8[0:r, 0:1], -1.0, None, ALU.mult).then_inc(S("top"), 1)
                dve.wait_ge(S("top"), i + 1)
                for k in range(4):
                    last = V.tensor_scalar(oneh[0:r, i, k], C("iota")[0:r], idxf[0:r, k:k + 1], None, ALU.is_equal)
                link(dve, "dve", last)
                V.tensor_reduce(mk[0:r, i], oneh[0:r, i].rearrange("p k e -> p e k"), AX, ALU.add).then_inc(S("mk"), 1)
                dve.wait_ge(S("wexp"), i + 1)
                link(dve, "dve", V.reciprocal(wrec[0:r], wsum[0:r]))
                link(dve, "dve", V.tensor_scalar(wts[0:r, i], wts[0:r, i], wrec[0:r], None, ALU.mult))
            after(dve, "cnt_ps")
            link(dve, "dve", V.tensor_scalar(nchT[0:E], banks[3][0:E, 0:P], float(SLOT), 1.0, ALU.is_gt, ALU.add))
            for v in range(2, JMAX):
                ins = V.scalar_tensor_tensor(nchT[0:E], banks[3][0:E, 0:P], float(SLOT * v), nchT[0:E], ALU.is_gt, ALU.add)
                if v < JMAX - 1:
                    link(dve, "dve", ins)
            ins.then_inc(S("nch"), 1)
            after(dve, "base_ps")
            V.tensor_copy(tab[0:1, 0:E], banks[4][0:1, E:2 * E])
            V.tensor_scalar(tab[0:1, 2 * E:3 * E], banks[4][0:1, E:2 * E], -1.0, None, ALU.add)
            V.tensor_copy(tab[0:1, E:2 * E], banks[4][0:1, 0:E]).then_inc(S("tab"), 1)
            link(dve, "dve", V.tensor_scalar(slotb, banks[4][:, 0:E], float(SLOT), None, ALU.mult))
            for i in range(3):
                r = ROWS[i]
                link(dve, "dve", V.tensor_tensor(roww[0:r], banks[2][0:r, E * i:E * i + E], slotb[0:r], ALU.add))
                for k in range(4):
                    link(dve, "dve", V.tensor_tensor_reduce(oneh[0:r, i, k], oneh[0:r, i, k], roww[0:r], 1.0, 0.0, ALU.mult, ALU.add,
                                                            rowf[0:r, 4 * i + k:4 * i + k + 1]))
                V.tensor_copy(rowu[0:r, 4 * i:4 * i + 4], rowf[0:r, 4 * i:4 * i + 4]).then_inc(S("rows"), 1)

            dve.wait_ge(S("scattered"), 16 * 12)
            after(dve, "tab")
            n_chunks = dve.value_load(tab[0:1, E - 1:E], min_val=E, max_val=CMAX)
            with dve.Fori(0, n_chunks) as c:
                dve.wait_ge(S("piece_used"), c * 12 + 8)
                V.tensor_scalar(gt, banks[0][:], 7.0, None, ALU.min).then_inc(S("gate"), 1)
                V.tensor_scalar(up, banks[1][:], -7.0, 7.0, ALU.max, ALU.min).then_inc(S("up"), 1)
                dve.wait_ge(S("gate"), c + 1)
                dve.wait_ge(S("up"), c + 1)
                V.scalar_tensor_tensor(up, up, 1.0, gt, ALU.add, ALU.mult).then_inc(S("prod"), 1)
                dve.wait_ge(S("prod"), c + 1)
                dve.wait_ge(S("sig"), c + 1)
                V.tensor_tensor(ac, up, sg, ALU.mult).then_inc(S("act"), 1)
                dve.wait_ge(S("aT_ps"), c + 1)
                V.tensor_copy(aT, banks[3][:]).then_inc(S("aT"), 1)
            for i in range(3):
                r = ROWS[i]
                dve.wait_ge(S(f"ld_gath{i}"), 64)
                link(dve, "dve", V.tensor_scalar(accr[0:r], gath[0:r, i, 0], wts[0:r, i, 0:1], None, ALU.mult))
                for k in range(1, 4):
                    link(dve, "dve", V.scalar_tensor_tensor(accr[0:r], gath[0:r, i, k], wts[0:r, i, k:k + 1], accr[0:r],
                                                            ALU.mult, ALU.add))
                link(dve, "dve", V.tensor_tensor_reduce(sqr[0:r], accr[0:r], accr[0:r], 1.0, 0.0, ALU.mult, ALU.add, ss[0:r, i:i + 1]))
                V.tensor_copy(ss[0:r, 3:4], ss[0:r, i:i + 1]).then_inc(S("ss"), 1)
                dve.wait_ge(S("rms"), 10 + i)
                link(dve, "dve", V.reciprocal(rstd[0:r, i:i + 1], rt_[0:r, i:i + 1]))
                link(dve, "dve", V.scalar_tensor_tensor(accr[0:r], accr[0:r], rstd[0:r, i:i + 1], gate_rows[0:r, i // 2],
                                                        ALU.mult, ALU.mult))
                link(dve, "dve", V.tensor_tensor(x[0:r, i], x[0:r, i], accr[0:r], ALU.add))
                V.tensor_copy(ss[0:r, 3:4], ss[0:r, i:i + 1]).then_inc(S("y2"), 1)

        @block.gpsimd
        def _(pool):
            after(pool, "zero_t")
            rows = slots.rearrange("(p a) (b c) -> p (a b) c", p=P, c=P)
            half = rows.shape[1] // 2
            for n in range(2):
                pool.wait_ge(S("zin_mm"), 3 * n + 1)
                if n:
                    pool.wait_ge(S("zero_slots"), 16)
                pool.dma_start(rows[:, half * n:half * n + half], zero_t.unsqueeze(1).broadcast_to([P, half, P])
                               ).then_inc(S("zero_slots"), 16)
            pool.wait_ge(S("zero_slots"), 32)
            load_pages(pool, (2, 3))
            pool.wait_ge(S("pre_ps"), 4)
            load_selected(pool, NPG // 2, "ld_key_p")

            for i in range(3):
                pool.wait_ge(S("rows"), i + 1)
                for k in range(4):
                    pool.indirect_dma_start(
                        out=slots, out_offset=bass.IndirectOffsetOnAxis(ap=rowu[0:ROWS[i], 4 * i + k:4 * i + k + 1], axis=0),
                        in_=h2r[0:ROWS[i], i], in_offset=None).then_inc(S("scattered"), 16)
            pool.wait_ge(S("scattered"), 16 * 12)
            after(pool, "tab")
            n_chunks = pool.value_load(tab[0:1, E - 1:E], min_val=E, max_val=CMAX)
            pool.dma_start(xrow[0:SLOT], slots[0:SLOT]).then_inc(S("ld_x2"), 16)
            with pool.Fori(0, n_chunks) as c:
                pool.wait_ge(S("xcT_ps"), c + 1)
                pool.dma_start(xrow[0:SLOT], slots[bass.ds(c * SLOT + SLOT, SLOT)]).then_inc(S("ld_x2"), 16)
                pool.wait_ge(S("yc"), c + 1)
                for s in range(2):
                    pool.dma_start(slots[bass.ds(c * SLOT, SLOT), 512 * s:512 * s + 512], yc[SLOT * s:SLOT * s + SLOT]
                                   ).then_inc(S("st_yc"), 16)
            after(pool, "all_out")
            for i in range(3):
                for k in range(4):
                    pool.indirect_dma_start(
                        out=gath[0:ROWS[i], i, k], out_offset=None, in_=slots,
                        in_offset=bass.IndirectOffsetOnAxis(ap=rowu[0:ROWS[i], 4 * i + k:4 * i + k + 1], axis=0)
                    ).then_inc(S(f"ld_gath{i}"), 16)


_INS = ["x_prompt", "x_sample", "c_prompt", "c_sample", "cache_cmp", "cache_sel", "state_win", "state_hgrn", "page_table",
        "w_ada", "b_ada", "norm_mix_pre", "norm_mix_post", "norm_ffn_pre", "norm_ffn_post", "w_in", "cmp_pe", "cmp_w1",
        "cmp_w2", "hg_lb_logits", "hg_norm", "w_branch_a", "w_branch_b", "w_out", "w_router", "b_router", "w_up", "b_up",
        "w_down", "b_down"]
_OUTS = [(1, TP, D), (NB, TS, D), (1, 1, TP, 2, G, DH), (1, NB, TS, 2, G, DH), (1, 1, TP, 2, G, DH), (1, NB, TS, 2, G, DH),
         (1, 1, TP, 2, G, DH), (1, NB, WIN, 2, G, DH), (1, 1, HH, DK, DK), (1, NB, HH, DK, DK)]


def kernel(**inputs):
    import numpy as _np
    import concourse.bacc as _bacc
    from concourse.bass_utils import run_bass_kernel_spmd as _run

    nc = _bacc.Bacc("TRN2", target_bir_lowering=False, num_devices=1)
    arrays, args = {}, {}
    for name in _INS:
        a = _np.ascontiguousarray(inputs[name])
        arrays[f"in_{name}"] = a
        args[name] = nc.dram_tensor(f"in_{name}", a.shape, mybir.dt.from_np(a.dtype), kind="ExternalInput").ap()
    arrays["in_const"] = CONST
    args["const"] = nc.dram_tensor("in_const", CONST.shape, F32, kind="ExternalInput").ap()
    outs = [nc.dram_tensor(f"out_{i}", s, F32, kind="ExternalOutput").ap() for i, s in enumerate(_OUTS)]
    build(nc, args, outs)
    r = _run(nc, [arrays], core_ids=[0])
    return tuple(r.results[0][f"out_{i}"] for i in range(len(_OUTS)))
```
